# Optimizing a Trainium2 kernel written in Bass

```python
import jax
import jax.numpy as jnp
from jax import lax
import numpy as np
import math, functools
import jax, jax.numpy as jnp

D_MODEL = 1024
BATCH = 1
SEQ = 256
DEPTH = 2

CTX_LEN = 256
GRID_W = 64
N_BRANCH = 4
BRANCH_W = D_MODEL // 2
RET_HEADS = 4
RET_DH = BRANCH_W // RET_HEADS
RET_CHUNK = 128
SC_KERNEL = 3
CF_KERNEL = 31
ATT_HEADS = 8
ATT_KV_HEADS = 2
ATT_DH = BRANCH_W // ATT_HEADS
ATT_KV_W = ATT_KV_HEADS * ATT_DH
ATT_BLOCK = 128
WINDOW = 128
ROPE_BASE = 10000.0
ROPE_AXIS_FREQS = ATT_DH // 4
EPS = 1e-6
NEG_INF = -1e30

IN_NAMES = ('ret_q', 'ret_k', 'ret_v', 'ret_z',
            'sc_b', 'sc_c', 'sc_x', 'sc_z',
            'cf_glu', 'cf_z',
            'att_q', 'att_k', 'att_v', 'att_z',
            'merge_gates')
IN_SIZES = (BRANCH_W, BRANCH_W, BRANCH_W, BRANCH_W,
            BRANCH_W, BRANCH_W, BRANCH_W, BRANCH_W,
            2 * BRANCH_W, BRANCH_W,
            BRANCH_W, ATT_KV_W, ATT_KV_W, BRANCH_W,
            N_BRANCH * D_MODEL)
IN_TOTAL = sum(IN_SIZES)


def split_proj(y):
    offsets = [int(o) for o in np.cumsum(IN_SIZES)[:-1]]
    return dict(zip(IN_NAMES, jnp.split(y, offsets, axis=-1)))

def in_cols(w, name):
    i = IN_NAMES.index(name)
    start = sum(IN_SIZES[:i])
    return w[:, start:start + IN_SIZES[i]]

def heads(t, n):
    return t.reshape(t.shape[:-1] + (n, t.shape[-1] // n))

def rmsnorm(x, w):
    xf = x.astype(jnp.float32)
    y = xf * lax.rsqrt(jnp.mean(xf * xf, axis=-1, keepdims=True) + EPS)
    return (y * w).astype(x.dtype)

def layer_norm(u, w, b):
    uf = u.astype(jnp.float32)
    mu = jnp.mean(uf, axis=-1, keepdims=True)
    var = jnp.mean(jnp.square(uf - mu), axis=-1, keepdims=True)
    return (uf - mu) * lax.rsqrt(var + EPS) * w + b

def head_group_norm(o, w):
    of = o.astype(jnp.float32)
    mu = jnp.mean(of, axis=-1, keepdims=True)
    var = jnp.mean(jnp.square(of - mu), axis=-1, keepdims=True)
    y = (of - mu) * lax.rsqrt(var + EPS)
    return y.reshape(o.shape[:-2] + (-1,)) * w

def ada_modulation(cvec, w, b):
    m = jax.nn.silu(cvec) @ w + b
    return jnp.split(m, 3, axis=-1)

def modulate(h, shift, scale):
    return h * (1 + scale) + shift

def depthwise_conv(u, w):
    K, C = w.shape
    return lax.conv_general_dilated(
        u, w[:, None, :].astype(u.dtype), window_strides=(1,), padding=[(K // 2, K // 2)],
        dimension_numbers=('NWC', 'WIO', 'NWC'), feature_group_count=C)

def axial_rope_tables(row, col):
    inv = ROPE_BASE ** (-jnp.arange(ROPE_AXIS_FREQS, dtype=jnp.float32) / ROPE_AXIS_FREQS)
    ang = jnp.concatenate([row.astype(jnp.float32)[:, None] * inv[None],
                           col.astype(jnp.float32)[:, None] * inv[None]], axis=-1)
    return jnp.cos(ang)[:, None, :], jnp.sin(ang)[:, None, :]

def axial_rope(t, cos, sin):
    half = t.shape[-1] // 2
    t1 = t[..., :half].astype(jnp.float32)
    t2 = t[..., half:].astype(jnp.float32)
    return jnp.concatenate([t1 * cos - t2 * sin, t2 * cos + t1 * sin], axis=-1).astype(t.dtype)

def retention_dir(q, k, v, log_gamma, s0, strict):
    B, N, H, d = q.shape
    C = RET_CHUNK
    nc = N // C
    qc, kc, vc = (t.reshape(B, nc, C, H, d) for t in (q, k, v))
    pos = jnp.arange(C)
    diff = pos[:, None] - pos[None, :]
    keep = (diff > 0) if strict else (diff >= 0)
    expo = jnp.where(keep, diff, 0).astype(jnp.float32)
    decay = jnp.where(keep[None], jnp.exp(expo[None] * log_gamma[:, None, None]), 0.0)
    scores = jnp.einsum('bnihd,bnjhd->bnhij', qc, kc) * decay
    intra = jnp.einsum('bnhij,bnjhe->bnihe', scores, vc)
    posf = pos.astype(jnp.float32)
    k_w = jnp.exp((C - 1 - posf)[:, None] * log_gamma[None])
    q_w = jnp.exp((posf + 1)[:, None] * log_gamma[None])
    kv = jnp.einsum('bnjhd,jh,bnjhe->nbhde', kc, k_w, vc)
    chunk_decay = jnp.exp(C * log_gamma)[None, :, None, None]

    def step(s, kv_c):
        return s * chunk_decay + kv_c, s

    s_final, s_prev = lax.scan(step, s0, kv)
    cross = jnp.einsum('bnihd,ih,nbhde->bnihe', qc, q_w, s_prev)
    return (intra + cross).reshape(B, N, H, d), s_final

def retention_bidir(q, k, v, log_gamma, s0_f, s0_b):
    out_f, s_f = retention_dir(q, k, v, log_gamma[0], s0_f, False)
    flip = lambda t: jnp.flip(t, axis=1)
    out_b, s_b = retention_dir(flip(q), flip(k), flip(v), log_gamma[1], s0_b, True)
    return out_f + flip(out_b), s_f, s_b

def retention_context_states(k, v, log_gamma):
    L = k.shape[1]
    pos = jnp.arange(L, dtype=jnp.float32)
    w_f = jnp.exp((L - 1 - pos)[:, None] * log_gamma[0][None])
    w_b = jnp.exp(pos[:, None] * log_gamma[1][None])
    s_f = jnp.einsum('blhd,lh,blhe->bhde', k, w_f, v)
    s_b = jnp.einsum('blhd,lh,blhe->bhde', k, w_b, v)
    return s_f, s_b

def windowed_gqa(q, k, v, k_ctx, v_ctx, sink):
    B, S, H, d = q.shape
    G = H // ATT_KV_HEADS
    nb = S // ATT_BLOCK
    L = k_ctx.shape[1]
    qb = q.reshape(B, nb, ATT_BLOCK, ATT_KV_HEADS, G, d)

    def band(t):
        tp = jnp.pad(t, ((0, 0), (ATT_BLOCK, ATT_BLOCK), (0, 0), (0, 0)))
        tp = tp.reshape(B, nb + 2, ATT_BLOCK, ATT_KV_HEADS, d)
        return jnp.concatenate([tp[:, :-2], tp[:, 1:-1], tp[:, 2:]], axis=2)

    kw, vw = band(k), band(v)
    qi = jnp.arange(ATT_BLOCK)
    kj = jnp.arange(3 * ATT_BLOCK) - ATT_BLOCK
    in_band = jnp.abs(kj[None, :] - qi[:, None]) <= WINDOW
    key_pos = jnp.arange(nb)[:, None] * ATT_BLOCK + kj[None, :]
    in_seq = (key_pos >= 0) & (key_pos < S)
    mask = in_band[None] & in_seq[:, None, :]
    scale = d ** -0.5
    s_loc = jnp.einsum('bnqhgd,bnkhd->bnhgqk', qb, kw).astype(jnp.float32) * scale
    s_loc = jnp.where(mask[None, :, None, None], s_loc, NEG_INF)
    s_ctx = jnp.einsum('bnqhgd,bchd->bnhgqc', qb, k_ctx).astype(jnp.float32) * scale
    s_sink = jnp.broadcast_to(sink.astype(jnp.float32).reshape(ATT_KV_HEADS, G, 1, 1),
                              s_loc.shape[:-1] + (1,))
    p = jax.nn.softmax(jnp.concatenate([s_loc, s_ctx, s_sink], axis=-1), axis=-1)
    nk = 3 * ATT_BLOCK
    p_loc = p[..., :nk].astype(v.dtype)
    p_ctx = p[..., nk:nk + L].astype(v.dtype)
    o = (jnp.einsum('bnhgqk,bnkhd->bnqhgd', p_loc, vw)
         + jnp.einsum('bnhgqc,bchd->bnqhgd', p_ctx, v_ctx))
    return o.reshape(B, S, H * d)

def context_attention(q, k, v, sink):
    B, L, H, d = q.shape
    G = H // ATT_KV_HEADS
    qg = q.reshape(B, L, ATT_KV_HEADS, G, d)
    s = jnp.einsum('bqhgd,bkhd->bhgqk', qg, k).astype(jnp.float32) * d ** -0.5
    s_sink = jnp.broadcast_to(sink.astype(jnp.float32).reshape(ATT_KV_HEADS, G, 1, 1), s.shape[:-1] + (1,))
    p = jax.nn.softmax(jnp.concatenate([s, s_sink], axis=-1), axis=-1)[..., :L]
    o = jnp.einsum('bhgqk,bkhd->bqhgd', p.astype(v.dtype), v)
    return o.reshape(B, L, H * d)

def short_conv(b_gate, c_gate, xv, w):
    return b_gate * depthwise_conv(c_gate * xv, w)

def conformer_conv(glu_in, w, bias, ln_w, ln_b):
    a, g = jnp.split(glu_in, 2, axis=-1)
    u = depthwise_conv(a * jax.nn.sigmoid(g), w) + bias
    return jax.nn.silu(layer_norm(u, ln_w, ln_b)).astype(glu_in.dtype)

def mixer_output(p, ret_o, att_o, ret_gn_w, sc_conv_w, cf_conv_w, cf_conv_b, cf_ln_w, cf_ln_b,
                 w_branch, w_out):
    dt = p['ret_z'].dtype
    r = (head_group_norm(ret_o, ret_gn_w) * jax.nn.silu(p['ret_z'])).astype(dt)
    s = short_conv(p['sc_b'], p['sc_c'], p['sc_x'], sc_conv_w) * jax.nn.silu(p['sc_z'])
    f = conformer_conv(p['cf_glu'], cf_conv_w, cf_conv_b, cf_ln_w, cf_ln_b) * jax.nn.silu(p['cf_z'])
    a = att_o * jax.nn.silu(p['att_z'])
    gates = jnp.split(p['merge_gates'], N_BRANCH, axis=-1)
    merged = sum(jax.nn.sigmoid(g) * (br @ w_branch[i])
                 for i, (g, br) in enumerate(zip(gates, (r, s, f, a))))
    return merged @ w_out

def first_inputs(seed: int = 0) -> dict:
    key = jax.random.key(seed)
    ks = jax.random.split(key, 20)
    f32 = jnp.float32
    D = D_MODEL

    def nrm(k, shape, fan_in):
        return jax.random.normal(k, shape, f32) * fan_in ** -0.5

    decay_logit = jnp.log(2.0 ** (5.0 + jnp.arange(RET_HEADS, dtype=f32)) - 1.0)
    return {
        'x': jax.random.normal(ks[0], (BATCH, SEQ, D), f32),
        'c': jax.random.normal(ks[1], (BATCH, D), f32),
        'ctx': jax.random.normal(ks[2], (BATCH, CTX_LEN, D), f32),
        'c_ctx': jax.random.normal(ks[3], (D,), f32),
        'w_mod': nrm(ks[4], (DEPTH, D, 3 * D), D),
        'b_mod': 0.02 * jax.random.normal(ks[5], (DEPTH, 3 * D), f32),
        'norm_w': 1.0 + 0.1 * jax.random.normal(ks[6], (DEPTH, D), f32),
        'w_in': nrm(ks[7], (DEPTH, D, IN_TOTAL), D),
        'ret_decay': decay_logit[None, None, :] + 0.1 * jax.random.normal(ks[8], (DEPTH, 2, RET_HEADS), f32),
        'ret_gn_w': 1.0 + 0.1 * jax.random.normal(ks[9], (DEPTH, BRANCH_W), f32),
        'sc_conv_w': nrm(ks[10], (DEPTH, SC_KERNEL, BRANCH_W), SC_KERNEL),
        'cf_conv_w': nrm(ks[11], (DEPTH, CF_KERNEL, BRANCH_W), CF_KERNEL),
        'cf_conv_b': 0.02 * jax.random.normal(ks[12], (DEPTH, BRANCH_W), f32),
        'cf_ln_w': 1.0 + 0.1 * jax.random.normal(ks[13], (DEPTH, BRANCH_W), f32),
        'cf_ln_b': 0.02 * jax.random.normal(ks[14], (DEPTH, BRANCH_W), f32),
        'att_sink': jax.random.normal(ks[15], (DEPTH, ATT_HEADS), f32),
        'w_branch': nrm(ks[16], (DEPTH, N_BRANCH, BRANCH_W, D), BRANCH_W),
        'w_out': nrm(ks[17], (DEPTH, D, D), D),
        'final_norm_w': 1.0 + 0.1 * jax.random.normal(ks[18], (D,), f32),
    }

def first_block(x, c, ctx, c_ctx, w_mod, b_mod, norm_w, w_in, ret_decay, ret_gn_w, sc_conv_w,
              cf_conv_w, cf_conv_b, cf_ln_w, cf_ln_b, att_sink, w_branch, w_out, final_norm_w):
    B, S, _ = x.shape
    ROWS = S // GRID_W
    row = jnp.repeat(jnp.arange(ROWS), GRID_W)
    col = jnp.tile(jnp.arange(GRID_W), ROWS)
    cos, sin = axial_rope_tables(row, col)
    k_scale = RET_DH ** -0.5
    xc = ctx
    for l in range(DEPTH):
        ctx_out_needed = l < DEPTH - 1
        log_gamma = jax.nn.log_sigmoid(ret_decay[l].astype(jnp.float32))
        shift_x, scale_x, gate_x = ada_modulation(c, w_mod[l], b_mod[l])
        shift_c, scale_c, gate_c = ada_modulation(c_ctx, w_mod[l], b_mod[l])
        hx = modulate(rmsnorm(x, norm_w[l]), shift_x[:, None], scale_x[:, None])
        hc = modulate(rmsnorm(xc, norm_w[l]), shift_c, scale_c)
        px = split_proj(hx @ w_in[l])
        if ctx_out_needed:
            pc = split_proj(hc @ w_in[l])
        else:
            pc = {n: hc @ in_cols(w_in[l], n) for n in ('ret_k', 'ret_v', 'att_k', 'att_v')}
        rk_c = heads(pc['ret_k'], RET_HEADS) * k_scale
        rv_c = heads(pc['ret_v'], RET_HEADS)
        ak_c = heads(pc['att_k'], ATT_KV_HEADS)
        av_c = heads(pc['att_v'], ATT_KV_HEADS)
        if ctx_out_needed:
            zero = jnp.zeros((B, RET_HEADS, RET_DH, RET_DH), jnp.float32)
            ret_c, s_f, s_b = retention_bidir(heads(pc['ret_q'], RET_HEADS), rk_c, rv_c, log_gamma, zero, zero)
            att_c = context_attention(heads(pc['att_q'], ATT_HEADS), ak_c, av_c, att_sink[l])
            out_c = mixer_output(pc, ret_c, att_c, ret_gn_w[l], sc_conv_w[l], cf_conv_w[l], cf_conv_b[l],
                                 cf_ln_w[l], cf_ln_b[l], w_branch[l], w_out[l])
        else:
            s_f, s_b = retention_context_states(rk_c, rv_c, log_gamma)
        ret_x, _, _ = retention_bidir(heads(px['ret_q'], RET_HEADS), heads(px['ret_k'], RET_HEADS) * k_scale,
                                      heads(px['ret_v'], RET_HEADS), log_gamma, s_f, s_b)
        att_x = windowed_gqa(axial_rope(heads(px['att_q'], ATT_HEADS), cos, sin),
                             axial_rope(heads(px['att_k'], ATT_KV_HEADS), cos, sin),
                             heads(px['att_v'], ATT_KV_HEADS), ak_c, av_c, att_sink[l])
        out_x = mixer_output(px, ret_x, att_x, ret_gn_w[l], sc_conv_w[l], cf_conv_w[l], cf_conv_b[l],
                             cf_ln_w[l], cf_ln_b[l], w_branch[l], w_out[l])
        x = x + gate_x[:, None] * out_x
        if ctx_out_needed:
            xc = xc + gate_c * out_c
    return rmsnorm(x, final_norm_w)


N_MIXERS = 2
N_A = (DEPTH + 1) // 2
N_B = DEPTH // 2
D_RNN = D_MODEL
RG_BLOCKS = 4
RG_BLOCK = D_RNN // RG_BLOCKS
RG_CONV = 4
RG_C = 8.0
GLA_HEADS = 4
GLA_DK = D_MODEL // 2 // GLA_HEADS
GLA_DV = D_MODEL // GLA_HEADS
GLA_RANK = 16
GLA_TAU = 16.0
GLA_CHUNK = 64
GLA_QK = GLA_HEADS * GLA_DK
GLA_IN = 2 * GLA_QK + 2 * D_MODEL + GLA_RANK
D_FF = ((8 * D_MODEL // 3 + 127) // 128) * 128
FFN_CONV = 3


def rmsnorm_2(x, g):
    x32 = x.astype(jnp.float32)
    y = x32 * lax.rsqrt(jnp.mean(x32 * x32, axis=-1, keepdims=True) + EPS)
    return (y * g.astype(jnp.float32)).astype(x.dtype)

def causal_dwconv(x, w, b):
    k_width = w.shape[0]
    s = x.shape[1]
    xp = jnp.pad(x, ((0, 0), (k_width - 1, 0), (0, 0)))
    y = b
    for k in range(k_width):
        y = y + xp[:, k:k + s] * w[k]
    return y

def _lru_combine(left, right):
    a1, b1 = left
    a2, b2 = right
    return a1 * a2, a2 * b1 + b2

def rglru_mixer(h, w_in, conv_w, conv_b, wa, ba, wx, bx, lam, w_out):
    bsz, s, _ = h.shape
    gate_br, x_br = jnp.split(h @ w_in, 2, axis=-1)
    x_br = causal_dwconv(x_br, conv_w, conv_b)
    xb = x_br.reshape(bsz, s, RG_BLOCKS, RG_BLOCK)
    r = jax.nn.sigmoid(jnp.einsum('bsgi,gij->bsgj', xb, wa).reshape(bsz, s, D_RNN) + ba)
    i_g = jax.nn.sigmoid(jnp.einsum('bsgi,gij->bsgj', xb, wx).reshape(bsz, s, D_RNN) + bx)
    log_a = -RG_C * r.astype(jnp.float32) * jax.nn.softplus(-lam.astype(jnp.float32))
    a = jnp.exp(log_a)
    mult = jnp.sqrt(-jnp.expm1(2.0 * log_a))
    u = mult * (i_g * x_br).astype(jnp.float32)
    _, hs = lax.associative_scan(_lru_combine, (a, u), axis=1)
    y = jax.nn.gelu(gate_br) * hs.astype(h.dtype)
    return y @ w_out

def gla_chunk_scan(q, k, v, g):
    n_c, bsz, nh, cl, dk = q.shape
    dv = v.shape[-1]
    mask = jnp.tril(jnp.ones((cl, cl), dtype=bool))[:, :, None]

    def step(state, inp):
        qc, kc, vc, gc = inp
        big_g = jnp.cumsum(gc, axis=2)
        o_inter = jnp.einsum('bhcd,bhde->bhce', qc * jnp.exp(big_g), state)
        diff = big_g[:, :, :, None, :] - big_g[:, :, None, :, :]
        decay = jnp.exp(jnp.where(mask, diff, -jnp.inf))
        attn = jnp.einsum('bhid,bhjd,bhijd->bhij', qc, kc, decay)
        o_intra = jnp.einsum('bhij,bhje->bhie', attn, vc)
        g_last = big_g[:, :, -1:, :]
        state = jnp.exp(g_last[:, :, 0, :])[..., None] * state + jnp.einsum(
            'bhjd,bhje->bhde', kc * jnp.exp(g_last - big_g), vc)
        return state, o_inter + o_intra

    state0 = jnp.zeros((bsz, nh, dk, dv), jnp.float32)
    _, o = lax.scan(step, state0, (q, k, v, g))
    return o

def gla_mixer(h, w_in, w_alpha, b_alpha, norm_g, w_out):
    bsz, s, _ = h.shape
    proj = h @ w_in
    q, k, v, r, z = jnp.split(proj, [GLA_QK, 2 * GLA_QK, 2 * GLA_QK + D_MODEL,
                                     2 * GLA_QK + 2 * D_MODEL], axis=-1)
    log_alpha = jax.nn.log_sigmoid((z @ w_alpha + b_alpha).astype(jnp.float32)) / GLA_TAU
    n_c = s // GLA_CHUNK

    def to_chunks(t, d):
        return t.reshape(bsz, n_c, GLA_CHUNK, GLA_HEADS, d).transpose(1, 0, 3, 2, 4).astype(jnp.float32)

    o = gla_chunk_scan(to_chunks(q * (GLA_DK ** -0.5), GLA_DK), to_chunks(k, GLA_DK),
                       to_chunks(v, GLA_DV), to_chunks(log_alpha, GLA_DK))
    o = o.transpose(1, 0, 3, 2, 4).reshape(bsz, s, GLA_HEADS, GLA_DV)
    o = rmsnorm_2(o, norm_g).reshape(bsz, s, D_MODEL).astype(h.dtype)
    return (o * jax.nn.silu(r)) @ w_out

def conv_ffn(h, w_up, conv_w, conv_b, w_down):
    u = causal_dwconv(h @ w_up, conv_w, conv_b)
    g, val = jnp.split(u, 2, axis=-1)
    return (jax.nn.gelu(g) * val) @ w_down

def second_inputs(seed: int = 0) -> dict:
    key = jax.random.key(seed)
    ks = iter(jax.random.split(key, 32))

    def nrm(shape, scale):
        return jax.random.normal(next(ks), shape, jnp.float32) * scale

    d = D_MODEL
    x = nrm((BATCH, SEQ, d), 1.0)
    c = nrm((BATCH, d), 1.0)
    ada_w = nrm((DEPTH, d, 6 * d), d ** -0.5)
    ada_b = nrm((DEPTH, 6 * d), 0.01)
    norm_g = 1.0 + nrm((DEPTH, 4, d), 0.05)
    ffn_w_up = nrm((DEPTH, d, 2 * D_FF), d ** -0.5)
    ffn_conv_w = nrm((DEPTH, FFN_CONV, 2 * D_FF), FFN_CONV ** -0.5)
    ffn_conv_b = nrm((DEPTH, 2 * D_FF), 0.01)
    ffn_w_down = nrm((DEPTH, D_FF, d), D_FF ** -0.5)
    rg_w_in = nrm((N_A, d, 2 * D_RNN), d ** -0.5)
    rg_conv_w = nrm((N_A, RG_CONV, D_RNN), RG_CONV ** -0.5)
    rg_conv_b = nrm((N_A, D_RNN), 0.01)
    rg_wa = nrm((N_A, RG_BLOCKS, RG_BLOCK, RG_BLOCK), RG_BLOCK ** -0.5)
    rg_ba = nrm((N_A, D_RNN), 0.01)
    rg_wx = nrm((N_A, RG_BLOCKS, RG_BLOCK, RG_BLOCK), RG_BLOCK ** -0.5)
    rg_bx = nrm((N_A, D_RNN), 0.01)
    a_pow = jax.random.uniform(next(ks), (N_A, D_RNN), jnp.float32, 0.9, 0.999)
    a_base = a_pow ** (1.0 / RG_C)
    rg_lambda = jnp.log(a_base) - jnp.log1p(-a_base)
    rg_w_out = nrm((N_A, D_RNN, d), D_RNN ** -0.5)
    gla_w_in = nrm((N_B, d, GLA_IN), d ** -0.5)
    gla_w_alpha = nrm((N_B, GLA_RANK, GLA_QK), GLA_RANK ** -0.5)
    gla_b_alpha = nrm((N_B, GLA_QK), 0.01)
    gla_norm_g = 1.0 + nrm((N_B, GLA_DV), 0.05)
    gla_w_out = nrm((N_B, d, d), d ** -0.5)
    return {"x": x, "c": c, "ada_w": ada_w, "ada_b": ada_b, "norm_g": norm_g,
            "ffn_w_up": ffn_w_up, "ffn_conv_w": ffn_conv_w, "ffn_conv_b": ffn_conv_b,
            "ffn_w_down": ffn_w_down, "rg_w_in": rg_w_in, "rg_conv_w": rg_conv_w,
            "rg_conv_b": rg_conv_b, "rg_wa": rg_wa, "rg_ba": rg_ba, "rg_wx": rg_wx,
            "rg_bx": rg_bx, "rg_lambda": rg_lambda, "rg_w_out": rg_w_out,
            "gla_w_in": gla_w_in, "gla_w_alpha": gla_w_alpha, "gla_b_alpha": gla_b_alpha,
            "gla_norm_g": gla_norm_g, "gla_w_out": gla_w_out}

def second_block(x, c, ada_w, ada_b, norm_g, ffn_w_up, ffn_conv_w, ffn_conv_b, ffn_w_down,
              rg_w_in, rg_conv_w, rg_conv_b, rg_wa, rg_ba, rg_wx, rg_bx, rg_lambda, rg_w_out,
              gla_w_in, gla_w_alpha, gla_b_alpha, gla_norm_g, gla_w_out):
    c_act = jax.nn.silu(c)
    for i in range(DEPTH):
        mod = (c_act @ ada_w[i] + ada_b[i])[:, None, :]
        sh_m, sc_m, gt_m, sh_f, sc_f, gt_f = jnp.split(mod, 6, axis=-1)
        j = i // N_MIXERS
        h = rmsnorm_2(x, norm_g[i, 0]) * (1.0 + sc_m) + sh_m
        if i % N_MIXERS == 0:
            y = rglru_mixer(h, rg_w_in[j], rg_conv_w[j], rg_conv_b[j], rg_wa[j], rg_ba[j],
                            rg_wx[j], rg_bx[j], rg_lambda[j], rg_w_out[j])
        else:
            y = gla_mixer(h, gla_w_in[j], gla_w_alpha[j], gla_b_alpha[j], gla_norm_g[j], gla_w_out[j])
        x = x + gt_m * rmsnorm_2(y, norm_g[i, 1])
        h = rmsnorm_2(x, norm_g[i, 2]) * (1.0 + sc_f) + sh_f
        y = conv_ffn(h, ffn_w_up[i], ffn_conv_w[i], ffn_conv_b[i], ffn_w_down[i])
        x = x + gt_f * rmsnorm_2(y, norm_g[i, 3])
    return x


def setup_inputs(seed=0):
    out = dict(first_inputs(seed))
    for name, value in second_inputs(seed + 1).items():
        if name != "x":
            out[name + "_2"] = value
    return out


def reference(
    x, c, ctx, c_ctx, w_mod, b_mod, norm_w, w_in, ret_decay, ret_gn_w, sc_conv_w, cf_conv_w,
    cf_conv_b, cf_ln_w, cf_ln_b, att_sink, w_branch, w_out, final_norm_w, c_2, ada_w_2, ada_b_2,
    norm_g_2, ffn_w_up_2, ffn_conv_w_2, ffn_conv_b_2, ffn_w_down_2, rg_w_in_2, rg_conv_w_2,
    rg_conv_b_2, rg_wa_2, rg_ba_2, rg_wx_2, rg_bx_2, rg_lambda_2, rg_w_out_2, gla_w_in_2,
    gla_w_alpha_2, gla_b_alpha_2, gla_norm_g_2, gla_w_out_2,
):
    x = first_block(
        x, c, ctx, c_ctx, w_mod, b_mod, norm_w, w_in, ret_decay, ret_gn_w, sc_conv_w, cf_conv_w,
        cf_conv_b, cf_ln_w, cf_ln_b, att_sink, w_branch, w_out, final_norm_w,
    )
    return second_block(
        x, c_2, ada_w_2, ada_b_2, norm_g_2, ffn_w_up_2, ffn_conv_w_2, ffn_conv_b_2,
        ffn_w_down_2, rg_w_in_2, rg_conv_w_2, rg_conv_b_2, rg_wa_2, rg_ba_2, rg_wx_2, rg_bx_2,
        rg_lambda_2, rg_w_out_2, gla_w_in_2, gla_w_alpha_2, gla_b_alpha_2, gla_norm_g_2,
        gla_w_out_2,
    )


_drawn_inputs = setup_inputs


def setup_inputs(seed=0):
    import zlib

    import numpy as np

    out = dict(_drawn_inputs(seed))
    spreads = {}
    factors = {'cf_conv_b': 6.894,
     'cf_ln_b': 8.0,
     'att_sink': 8.0,
     'ffn_conv_b_2': 7.082,
     'rg_conv_b_2': 4.303,
     'rg_ba_2': 48.635,
     'rg_bx_2': 22.341,
     'gla_b_alpha_2': 8.0}
    for name, (base, spread) in spreads.items():
        noise = np.random.default_rng([zlib.crc32(name.encode()), seed]).standard_normal(out[name].shape)
        drawn = base * np.exp(spread * noise) if base else spread * noise
        out[name] = jnp.asarray(drawn.astype(out[name].dtype))
    for name, factor in factors.items():
        out[name] = (out[name] * factor).astype(out[name].dtype)
    return out
```

```python
from contextlib import ExitStack

import numpy as np
import concourse.bass as bass
from concourse import mybir

F32 = mybir.dt.float32
ACT = mybir.ActivationFunctionType
ALU = mybir.AluOpType
AX_X = mybir.AxisListType.X

P = 128
D = 1024
KT = D // P
S = 256
ST = S // P
BW = 512
BT = BW // P
HEADS = 4
ATT_DH = 64
ATT_SCALE = ATT_DH ** -0.5
K_SCALE = 128 ** -0.5
SC_K, CF_K, FF_K, RG_K = 3, 31, 3, 4
PAD = CF_K // 2
D_FF = 2816
FT = D_FF // P
GLA_H = 4
GLA_DK = 128
EPS = 1e-6
LEVELS = (1, 2, 4, 8, 16, 32, 64)
RING = 6
SLAB = 2048
BANKS = 8

IN_COL = dict(ret_q=0, ret_k=512, ret_v=1024, ret_z=1536, sc_b=2048, sc_c=2560, sc_x=3072, sc_z=3584,
              cf_a=4096, cf_g=4608, cf_z=5120, att_q=5632, att_kv=6144, att_z=6400, gates=6912)
BRANCHES = dict(ret=0, sc=1, cf=2, att=3)
MERGE_ORDER = ("sc", "ret", "att", "cf")

PARAMS = dict(norm_w=2 * 8, gn_w=2 * 4, sc_w=2 * 4 * SC_K, cf_w=2 * 4 * CF_K, cf_b=2 * 4, ln_w=2 * 4, ln_b=2 * 4,
              sink=2 * 8, b_mod=2 * 24, fin_w=8, decay=16, lam=8, c_vec=24,
              ada_b=2 * 48, norm_g=2 * 4 * 8, ff_w=2 * FF_K * 44, ff_b=2 * 44,
              rg_w=RG_K * 8, rg_b=8, rg_ba=8, rg_bx=8, gla_b=4, gla_g=2, gla_z=8 * 16)
TABLES = dict(ident=P, ones=S, turn=P, cos=S, sin=S, ahead=2 * S, behind=2 * S, q_pos=2 * S, k_pos=4,
              band=2 * P, eps=1)
LATE = 8 * P


def offsets(sizes):
    at, out = 0, {}
    for name, n in sizes.items():
        out[name] = (at, n)
        at += n
    return out, at


PARAM_AT, N_PARAM = offsets(PARAMS)
TABLE_AT, N_TABLE = offsets(TABLES)


class Steps:

    def __init__(self, sem, known):
        self.sem, self.known, self.n, self.now = sem, known, 0, {}

    def does(self, *names):
        self.n += 1
        for name in names:
            assert name not in self.now, name
            self.now[name] = self.n
        return self.sem, 1

    def did(self, name):
        if name in self.now:
            return self.sem, self.now[name]
        return self.sem, (self.known[name] if self.known is not None else 1)


def program(nc, io, counts):
    ctx = ExitStack()
    with ctx:
        def sbuf(name, cols):
            return ctx.enter_context(nc.sbuf_tensor(name, [P, cols], F32))

        def sem(name):
            return ctx.enter_context(nc.semaphore(name))

        counts = counts or dict(tensor=None, vector=None, scalar=None)
        tensor = Steps(sem("tensor_done"), counts["tensor"])
        vector = Steps(sem("vector_done"), counts["vector"])
        scalar = Steps(sem("scalar_done"), counts["scalar"])

        def emptied(name):
            for e in (vector, scalar):
                if "emptied " + name in (e.known or {}):
                    return e.did("emptied " + name)
            return vector.sem, 1

        slab_landed = [sem(f"slab_landed{i}") for i in range(RING)]
        params_landed, tables_landed = sem("params_landed"), sem("tables_landed")
        x_landed, late_landed, out_landed = sem("x_landed"), sem("late_landed"), sem("out_landed")

        ring = [sbuf(f"ring{i}", SLAB) for i in range(RING)]
        params, tables = sbuf("params", N_PARAM), sbuf("tables", N_TABLE)
        xT = sbuf("xT", KT * 2 * S)[:].rearrange("p (t s) -> p t s", t=KT)
        hT = sbuf("hT", KT * 2 * S)[:].rearrange("p (t s) -> p t s", t=KT)

        def param(name, *dims):
            at, n = PARAM_AT[name]
            ap = params[:, at:at + n]
            if len(dims) == 1:
                return ap.rearrange("p (a b) -> p a b", a=dims[0])
            if len(dims) == 2:
                return ap.rearrange("p (a b c) -> p a b c", a=dims[0], b=dims[1])
            if len(dims) == 3:
                return ap.rearrange("p (a b c d) -> p a b c d", a=dims[0], b=dims[1], c=dims[2])
            return ap

        def table(name):
            at, n = TABLE_AT[name]
            return tables[:, at:at + n]

        ident, ones, turn = table("ident"), table("ones"), table("turn")
        ones_pp = ones[:, 0:P]
        eps = table("eps")
        at = TABLE_AT["ahead"][0]
        level = tables[:, at:at + LATE]
        gla_a = tables[0:16, at + LATE:at + LATE + 512]

        arena_cols = 20740
        arena = sbuf("arena", arena_cols)

        def carve(at, *dims):
            n = int(np.prod(dims))
            assert at + n <= arena_cols, (at, dims)
            ap = arena[:, at:at + n]
            if len(dims) == 2:
                return ap.rearrange("p (a b) -> p a b", a=dims[0])
            if len(dims) == 3:
                return ap.rearrange("p (a b c) -> p a b c", a=dims[0], b=dims[1])
            if len(dims) == 4:
                return ap.rearrange("p (a b c d) -> p a b c d", a=dims[0], b=dims[1], c=dims[2])
            return ap

        cx = carve(0, BT, 2, S + 2)
        ret_o = carve(0, BT, 2 * S)
        s_br = carve(2064, BT, 2 * S)
        u_pad = carve(4112, BT, 2, S + 2 * PAD)
        att_o = carve(4112, BT, 2 * S)
        f_br = carve(6400, BT, 2 * S)
        ret_q, ret_k = carve(8448, BT, 2 * S), carve(10496, BT, 2 * S)
        merged = carve(8448, KT, 2 * S)
        ret_v = carve(12544, 2 * ST, BW)
        att_q = carve(14592, BT, 2 * S)
        att_k, att_ks = carve(16640, 2 * S), carve(17152, 2 * S)
        att_v = carve(17664, 2 * ST, P)
        state = carve(18176, HEADS, 2, P)
        k_wt = [carve(4112 + 1024 * i, ST, HEADS, P) for i in range(2)]
        branch = dict(ret=ret_o, sc=s_br, cf=f_br, att=att_o)

        yT, sq8 = carve(0, KT, S), carve(2048, KT, S)
        xb_pad = carve(4096, KT, S + RG_K - 1)
        xc, gel, rr, tt_, ix = (carve(6176 + 2048 * i, KT, S) for i in range(5))
        a2 = carve(6176 + 2048 * 5, KT, S)
        lv = carve(0, 8, GLA_H * S)
        gla_o = carve(4096, KT, S)
        gq, gk, la, le, gg = (carve(8192 + 1024 * i, GLA_H, S) for i in range(5))
        lprod = carve(13312, 8, P)
        attT = carve(14336, GLA_H, ST, S)
        r_sil = carve(16384, KT, S)
        gv = carve(18432, ST, D)
        zT = carve(20480, S)
        ff_act = carve(4096, FT, S)

        work = [sbuf(f"work{i}", 2 * S) for i in range(8)]
        act_t = work[0:4]
        dve_t = work[4:8]
        stat = sbuf("stat", 2 * S)
        stat2 = sbuf("stat2", 2 * S)
        small = sbuf("small", 256)
        soft_m, soft_s = small[:, 0:8], small[:, 8:16]
        soft_e, soft_d = small[:, 16:24], small[:, 24:32]
        csil = small[:, 32:56].rearrange("p (t v) -> p t v", t=KT)
        soft_p = small[:, 56:80]
        k_decay = small[:, 80:112].rearrange("p (l d t h) -> p l d t h", l=2, d=2, t=2)
        nsink = small[:, 112:128].rearrange("p (l h) -> p l h", l=2)
        lp = [small[:, 128 + 24 * i:152 + 24 * i] for i in range(4)]
        log_g = small[:, 224:240].rearrange("p (l d h) -> p l d h", l=2, d=2)
        lam8, lam8n = small[:, 240:248], small[:, 248:256]
        rows = [sbuf(f"rows{i}", 2 * P) for i in range(2)]
        mods = sbuf("mods", 2 * 48 + 2 * 16 + 2 * 48 + 2 * 32)
        mod1 = [mods[:, 48 * l:48 * l + 48].rearrange("p (n v) -> p n v", v=2) for l in range(2)]
        gain1 = [mods[:, 96 + 16 * l:112 + 16 * l].rearrange("p (n v) -> p n v", v=2) for l in range(2)]
        mod2 = [mods[:, 128 + 48 * l:176 + 48 * l] for l in range(2)]
        gain2 = [mods[:, 224 + 32 * l:256 + 32 * l].rearrange("p (q t) -> p q t", q=4) for l in range(2)]

        psum = [ctx.enter_context(nc.psum_tensor(f"bank{i}", [P, 512], F32)) for i in range(BANKS)]
        bank_at = {}

        def bank(name):
            return psum[bank_at[name] % BANKS]

        stream = []

        def by_rows(w):
            return w.rearrange("(t p) n -> p t n", p=P)

        def cols(name, w, c0, n=256):
            src = by_rows(w)[:, :, c0:c0 + n]
            stream.append((name, src, (src.shape[1], n)))

        def section(l, name, i):
            cols(f"w {name} {l}.{i}", io["w_in"][l], IN_COL[name] + 256 * i)

        mod_at = {"start": [("mod", 0, i) for i in range(12)],
                  "att 0": [("mod", 1, i) for i in range(12)],
                  "gv 0": [("ada", 0, i) for i in range(0, 5)],
                  "n1 1": [("ada", 0, i) for i in range(5, 10)],
                  "att 1": [("ada", 0, i) for i in range(10, 18)],
                  "gv 1": [("ada", 0, i) for i in range(18, 24)],
                  "fin": [("ada", 1, i) for i in range(0, 5)],
                  "n2 0": [("ada", 1, i) for i in range(5, 10)],
                  "rg": [("ada", 1, i) for i in range(10, 16)],
                  "post rg": [("ada", 1, i) for i in range(16, 20)],
                  "n3 0": [("ada", 1, i) for i in range(20, 24)]}

        def mod_slabs(at):
            for kind, l, i in mod_at[at]:
                cols(f"w {kind} {l}.{i}", io["w_mod" if kind == "mod" else "ada_w_2"][l], 256 * i)

        mod_slabs("start")
        for l in range(2):
            if l:
                mod_slabs("n1 1")
            for a, b in (("sc_c", "sc_x"), ("cf_g", "cf_a")):
                for i in range(2):
                    section(l, a, i)
                    section(l, b, i)
            for a in ("ret_q", "ret_k", "ret_v", "att_q"):
                for i in range(2):
                    section(l, a, i)
            section(l, "att_kv", 0)
            for i in range(2):
                section(l, "sc_b", i)
                section(l, "sc_z", i)
            mod_slabs(f"att {l}")
            mod_slabs(f"gv {l}")
            for a in ("ret_z", "att_z", "cf_z"):
                for i in range(2):
                    section(l, a, i)
            for b in MERGE_ORDER:
                for c in range(2):
                    cols(f"w branch {l}.{b}.{c}", io["w_branch"][l, BRANCHES[b]], 512 * c, 512)
                    for i in range(2):
                        cols(f"w gate {l}.{b}.{2 * c + i}", io["w_in"][l],
                             IN_COL["gates"] + D * BRANCHES[b] + 512 * c + 256 * i)
            for i in range(4):
                cols(f"w out {l}.{i}", io["w_out"][l], 256 * i)

        def mod_turns(at, n):
            last = len(mod_at[at])
            return [b for b in ((n - 2, n - 1) if n == last else (n - 2,)) if b >= 0]

        def mod_col(at, b, j):
            return 256 + 4 * (b % 2) + 2 * j

        def ffn_slabs(l):
            for i in range(11):
                cols(f"w ffg {l}.{i}", io["ffn_w_up_2"][l], 256 * i)
                cols(f"w ffv {l}.{i}", io["ffn_w_up_2"][l], D_FF + 256 * i)
            down = by_rows(io["ffn_w_down_2"][l])
            for c in range(4):
                for k0 in range(0, FT, 8):
                    n = min(8, FT - k0)
                    stream.append((f"w down {l}.{c}.{k0}", down[:, k0:k0 + n, 256 * c:256 * c + 256], (n, 256)))

        mod_slabs("fin")
        mod_slabs("n2 0")
        for i in range(4):
            cols(f"w rgx {i}", io["rg_w_in_2"][0], D + 256 * i)
        for i in range(4):
            cols(f"w rgg {i}", io["rg_w_in_2"][0], 256 * i)
        for n in ("a", "x"):
            stream.append((f"w rg{n}", io[f"rg_w{n}_2"][0].rearrange("g (t p) n -> p (g t) n", p=P), (8, 256)))
        mod_slabs("rg")
        for i in range(4):
            cols(f"w rgo {i}", io["rg_w_out_2"][0], 256 * i)
        mod_slabs("post rg")
        mod_slabs("n3 0")
        ffn_slabs(0)
        for n, c0, k in (("q", 0, 2), ("k", 512, 2), ("v", 1024, 4), ("r", 2048, 4)):
            for i in range(k):
                cols(f"w gla{n} {i}", io["gla_w_in_2"][0], c0 + 256 * i)
        for i in range(4):
            cols(f"w glao {i}", io["gla_w_out_2"][0], 256 * i)
        ffn_slabs(1)

        def slot_of(n):
            a, b = stream[n][2]
            return ring[n % RING][:, 0:a * b].rearrange("p (a b) -> p a b", a=a)

        block = ctx.enter_context(nc.Block())

        @block.tensor
        def _(pe):
            state_ = dict(slab=0, bank=0)

            def take(name):
                n = state_["slab"]
                assert stream[n][0] == name, (stream[n][0], name)
                state_["slab"] += 1
                pe.wait_ge(slab_landed[n % RING], 16 * (n // RING + 1))
                return slot_of(n)

            def open_bank(name):
                n = state_["bank"]
                state_["bank"] += 1
                bank_at[name] = n
                if n >= BANKS:
                    pe.wait_ge(*emptied(order[n - BANKS]))
                order.append(name)
                return psum[n % BANKS]

            order = []

            def tile(name, w, c0, rhs, n, free=None):
                out = open_bank(name)
                nk = w.shape[1]
                for k in range(nk):
                    m = pe.matmul(out[:, 0:n], w[:, k, c0:c0 + P], rhs(k), start=k == 0, stop=k == nk - 1)
                m.then_inc(*tensor.does("filled " + name, *([f"used {free}"] if free else [])))

            def h(n):
                return lambda k: hT[:, k, 0:n]

            def project(l, name, n, i, tag=None):
                w = take(f"w {name} {l}.{i}")
                for j in range(2):
                    tile(f"{name} {l}.{2 * i + j}", w, P * j, h(n), n, f"w {name} {l}.{i}" if j else None)

            def mod_step(at, n):
                todo = mod_at[at]
                name = "%s %d.%d" % todo[n] if n < len(todo) else "end " + at
                w = take("w " + name) if n < len(todo) else None
                out = open_bank("row " + name)
                if w is not None:
                    vecs = csil[:, :, 0:2] if todo[n][0] == "mod" else csil[:, :, 2:3]
                    for k in range(KT):
                        m = pe.matmul(out[0:vecs.shape[2], 0:256], vecs[:, k, :], w[:, k, :],
                                      start=k == 0, stop=k == KT - 1)
                for b in mod_turns(at, n):
                    kind, l, i = todo[b]
                    nv = 2 if kind == "mod" else 1
                    pe.wait_ge(*scalar.did(f"row {kind} {l}.{i}"))
                    for j in range(2):
                        c = mod_col(at, b, j)
                        m = pe.transpose(out[:, c:c + nv], rows[b % 2][0:nv, P * j:P * j + P], ident[0:nv, 0:nv])
                m.then_inc(*tensor.does("filled row " + name, *(["used w " + name] if w is not None else [])))

            def modulations(at):
                for n in range(len(mod_at[at]) + 1):
                    mod_step(at, n)

            def sum_squares(name, n, tiles):
                out = open_bank(name)
                for k in range(tiles):
                    pe.wait_ge(*scalar.did(f"sq {name}.{k}"))
                    m = pe.matmul(out[:, 0:n], ones_pp, squares(name, k, n), start=k == 0, stop=k == tiles - 1)
                    m.then_inc(*tensor.does(f"summed {name}.{k}", *(["filled " + name] if k == tiles - 1 else [])))

            def squares(name, k, n):
                return act_t[k % 4][:, 0:n]

            def h_ready(name):
                for k in range(KT):
                    pe.wait_ge(*scalar.did(f"h {name}.{k}"))

            pe.wait_ge(params_landed, 16)
            pe.wait_ge(tables_landed, 16)
            pe.wait_ge(*scalar.did("csil"))

            for l in range(2):
                nx = 2 * S if l == 0 else S
                groups = (0, 1) if l == 0 else (0,)
                sum_squares(f"n1 {l}", 2 * S, KT)
                modulations("n1 1" if l else "start")
                h_ready(f"n1 {l}")
                for a, b in (("sc_c", "sc_x"), ("cf_g", "cf_a")):
                    for i in range(2):
                        project(l, a, nx, i)
                        project(l, b, nx, i)
                for i in range(2):
                    project(l, "ret_q", nx, i)
                for i in range(2):
                    project(l, "ret_k", 2 * S, i)
                for i in range(2):
                    w = take(f"w ret_v {l}.{i}")
                    for t in range(2 * ST):
                        name = f"ret_v {l}.{i}.{t}"
                        out = open_bank(name)
                        for k in range(KT):
                            m = pe.matmul(out[:, 0:256], hT[:, k, P * t:P * t + P], w[:, k, :],
                                          start=k == 0, stop=k == KT - 1)
                        m.then_inc(*tensor.does("filled " + name, *([f"used w ret_v {l}.{i}"] if t == 2 * ST - 1 else [])))
                for i in range(2):
                    project(l, "att_q", nx, i)
                w = take(f"w att_kv {l}.0")
                tile(f"att_k {l}", w, 0, h(2 * S), 2 * S)
                out = open_bank(f"att_v {l}")
                for t in range(2 * ST):
                    for k in range(KT):
                        m = pe.matmul(out[:, P * t:P * t + P], hT[:, k, P * t:P * t + P], w[:, k, P:2 * P],
                                      start=k == 0, stop=k == KT - 1)
                m.then_inc(*tensor.does(f"filled att_v {l}", f"used w att_kv {l}.0"))
                for i in range(2):
                    project(l, "sc_b", nx, i)
                    project(l, "sc_z", nx, i)

                for t in range(BT + 1):
                    src = att_q[:, t, 0:S] if t < BT else att_k[:, 0:S]
                    pe.wait_ge(*scalar.did(f"att_q {l}.{t}" if t < BT else f"att_k {l}"))
                    out = open_bank(f"turn {l}.{t}")
                    pe.matmul(out[:, 0:S], turn, src, start=True, stop=True)\
                        .then_inc(*tensor.does(f"filled turn {l}.{t}"))

                for t in range(ST):
                    out = open_bank(f"kT {l}.{t}")
                    for hd in range(HEADS):
                        pe.wait_ge(*scalar.did(f"ret_k {l}.{hd}"))
                        m = pe.transpose(out[:, P * hd:P * hd + P], ret_k[:, hd, S + P * t:S + P * t + P], ident)
                    m.then_inc(*tensor.does(f"filled kT {l}.{t}"))
                pe.wait_ge(*scalar.did(f"ret_v {l}.1.{2 * ST - 1}"))
                for hd in range(HEADS):
                    out = open_bank(f"state {l}.{hd}")
                    for d in range(2):
                        pe.wait_ge(*vector.did(f"k_wt {l}.{ST - 1}.{d}"))
                        for t in range(ST):
                            m = pe.matmul(out[:, P * d:P * d + P], k_wt[d][:, t, hd, :],
                                          ret_v[:, ST + t, P * hd:P * hd + P], start=t == 0, stop=t == ST - 1)
                    m.then_inc(*tensor.does(f"filled state {l}.{hd}"))

                units = [(hd, g) for hd in range(HEADS) for g in groups]

                def ret_scores(hd, g):
                    name = f"rs {l}.{hd}.{g}"
                    pe.wait_ge(*scalar.did(f"ret_q {l}.{hd}"))
                    out = open_bank(name)
                    for j in range(ST):
                        m = pe.matmul(out[:, S * j:S * j + S], ret_k[:, hd, S * g + P * j:S * g + P * j + P],
                                      ret_q[:, hd, S * g:S * g + S], start=True, stop=True)
                    m.then_inc(*tensor.does("filled " + name))

                def ret_out(hd, g):
                    name = f"ro {l}.{hd}.{g}"
                    pe.wait_ge(*vector.did(f"ret_p {l}.{hd}.{g}"))
                    p_t = dve_t[2 + units.index((hd, g)) % 2]
                    out = open_bank(name)
                    for j in range(ST):
                        m = pe.matmul(out[:, 0:S], ret_v[:, ST * g + j, P * hd:P * hd + P], p_t[:, S * j:S * j + S],
                                      start=j == 0, stop=g == 1 and j == ST - 1)
                    if g == 0:
                        pe.wait_ge(*scalar.did(f"state {l}.{hd}"))
                        pe.wait_ge(*vector.did(f"q_wt {l}.{hd}"))
                        for d in range(2):
                            m = pe.matmul(out[:, 0:S], state[:, hd, d, :], dve_t[hd % 2][:, S * d:S * d + S],
                                          start=False, stop=d == 1)
                    m.then_inc(*tensor.does("filled " + name))

                for n, (hd, g) in enumerate(units):
                    ret_scores(hd, g)
                    if n:
                        ret_out(*units[n - 1])
                ret_out(*units[-1])

                att = [(g, t, q) for g in groups for t in range(BT) for q in range(ST)]

                def att_scores(i):
                    g, t, q = att[i]
                    keys = 0 if g == 0 else S
                    for s in range(2):
                        name = f"as {l}.{i}.{s}"
                        rows = slice(64 * s, 64 * s + 64)
                        k_src = att_k if s == t // 2 else att_ks
                        out = open_bank(name)
                        pe.matmul(out[:, 0:2 * S - keys], att_q[rows, t, S * g + P * q:S * g + P * q + P],
                                  k_src[rows, keys:2 * S], start=True, stop=True)\
                            .then_inc(*tensor.does("filled " + name))

                def att_turn(i):
                    g, t, q = att[i]
                    for s in range(2):
                        name = f"at {l}.{i}.{s}"
                        pe.wait_ge(*vector.did(f"att_p {l}.{i}.{s}"))
                        out = open_bank(name)
                        for b in range(4 - 2 * g):
                            m = pe.transpose(out[:, P * b:P * b + P], dve_t[2 * (i % 2) + s][:, P * b:P * b + P], ident)
                        m.then_inc(*tensor.does("filled " + name))

                def att_out(i):
                    g, t, q = att[i]
                    name = f"ao {l}.{i}"
                    out = open_bank(name)
                    for s in range(2):
                        pe.wait_ge(*scalar.did(f"att_t {l}.{i}.{s}"))
                        nb = 4 - 2 * g
                        c = 64 * (t // 2)
                        for b in range(nb):
                            m = pe.matmul(out[64 * s:64 * s + 64, 0:P], att_v[:, 2 * g + b, c:c + 64],
                                          act_t[2 + s][:, P * b:P * b + P], start=b == 0, stop=b == nb - 1)
                    m.then_inc(*tensor.does("filled " + name))

                pe.wait_ge(*vector.did(f"att_q roped {l}.{BT - 1}"))
                pe.wait_ge(*vector.did(f"att_ks {l}"))
                pe.wait_ge(*scalar.did(f"att_v {l}"))
                for i in range(len(att) + 2):
                    if i < len(att):
                        att_scores(i)
                    if i <= len(mod_at[f"att {l}"]):
                        mod_step(f"att {l}", i)
                    if 1 <= i <= len(att):
                        att_turn(i - 1)
                    if i >= 2:
                        att_out(i - 2)

                for hd in range(HEADS):
                    pe.wait_ge(*scalar.did(f"ret_o {l}.{hd}.{groups[-1]}"))
                    name = f"gm {l}.{hd}"
                    out = open_bank(name)
                    pe.matmul(out[:, 0:nx], ones_pp, ret_o[:, hd, 0:nx], start=True, stop=True)\
                        .then_inc(*tensor.does("filled " + name))
                name = f"lm {l}"
                out = open_bank(name)
                for t in range(BT):
                    pe.wait_ge(*vector.did(f"conv {l}.{t}"))
                    m = pe.matmul(out[:, 0:nx], ones_pp, f_br[:, t, 0:nx], start=t == 0, stop=t == BT - 1)
                m.then_inc(*tensor.does("filled " + name))
                for hd in range(HEADS):
                    sum_squares(f"gv {l}.{hd}", nx, 1)
                sum_squares(f"lv {l}", nx, BT)
                modulations(f"gv {l}")

                for a in ("ret_z", "att_z", "cf_z"):
                    for i in range(2):
                        project(l, a, nx, i)

                for b in MERGE_ORDER:
                    for t in range(BT):
                        pe.wait_ge(*vector.did(f"branch {l}.{b}.{t}"))
                    for c in range(2):
                        wb = take(f"w branch {l}.{b}.{c}")
                        for j in range(4):
                            n = 4 * c + j
                            if j % 2 == 0:
                                wg = take(f"w gate {l}.{b}.{n // 2}")
                            tile(f"gate {l}.{b}.{n}", wg, P * (j % 2), h(nx), nx,
                                 f"w gate {l}.{b}.{n // 2}" if j % 2 else None)
                            tile(f"br {l}.{b}.{n}", wb, P * j, lambda k: branch[b][:, k, 0:nx], nx,
                                 f"w branch {l}.{b}.{c}" if j == 3 else None)
                for k in range(KT):
                    pe.wait_ge(*vector.did(f"merged {l}.{MERGE_ORDER[-1]}.{k}"))
                for i in range(4):
                    w = take(f"w out {l}.{i}")
                    for j in range(2):
                        tile(f"out {l}.{2 * i + j}", w, P * j, lambda k: merged[:, k, 0:nx], nx,
                             f"w out {l}.{i}" if j else None)

            sum_squares("fin", S, KT)
            modulations("fin")

            def ffn(l):
                sum_squares(f"n3 {l}", S, KT)
                if l == 0:
                    modulations("n3 0")
                h_ready(f"n3 {l}")
                for i in range(11):
                    for nm in ("ffg", "ffv"):
                        w = take(f"w {nm} {l}.{i}")
                        for j in range(2):
                            tile(f"{nm} {l}.{2 * i + j}", w, P * j, h(S), S, f"w {nm} {l}.{i}" if j else None)
                for c in range(4):
                    slabs = [(k0, take(f"w down {l}.{c}.{k0}")) for k0 in range(0, FT, 8)]
                    for j in range(2):
                        name = f"y ffn {l}.{2 * c + j}"
                        out = open_bank(name)
                        for k0, w in slabs:
                            for k in range(w.shape[1]):
                                if c == 0 and j == 0:
                                    pe.wait_ge(*vector.did(f"ff_act {l}.{k0 + k}"))
                                m = pe.matmul(out[:, 0:S], w[:, k, P * j:P * j + P], ff_act[:, k0 + k, :],
                                              start=k0 + k == 0, stop=k0 + k == FT - 1)
                            if j == 1:
                                names = [f"used w down {l}.{c}.{k0}"]
                                if k0 + 8 >= FT:
                                    names.append("filled " + name)
                                m.then_inc(*tensor.does(*names))
                        if j == 0:
                            m.then_inc(*tensor.does("filled " + name))
                post(f"ffn {l}")

            def post(tag):
                out = open_bank(f"ys {tag}")
                for k in range(KT):
                    pe.wait_ge(*scalar.did(f"y {tag}.{k}"))
                    m = pe.matmul(out[:, 0:S], ones_pp, sq8[:, k, :], start=k == 0, stop=k == KT - 1)
                m.then_inc(*tensor.does(f"filled ys {tag}"))

            sum_squares("n2 0", S, KT)
            modulations("n2 0")
            h_ready("n2 0")
            for nm in ("rgx", "rgg"):
                for i in range(4):
                    w = take(f"w {nm} {i}")
                    for j in range(2):
                        tile(f"{nm} {2 * i + j}", w, P * j, h(S), S, f"w {nm} {i}" if j else None)
            for nm in ("rga", "rgx2"):
                slab = "w rga" if nm == "rga" else "w rgx"
                w = take(slab)
                for n in range(KT):
                    gblk, j = n // 2, n % 2
                    out = open_bank(f"{nm} {n}")
                    for i in range(2):
                        pe.wait_ge(*vector.did(f"xc {2 * gblk + i}"))
                        m = pe.matmul(out[:, 0:S], w[:, 2 * gblk + i, P * j:P * j + P], xc[:, 2 * gblk + i, :],
                                      start=i == 0, stop=i == 1)
                    m.then_inc(*tensor.does(f"filled {nm} {n}", *([f"used {slab}"] if n == KT - 1 else [])))
            modulations("rg")
            for k in range(KT):
                pe.wait_ge(*vector.did(f"rg_y {k}"))
            for i in range(4):
                w = take(f"w rgo {i}")
                for j in range(2):
                    tile(f"y rg.{2 * i + j}", w, P * j, lambda k: xc[:, k, :], S, f"w rgo {i}" if j else None)
            post("rg")
            modulations("post rg")
            ffn(0)

            sum_squares("n2 1", S, KT)
            h_ready("n2 1")
            wz, wa = param("gla_z", KT), gla_a
            out = open_bank("gla z")
            for k in range(KT):
                m = pe.matmul(out[0:16, 0:S], wz[:, k, :], hT[:, k, 0:S], start=k == 0, stop=k == KT - 1)
            m.then_inc(*tensor.does("filled gla z"))
            pe.wait_ge(*scalar.did("zT"))
            pe.wait_ge(late_landed, 32)
            for hd in range(GLA_H):
                out = open_bank(f"alpha {hd}")
                pe.matmul(out[:, 0:S], wa[:, P * hd:P * hd + P], zT[0:16, :], start=True, stop=True)\
                    .then_inc(*tensor.does(f"filled alpha {hd}"))
            for nm in ("q", "k"):
                for i in range(2):
                    w = take(f"w gla{nm} {i}")
                    for j in range(2):
                        tile(f"gla{nm} {2 * i + j}", w, P * j, h(S), S, f"w gla{nm} {i}" if j else None)
            for i in range(4):
                w = take(f"w glav {i}")
                for t in range(ST):
                    out = open_bank(f"glav {i}.{t}")
                    for k in range(KT):
                        m = pe.matmul(out[:, 0:256], hT[:, k, P * t:P * t + P], w[:, k, :],
                                      start=k == 0, stop=k == KT - 1)
                    m.then_inc(*tensor.does(f"filled glav {i}.{t}", *([f"used w glav {i}"] if t else [])))
            for n in range(GLA_H * ST):
                hd, t = n // ST, n % ST
                sl = slice(S * hd + P * t, S * hd + P * t + P)
                for half in range(2):
                    name = f"lev {n}.{half}"
                    for q in range(4):
                        if n == 0:
                            pe.wait_ge(*vector.did(f"lv {4 * half + q}"))
                    out = open_bank(name)
                    for q in range(4):
                        i = 4 * half + q
                        if i < len(LEVELS):
                            m = pe.matmul(out[:, P * q:P * q + P], lv[:, i, sl], lv[:, i, sl], start=True, stop=True)
                        else:
                            m = pe.matmul(out[:, P * q:P * q + P], gk[:, hd, P * t:P * t + P],
                                          gq[:, hd, P * t:P * t + P], start=True, stop=True)
                    m.then_inc(*tensor.does("filled " + name))
                if t == 1:
                    out = open_bank(f"cross {hd}")
                    pe.matmul(out[:, 0:P], lv[:, 7, S * hd:S * hd + P], lv[:, 7, S * hd + P:S * hd + S],
                              start=True, stop=True).then_inc(*tensor.does(f"filled cross {hd}"))
                if n % 2 == 0:
                    w = take(f"w glar {n // 2}")
                tile(f"glar {n}", w, P * (n % 2), h(S), S, f"w glar {n // 2}" if n % 2 else None)
            pe.wait_ge(*scalar.did("gv 3.1"))
            for hd in range(GLA_H):
                for j in range(ST):
                    pe.wait_ge(*vector.did(f"attT {ST * hd + j}"))
                pe.wait_ge(*scalar.did(f"cross {hd}"))
                for e in range(2):
                    name = f"go {2 * hd + e}"
                    out = open_bank(name)
                    c = 256 * hd + P * e
                    pe.matmul(out[:, 0:S], gv[:, 0, c:c + P], attT[:, hd, 0, :], start=True, stop=False)
                    pe.matmul(out[:, P:S], gv[:, 1, c:c + P], attT[:, hd, 1, P:S], start=False, stop=True)\
                        .then_inc(*tensor.does("filled " + name))
            for hd in range(GLA_H):
                out = open_bank(f"gs {hd}")
                for e in range(2):
                    pe.wait_ge(*scalar.did(f"go {2 * hd + e}"))
                    m = pe.matmul(out[:, 0:S], ones_pp, sq8[:, 2 * hd + e, :], start=e == 0, stop=e == 1)
                m.then_inc(*tensor.does(f"filled gs {hd}"))
            for k in range(KT):
                pe.wait_ge(*vector.did(f"gla_y {k}"))
            for i in range(4):
                w = take(f"w glao {i}")
                for j in range(2):
                    tile(f"y gla.{2 * i + j}", w, P * j, lambda k: gla_o[:, k, :], S, f"w glao {i}" if j else None)
            post("gla")
            ffn(1)
            assert state_["slab"] == len(stream)

        @block.sync
        def _(sp):
            sp.dma_start(params[:], io["params"]).then_inc(params_landed, 16)
            sp.dma_start(xT[:, :, 0:S], by_rows(io["x"])).then_inc(x_landed, 16)
            sp.dma_start(xT[:, :, S:2 * S], by_rows(io["ctx"])).then_inc(x_landed, 16)
            sp.dma_start(tables[:], io["tables"]).then_inc(tables_landed, 16)
            for n, (name, src, _) in enumerate(stream):
                if name == "w rgo 0":
                    sp.wait_ge(*vector.did(f"expo 1.{HEADS - 1}"))
                    sp.wait_ge(*scalar.did(f"q_dec 1.{HEADS - 1}"))
                    sp.dma_start(level, io["level"]).then_inc(late_landed, 16)
                    sp.dma_start(gla_a, io["gla_w_alpha_2"][0]).then_inc(late_landed, 16)
                if n >= RING:
                    sp.wait_ge(*tensor.did("used " + stream[n - RING][0]))
                sp.dma_start(slot_of(n), src).then_inc(slab_landed[n % RING], 16)
            for k in range(KT):
                sp.wait_ge(*vector.did(f"x ffn 1.{k}"))
                sp.dma_start(by_rows(io["out"])[:, k, :], xT[:, k, 0:S]).then_inc(out_landed, 16)
            sp.wait_ge(out_landed, 16 * KT)

        @block.scalar
        def _(act):
            def evacuate(name, dst, func=ACT.Copy, also=(), last=True, **kw):
                act.wait_ge(*tensor.did("filled " + name))
                names = list(also) + ([f"emptied {name}"] if last else [])
                return nc.scalar.activation(dst, bank(name)[0:dst.shape[0], 0:int(np.prod(dst.shape[1:]))], func, **kw)\
                    .then_inc(*scalar.does(*names))

            def square_all(name, n, tiles, src, ready=None):
                for k in range(tiles):
                    if ready:
                        act.wait_ge(*ready(k))
                    if k >= 4:
                        act.wait_ge(*tensor.did(f"summed {name}.{k - 4}"))
                    nc.scalar.activation(act_t[k % 4][:, 0:n], src(k), ACT.Square)\
                        .then_inc(*scalar.does(f"sq {name}.{k}"))

            def deviation(name, n, count):
                evacuate(name, stat[:, 0:n], ACT.Sqrt, [f"dev {name}"], scale=1.0 / count, bias=eps)

            def mod_row(at, n):
                todo = mod_at[at]
                name = "row %s %d.%d" % todo[n] if n < len(todo) else f"row end {at}"
                turned = mod_turns(at, n)
                if n < len(todo):
                    evacuate(name, rows[n % 2][0:2 if todo[n][0] == "mod" else 1, :], also=[name], last=not turned)
                else:
                    act.wait_ge(*tensor.did("filled " + name))
                for b in turned:
                    kind, l, i = todo[b]
                    for j in range(2):
                        c = 2 * i + j
                        if kind == "mod":
                            dst, bias = mod1[l][:, c, :], param("b_mod", 2)[:, l, c:c + 1]
                        else:
                            dst, bias = mod2[l][:, c:c + 1], param("ada_b", 2)[:, l, c:c + 1]
                        at_ = mod_col(at, b, j)
                        a = nc.scalar.activation(dst, bank(name)[:, at_:at_ + dst.shape[1]], ACT.Identity, bias=bias)
                if turned:
                    a.then_inc(*scalar.does("emptied " + name, *["col %s %d.%d" % todo[b] for b in turned]))

            def mod_rows(at):
                for n in range(len(mod_at[at]) + 1):
                    mod_row(at, n)

            def modulated(name, n, groups, gain, shift, at=None):
                more = len(mod_at[at]) + 1 if at else 0
                for k in range(KT):
                    if k < more:
                        mod_row(at, k)
                    act.wait_ge(*vector.did(f"normed {name}.{k}"))
                    for g in groups:
                        a = nc.scalar.activation(hT[:, k, S * g:S * g + S], dve_t[k % 4][:, S * g:S * g + S],
                                                 ACT.Identity, scale=gain(k, g), bias=shift(k, g))
                    a.then_inc(*scalar.does(f"h {name}.{k}"))

            act.wait_ge(params_landed, 16)
            act.wait_ge(tables_landed, 16)
            nc.scalar.activation(small[:, 32:56], param("c_vec"), ACT.Silu).then_inc(*scalar.does("csil"))
            at = PARAM_AT["decay"][0]
            both = params[:, at:at + 24]
            nc.scalar.activation(lp[0], both, ACT.Abs).then_inc(*scalar.does("lp abs"))
            act.wait_ge(*scalar.did("lp abs"))
            nc.scalar.activation(lp[1], lp[0], ACT.Exp, scale=-1.0).then_inc(*scalar.does("lp exp"))
            act.wait_ge(*vector.did("k_exps"))
            nc.scalar.activation(small[:, 80:112], small[:, 80:112], ACT.Exp).then_inc(*scalar.does("k_decay"))
            act.wait_ge(x_landed, 32)

            for l in range(2):
                nx = 2 * S if l == 0 else S
                groups = (0, 1) if l == 0 else (0,)
                square_all(f"n1 {l}", 2 * S, KT, lambda k: xT[:, k, :],
                           (lambda k: vector.did(f"x out 0.{k}")) if l else None)
                deviation(f"n1 {l}", 2 * S, D)
                if l == 0:
                    mod_rows("start")
                act.wait_ge(*vector.did(f"gain1 {l}"))
                modulated(f"n1 {l}", 2 * S, (0, 1), lambda k, g: gain1[l][:, k, g:g + 1],
                          lambda k, g: mod1[l][:, k, g:g + 1], "n1 1" if l else None)
                for n in range(BT):
                    if n >= 2:
                        act.wait_ge(*vector.did(f"cx {l}.{n - 2}"))
                    evacuate(f"sc_c {l}.{n}", act_t[n % 2][:, 0:nx], also=[f"sc_c {l}.{n}"])
                for n in range(BT):
                    if n >= 2:
                        act.wait_ge(*vector.did(f"u {l}.{n - 2}"))
                    evacuate(f"cf_g {l}.{n}", act_t[2 + n % 2][:, 0:nx], ACT.Sigmoid, [f"cf_g {l}.{n}"])
                for n in range(BT):
                    evacuate(f"ret_q {l}.{n}", ret_q[:, n, 0:nx], also=[f"ret_q {l}.{n}"])
                for n in range(BT):
                    evacuate(f"ret_k {l}.{n}", ret_k[:, n, :], also=[f"ret_k {l}.{n}"], scale=K_SCALE)
                for i in range(2):
                    for t in range(2 * ST):
                        evacuate(f"ret_v {l}.{i}.{t}", ret_v[:, t, 256 * i:256 * i + 256], also=[f"ret_v {l}.{i}.{t}"])
                for n in range(BT):
                    evacuate(f"att_q {l}.{n}", att_q[:, n, 0:nx], also=[f"att_q {l}.{n}"])
                evacuate(f"att_k {l}", att_k, also=[f"att_k {l}"])
                evacuate(f"att_v {l}", carve(17664, 2 * ST * P), also=[f"att_v {l}"])
                for n in range(BT):
                    if n >= 2:
                        act.wait_ge(*vector.did(f"branch {l}.sc.{n - 2}"))
                    evacuate(f"sc_z {l}.{n}", act_t[n % 2][:, 0:nx], ACT.Silu, [f"sc_z {l}.{n}"])

                for hd in range(HEADS):
                    evacuate(f"state {l}.{hd}", carve(18176 + 2 * P * hd, 2 * P), also=[f"state {l}.{hd}"])
                units = [(hd, g) for hd in range(HEADS) for g in groups]

                def ret_evacuate(hd, g):
                    evacuate(f"ro {l}.{hd}.{g}", ret_o[:, hd, S * g:S * g + S], also=[f"ret_o {l}.{hd}.{g}"])

                for n, (hd, g) in enumerate(units):
                    if g == 0:
                        if hd >= 2:
                            act.wait_ge(*vector.did(f"q_wt {l}.{hd - 2}"))
                        for d in range(2):
                            a = nc.scalar.activation(act_t[hd % 2][:, S * d:S * d + S],
                                                     table("q_pos")[:, S * d:S * d + S], ACT.Exp,
                                                     scale=log_g[:, l, d, hd:hd + 1])
                        a.then_inc(*scalar.does(f"q_dec {l}.{hd}"))
                        act.wait_ge(*vector.did(f"expo {l}.{hd}"))
                        nc.scalar.activation(act_t[2 + hd % 2][:], stat2[:], ACT.Exp)\
                            .then_inc(*scalar.does(f"decay {l}.{hd}"))
                    if n:
                        ret_evacuate(*units[n - 1])
                ret_evacuate(*units[-1])

                att = [(g, t, q) for g in groups for t in range(BT) for q in range(ST)]

                def att_turned(i):
                    nb = 4 - 2 * att[i][0]
                    for s in range(2):
                        if i >= 1:
                            act.wait_ge(*tensor.did(f"filled ao {l}.{i - 1}"))
                        evacuate(f"at {l}.{i}.{s}", act_t[2 + s][:, 0:P * nb], also=[f"att_t {l}.{i}.{s}"])

                for i in range(len(att) + 1):
                    if i < len(att):
                        g, t, q = att[i]
                        n = 2 * S - S * g
                        o = 2 * (i % 2)
                        act.wait_ge(*vector.did(f"att_m {l}.{i}"))
                        for s in range(2):
                            if i >= 1:
                                act.wait_ge(*vector.did(f"att_p {l}.{i - 1}.{s}"))
                            name = f"as {l}.{i}.{s}"
                            nc.scalar.activation(act_t[s][:, 0:n], bank(name)[:, 0:n], ACT.Exp, scale=ATT_SCALE,
                                                 bias=soft_m[:, o + s:o + s + 1], accum_out=soft_s[:, o + s:o + s + 1])\
                                .then_inc(*scalar.does(f"att_e {l}.{i}.{s}", "emptied " + name))
                        act.wait_ge(*vector.did(f"att_sk {l}.{i}"))
                        nc.scalar.activation(soft_e[:, o:o + 2], soft_d[:, o:o + 2], ACT.Exp)\
                            .then_inc(*scalar.does(f"att_se {l}.{i}"))
                    if i <= len(mod_at[f"att {l}"]):
                        mod_row(f"att {l}", i)
                    if i >= 1:
                        att_turned(i - 1)

                for hd in range(HEADS):
                    act.wait_ge(*vector.did(f"gd {l}.{hd}"))
                    if hd:
                        act.wait_ge(*tensor.did(f"summed gv {l}.{hd - 1}.0"))
                    square_all(f"gv {l}.{hd}", nx, 1, lambda k: ret_o[:, hd, 0:nx])
                    if hd:
                        act.wait_ge(*vector.did(f"rinv gv {l}.{hd - 1}"))
                    deviation(f"gv {l}.{hd}", nx, P)
                act.wait_ge(*tensor.did(f"summed gv {l}.{HEADS - 1}.0"))
                square_all(f"lv {l}", nx, BT, lambda k: f_br[:, k, 0:nx], lambda k: vector.did(f"ld {l}.{k}"))
                act.wait_ge(*vector.did(f"rinv gv {l}.{HEADS - 1}"))
                deviation(f"lv {l}", nx, BW)
                mod_rows(f"gv {l}")
                for n in range(BT):
                    act.wait_ge(*vector.did(f"ln {l}.{n}"))
                    nc.scalar.activation(f_br[:, n, 0:nx], f_br[:, n, 0:nx], ACT.Silu,
                                         scale=param("ln_w", 2)[:, l, n:n + 1], bias=param("ln_b", 2)[:, l, n:n + 1])\
                        .then_inc(*scalar.does(f"ln {l}.{n}"))
                act.wait_ge(*tensor.did(f"summed lv {l}.{BT - 1}"))
                zs = [(a, n) for a in ("ret", "att", "cf") for n in range(BT)]
                for i, (a, n) in enumerate(zs):
                    if i >= 4:
                        act.wait_ge(*vector.did("branch %d.%s.%d" % (l, *zs[i - 4])))
                    evacuate(f"{a}_z {l}.{n}", act_t[i % 4][:, 0:nx], ACT.Silu, [f"{a}_z {l}.{n}"])
                m = 0
                for b in MERGE_ORDER:
                    for n in range(KT):
                        if m >= 4:
                            act.wait_ge(*vector.did(f"gated {l}.{m - 4}"))
                        else:
                            act.wait_ge(*vector.did(f"branch {l}.cf.{BT - 1}"))
                        evacuate(f"gate {l}.{b}.{n}", act_t[m % 4][:, 0:nx], ACT.Sigmoid, [f"gate {l}.{m}"])
                        m += 1

            square_all("fin", S, KT, lambda k: xT[:, k, 0:S], lambda k: vector.did(f"x out 1.{k}"))
            deviation("fin", S, D)
            mod_rows("fin")

            def pre_norm(name, ready, l, q, at=None):
                square_all(name, S, KT, lambda k: xT[:, k, 0:S], ready)
                deviation(name, S, D)
                act.wait_ge(*vector.did(f"gain2 {l}"))
                modulated(name, S, (0,), lambda k, g: gain2[l][:, q, k:k + 1],
                          lambda k, g: mod2[l][:, 12 * q + k:12 * q + k + 1], at)

            def post(tag):
                for k in range(KT):
                    name = f"y {tag}.{k}"
                    act.wait_ge(*tensor.did("filled " + name))
                    nc.scalar.activation(yT[:, k, :], bank(name)[:, 0:S], ACT.Copy)
                    nc.scalar.activation(sq8[:, k, :], bank(name)[:, 0:S], ACT.Square)\
                        .then_inc(*scalar.does(name, "emptied " + name))
                deviation(f"ys {tag}", S, D)

            def ffn(l, ready):
                pre_norm(f"n3 {l}", ready, l, 2, None if l else "n3 0")
                fw, fb = param("ff_w", 2, FF_K), param("ff_b", 2)
                m = 0
                for i in range(11):
                    for nm in ("ffg", "ffv"):
                        for j in range(2):
                            n = 2 * i + j
                            c = n + (FT if nm == "ffv" else 0)
                            name = f"{nm} {l}.{n}"
                            if m >= 4:
                                act.wait_ge(*vector.did(f"ff_free {l}.{m - 4}"))
                            evacuate(name, act_t[m % 4][:, 0:S], ACT.Identity, [f"tap {name}"], last=False,
                                     scale=fw[:, l, FF_K - 1, c:c + 1], bias=fb[:, l, c:c + 1])
                            m += 1
                    for j in range(2):
                        n = 2 * i + j
                        act.wait_ge(*vector.did(f"conv ffg {l}.{n}"))
                        if n >= 4:
                            act.wait_ge(*vector.did(f"ff_act {l}.{n - 4}"))
                        nc.scalar.activation(act_t[n % 4][:, S:2 * S], dve_t[n % 4][:, 0:S], ACT.Gelu_apprx_tanh)\
                            .then_inc(*scalar.does(f"gelu {l}.{n}"))
                post(f"ffn {l}")

            pre_norm("n2 0", lambda k: vector.did(f"x fin.{k}"), 0, 0, "n2 0")
            for n in range(KT):
                evacuate(f"rgx {n}", xb_pad[:, n, RG_K - 1:], also=[f"xb {n}"])
            for n in range(KT):
                evacuate(f"rgg {n}", gel[:, n, :], ACT.Gelu_apprx_tanh, [f"gel {n}"])
            for n in range(KT):
                evacuate(f"rga {n}", rr[:, n, :], ACT.Sigmoid, [f"rr {n}"], bias=param("rg_ba")[:, n:n + 1])
            for n in range(KT):
                evacuate(f"rgx2 {n}", ix[:, n, :], ACT.Sigmoid, [f"ig {n}"], bias=param("rg_bx")[:, n:n + 1])
            for n in range(KT):
                nc.scalar.activation(tt_[:, n, :], rr[:, n, :], ACT.Tanh, scale=lam8[:, n:n + 1])
                nc.scalar.activation(rr[:, n, :], rr[:, n, :], ACT.Exp, scale=lam8n[:, n:n + 1])\
                    .then_inc(*scalar.does(f"a {n}"))
            mod_rows("rg")
            for n in range(KT):
                act.wait_ge(*vector.did(f"one_a2 {n}"))
                nc.scalar.activation(tt_[:, n, :], tt_[:, n, :], ACT.Sqrt).then_inc(*scalar.does(f"mult {n}"))
            post("rg")
            mod_rows("post rg")
            ffn(0, lambda k: vector.did(f"x rg.{k}"))

            pre_norm("n2 1", lambda k: vector.did(f"x ffn 0.{k}"), 1, 0)
            evacuate("gla z", zT[0:16, :], also=["zT"])
            for hd in range(GLA_H):
                evacuate(f"alpha {hd}", le[:, hd, :], ACT.Abs, [f"le {hd}"], last=False,
                         bias=param("gla_b")[:, hd:hd + 1])
            for hd in range(GLA_H):
                act.wait_ge(*scalar.did(f"le {hd}"))
                nc.scalar.activation(le[:, hd, :], le[:, hd, :], ACT.Exp, scale=-1.0)\
                    .then_inc(*scalar.does(f"le2 {hd}"))
            for hd in range(GLA_H):
                act.wait_ge(*scalar.did(f"le2 {hd}"))
                nc.scalar.activation(le[:, hd, :], le[:, hd, :], ACT.Ln, bias=ones[:, 0:1])\
                    .then_inc(*scalar.does(f"le3 {hd}"))
            for n in range(GLA_H):
                evacuate(f"glaq {n}", gq[:, n, :], also=[f"gq {n}"], scale=GLA_DK ** -0.5)
            for n in range(GLA_H):
                evacuate(f"glak {n}", gk[:, n, :], also=[f"gk {n}"])
            vs = [(i, t) for i in range(4) for t in range(ST)]
            for i in range(8):
                if i < 8:
                    a_, b_ = vs[i]
                    evacuate(f"glav {a_}.{b_}", gv[:, b_, 256 * a_:256 * a_ + 256], also=[f"gv {a_}.{b_}"])
                j = (7 + i) % 8
                act.wait_ge(*vector.did(f"ldiff {j}"))
                nc.scalar.activation(lv[:, j, :], lv[:, j, :], ACT.Exp, scale=1.0 / 16.0)\
                    .then_inc(*scalar.does(f"lexp {j}"))
            for n in range(GLA_H * ST):
                if n % 2:
                    evacuate(f"cross {n // 2}", attT[:, n // 2, 0, P:S], also=[f"cross {n // 2}"])
                evacuate(f"glar {n}", r_sil[:, n, :], ACT.Silu, [f"r_sil {n}"])
            for n in range(KT):
                name = f"go {n}"
                act.wait_ge(*tensor.did("filled " + name))
                nc.scalar.activation(gla_o[:, n, :], bank(name)[:, 0:S], ACT.Copy)
                nc.scalar.activation(sq8[:, n, :], bank(name)[:, 0:S], ACT.Square)\
                    .then_inc(*scalar.does(name, "emptied " + name))
            for hd in range(GLA_H):
                if hd:
                    act.wait_ge(*vector.did(f"rinv gs {hd - 1}"))
                deviation(f"gs {hd}", S, 2 * P)
            post("gla")
            ffn(1, lambda k: vector.did(f"x gla.{k}"))

        @block.vector
        def _(dve):
            def step(ins, *names):
                ins.then_inc(*vector.does(*names))

            def after(name):
                dve.wait_ge(*vector.did(name))

            def filled(name):
                dve.wait_ge(*tensor.did("filled " + name))

            def settled():
                dve.wait_ge(vector.sem, vector.n)

            def inverse(name, n):
                settled()
                dve.wait_ge(*scalar.did(f"dev {name}"))
                step(nc.vector.reciprocal(stat2[:, 0:n], stat[:, 0:n]), f"rinv {name}")
                after(f"rinv {name}")

            def normed(name, n):
                inverse(name, n)
                for k in range(KT):
                    if k >= 4:
                        dve.wait_ge(*scalar.did(f"h {name}.{k - 4}"))
                    step(nc.vector.tensor_tensor(dve_t[k % 4][:, 0:n], xT[:, k, 0:n], stat2[:, 0:n], ALU.mult),
                         f"normed {name}.{k}")

            def bcast(ap, n):
                return ap.unsqueeze(2).broadcast_to([ap.shape[0], ap.shape[1], n])

            dve.wait_ge(params_landed, 16)
            dve.wait_ge(tables_landed, 16)
            step(nc.vector.memset(cx[:, :, :, 0:1], 0.0), "cx z0")
            step(nc.vector.memset(cx[:, :, :, S + 1:S + 2], 0.0), "cx z1")
            step(nc.vector.memset(u_pad[:, :, :, 0:PAD], 0.0), "u z0")
            step(nc.vector.memset(u_pad[:, :, :, PAD + S:], 0.0), "u z1")
            at = PARAM_AT["decay"][0]
            both = params[:, at:at + 24]
            dve.wait_ge(*scalar.did("lp exp"))
            step(nc.vector.tensor_scalar(lp[0], lp[1], 2.0, None, ALU.add), "lp0")
            after("lp0")
            step(nc.vector.reciprocal(lp[2], lp[0]), "lp1")
            after("lp1")
            step(nc.vector.tensor_tensor(lp[1], lp[1], lp[2], ALU.mult), "lp2")
            after("lp2")
            step(nc.vector.tensor_tensor(lp[2], lp[1], lp[1], ALU.mult), "lp3")
            after("lp3")
            step(nc.vector.tensor_scalar(lp[3], lp[2], 1.0 / 15, 1.0 / 13, ALU.mult, ALU.add), "lp4")
            for i, d in enumerate((11, 9, 7, 5, 3, 1)):
                after(f"lp{4 + 2 * i}")
                step(nc.vector.tensor_tensor(lp[3], lp[3], lp[2], ALU.mult), f"lp{5 + 2 * i}")
                after(f"lp{5 + 2 * i}")
                step(nc.vector.tensor_scalar(lp[3], lp[3], 1.0 / d, None, ALU.add), f"lp{6 + 2 * i}")
            after("lp16")
            step(nc.vector.scalar_tensor_tensor(lp[3], lp[1], 2.0, lp[3], ALU.mult, ALU.mult), "lp17")
            step(nc.vector.tensor_scalar(lp[0], both, -1.0, 0.0, ALU.mult, ALU.max), "lp18")
            after("lp18")
            step(nc.vector.tensor_tensor(soft_p, lp[0], lp[3], ALU.add), "soft_p")
            after("soft_p")
            step(nc.vector.tensor_scalar(small[:, 224:240], soft_p[:, 0:16], -1.0, None, ALU.mult), "log_g")
            step(nc.vector.tensor_scalar(lam8, soft_p[:, 16:24], 8.0, None, ALU.mult), "lam8")
            step(nc.vector.tensor_scalar(lam8n, soft_p[:, 16:24], -8.0, None, ALU.mult), "lam8n")
            step(nc.vector.tensor_scalar(small[:, 112:128], param("sink"), -1.0, None, ALU.mult), "nsink")
            after("log_g")
            for l in range(2):
                for d in range(2):
                    for t in range(ST):
                        ins = nc.vector.tensor_scalar(k_decay[:, l, d, t, :], log_g[:, l, d, :],
                                                      table("k_pos")[:, 2 * d + t:2 * d + t + 1], None, ALU.mult)
                        step(ins, *(["k_exps"] if (l, d, t) == (1, 1, 1) else []))

            def modulation1(l):
                dve.wait_ge(*scalar.did(f"col mod {l}.11"))
                step(nc.vector.scalar_tensor_tensor(gain1[l], mod1[l][:, 8:16, :], 1.0,
                                                    bcast(param("norm_w", 2)[:, l, :], 2), ALU.add, ALU.mult),
                     f"gain1 {l}")

            def modulation2(l):
                dve.wait_ge(*scalar.did(f"col ada {l}.23"))
                g = param("norm_g", 2, 4)
                for q in range(2):
                    c = 24 * q
                    step(nc.vector.scalar_tensor_tensor(gain2[l][:, 2 * q, :], mod2[l][:, c + 8:c + 16], 1.0,
                                                        g[:, l, 2 * q, :], ALU.add, ALU.mult))
                    step(nc.vector.tensor_tensor(gain2[l][:, 2 * q + 1, :], mod2[l][:, c + 16:c + 24],
                                                 g[:, l, 2 * q + 1, :], ALU.mult), *([f"gain2 {l}"] if q else []))

            dve.wait_ge(x_landed, 32)
            for l in range(2):
                nx = 2 * S if l == 0 else S
                groups = (0, 1) if l == 0 else (0,)
                ng = len(groups)
                settled()
                modulation1(l)
                if l:
                    step(nc.vector.memset(cx[:, :, 0:1, 0:1], 0.0), "cx z2")
                    step(nc.vector.memset(cx[:, :, 0:1, S + 1:S + 2], 0.0), "cx z3")
                    step(nc.vector.memset(u_pad[:, :, 0:1, 0:PAD], 0.0), "u z2")
                    step(nc.vector.memset(u_pad[:, :, 0:1, PAD + S:], 0.0), "u z3")
                normed(f"n1 {l}", 2 * S)

                def grouped(ap):
                    return ap.rearrange("p (g s) -> p g s", g=ng)

                settled()
                for n in range(BT):
                    dve.wait_ge(*scalar.did(f"sc_c {l}.{n}"))
                    name = f"sc_x {l}.{n}"
                    filled(name)
                    step(nc.vector.tensor_tensor(cx[:, n, 0:ng, 1:S + 1], grouped(bank(name)[:, 0:nx]),
                                                 grouped(act_t[n % 2][:, 0:nx]), ALU.mult),
                         f"cx {l}.{n}", "emptied " + name)
                sw = param("sc_w", 2, SC_K)
                for k in range(SC_K):
                    for n in range(BT):
                        src, dst = cx[:, n, 0:ng, k:k + S], grouped(s_br[:, n, 0:nx])
                        if k == 0:
                            after(f"cx {l}.{n}")
                            step(nc.vector.tensor_scalar(dst, src, sw[:, l, k, n:n + 1], None, ALU.mult),
                                 f"sc {l}.{n}.{k}")
                        else:
                            after(f"sc {l}.{n}.{k - 1}")
                            step(nc.vector.scalar_tensor_tensor(dst, src, sw[:, l, k, n:n + 1], dst, ALU.mult, ALU.add),
                                 f"sc {l}.{n}.{k}")
                settled()
                for n in range(BT):
                    dve.wait_ge(*scalar.did(f"cf_g {l}.{n}"))
                    name = f"cf_a {l}.{n}"
                    filled(name)
                    step(nc.vector.tensor_tensor(u_pad[:, n, 0:ng, PAD:PAD + S], grouped(bank(name)[:, 0:nx]),
                                                 grouped(act_t[2 + n % 2][:, 0:nx]), ALU.mult),
                         f"u {l}.{n}", "emptied " + name)
                cw, cb = param("cf_w", 2, CF_K), param("cf_b", 2)
                for k in range(CF_K):
                    for n in range(BT):
                        src, dst = u_pad[:, n, 0:ng, k:k + S], grouped(f_br[:, n, 0:nx])
                        name = f"cf {l}.{n}.{k}" if k < CF_K - 1 else f"conv {l}.{n}"
                        if k == 0:
                            after(f"u {l}.{n}")
                            step(nc.vector.tensor_scalar(dst, src, cw[:, l, k, n:n + 1], cb[:, l, n:n + 1],
                                                         ALU.mult, ALU.add), name)
                        else:
                            after(f"cf {l}.{n}.{k - 1}")
                            step(nc.vector.scalar_tensor_tensor(dst, src, cw[:, l, k, n:n + 1], dst, ALU.mult, ALU.add),
                                 name)
                settled()
                for n in range(BT):
                    name = f"sc_b {l}.{n}"
                    filled(name)
                    step(nc.vector.tensor_tensor(s_br[:, n, 0:nx], bank(name)[:, 0:nx], s_br[:, n, 0:nx], ALU.mult),
                         f"sb {l}.{n}", "emptied " + name)
                    dve.wait_ge(*scalar.did(f"sc_z {l}.{n}"))
                    after(f"sb {l}.{n}")
                    step(nc.vector.tensor_tensor(s_br[:, n, 0:nx], s_br[:, n, 0:nx], act_t[n % 2][:, 0:nx], ALU.mult),
                         f"branch {l}.sc.{n}")
                settled()
                for t in range(BT + 1):
                    q = att_q[:, t, 0:S] if t < BT else att_k[:, 0:S]
                    name = f"turn {l}.{t}"
                    filled(name)
                    if t >= 2:
                        after(f"roped {l}.{t - 2}")
                    step(nc.vector.tensor_tensor(dve_t[t % 2][:, 0:S], bank(name)[:, 0:S], table("sin"), ALU.mult),
                         f"rope0 {l}.{t}", "emptied " + name)
                    step(nc.vector.tensor_tensor(q, q, table("cos"), ALU.mult), f"rope1 {l}.{t}")
                    after(f"rope1 {l}.{t}")
                    step(nc.vector.tensor_tensor(q, q, dve_t[t % 2][:, 0:S], ALU.add),
                         f"roped {l}.{t}", *([f"att_q roped {l}.{t}"] if t < BT else []))
                after(f"roped {l}.{BT}")
                step(nc.vector.tensor_copy(att_ks[0:64, :], att_k[64:P, :]))
                step(nc.vector.tensor_copy(att_ks[64:P, :], att_k[0:64, :]), f"att_ks {l}")

                settled()
                dve.wait_ge(*scalar.did("k_decay"))
                for t in range(ST):
                    name = f"kT {l}.{t}"
                    filled(name)
                    for d in range(2):
                        step(nc.vector.tensor_tensor(k_wt[d][:, t, :, :], bank(name)[:].rearrange("p (h n) -> p h n", h=HEADS),
                                                     bcast(k_decay[:, l, d, t, :], P), ALU.mult),
                             f"k_wt {l}.{t}.{d}", *(["emptied " + name] if d else []))
                units = [(hd, g) for hd in range(HEADS) for g in groups]
                for n, (hd, g) in enumerate(units):
                    if g == 0:
                        if hd:
                            dve.wait_ge(*scalar.did(f"decay {l}.{hd - 1}"))
                        step(nc.vector.tensor_scalar(stat2[:], table("ahead"), log_g[:, l, 1, hd:hd + 1], None, ALU.mult),
                             f"expo0 {l}.{hd}")
                        after(f"expo0 {l}.{hd}")
                        step(nc.vector.scalar_tensor_tensor(stat2[:], table("behind"), log_g[:, l, 0, hd:hd + 1], stat2[:],
                                                            ALU.mult, ALU.add), f"expo {l}.{hd}")
                        dve.wait_ge(*scalar.did(f"q_dec {l}.{hd}"))
                        if hd >= 2:
                            dve.wait_ge(*tensor.did(f"filled ro {l}.{hd - 2}.0"))
                        dve.wait_ge(*scalar.did(f"ret_q {l}.{hd}"))
                        for d in range(2):
                            ins = nc.vector.tensor_tensor(dve_t[hd % 2][:, S * d:S * d + S], ret_q[:, hd, 0:S],
                                                          act_t[hd % 2][:, S * d:S * d + S], ALU.mult)
                            step(ins, *([f"q_wt {l}.{hd}"] if d else []))
                        dve.wait_ge(*scalar.did(f"decay {l}.{hd}"))
                    name = f"rs {l}.{hd}.{g}"
                    filled(name)
                    if n >= 2:
                        dve.wait_ge(*tensor.did("filled ro %d.%d.%d" % (l, *units[n - 2])))
                    step(nc.vector.tensor_tensor(dve_t[2 + n % 2][:], bank(name)[:], act_t[2 + hd % 2][:], ALU.mult),
                         f"ret_p {l}.{hd}.{g}", "emptied " + name)

                settled()
                att = [(g, t, q) for g in groups for t in range(BT) for q in range(ST)]

                def att_max(i):
                    g, t, q = att[i]
                    o = 2 * (i % 2)
                    for s in range(2):
                        name = f"as {l}.{i}.{s}"
                        filled(name)
                        if g == 0:
                            c = P * (1 - q)
                            step(nc.vector.tensor_tensor(bank(name)[:, c:c + P], bank(name)[:, c:c + P],
                                                         table("band")[:, P * q:P * q + P], ALU.add), f"band {l}.{i}.{s}")
                    for s in range(2):
                        if g == 0:
                            after(f"band {l}.{i}.{s}")
                        step(nc.vector.tensor_reduce(soft_m[:, 4 + s:5 + s], bank(f"as {l}.{i}.{s}")[:, 0:2 * S - S * g],
                                                     AX_X, ALU.max), f"rowmax {l}.{i}.{s}")
                    after(f"rowmax {l}.{i}.1")
                    if i >= 2:
                        dve.wait_ge(*scalar.did(f"att_se {l}.{i - 2}"))
                    step(nc.vector.scalar_tensor_tensor(soft_m[:, o:o + 2], soft_m[:, 4:6], -ATT_SCALE,
                                                        nsink[:, l, 2 * t:2 * t + 2], ALU.mult, ALU.min), f"att_m {l}.{i}")
                    after(f"att_m {l}.{i}")
                    step(nc.vector.tensor_tensor(soft_d[:, o:o + 2], soft_m[:, o:o + 2],
                                                 param("sink", 2)[:, l, 2 * t:2 * t + 2], ALU.add), f"att_sk {l}.{i}")

                def att_weights(i):
                    g, t, q = att[i]
                    o = 2 * (i % 2)
                    n = 2 * S - S * g
                    dve.wait_ge(*scalar.did(f"att_se {l}.{i}"))
                    step(nc.vector.tensor_tensor(soft_s[:, 4:6], soft_s[:, o:o + 2], soft_e[:, o:o + 2], ALU.add),
                         f"att_d0 {l}.{i}")
                    after(f"att_d0 {l}.{i}")
                    if i:
                        after(f"att_p {l}.{i - 1}.1")
                    step(nc.vector.reciprocal(soft_e[:, 4:6], soft_s[:, 4:6]), f"att_d1 {l}.{i}")
                    after(f"att_d1 {l}.{i}")
                    for s in range(2):
                        if i >= 2:
                            dve.wait_ge(*tensor.did(f"filled at {l}.{i - 2}.{s}"))
                        step(nc.vector.tensor_scalar(dve_t[2 * (i % 2) + s][:, 0:n], act_t[s][:, 0:n],
                                                     soft_e[:, 4 + s:5 + s], None, ALU.mult), f"att_p {l}.{i}.{s}")

                def att_store(i):
                    g, t, q = att[i]
                    name = f"ao {l}.{i}"
                    filled(name)
                    step(nc.vector.tensor_copy(att_o[:, t, S * g + P * q:S * g + P * q + P], bank(name)[:, 0:P]),
                         f"att_o {l}.{i}", "emptied " + name)

                dve.wait_ge(*tensor.did("filled ro %d.%d.%d" % (l, *units[-1])))
                for i in range(len(att) + 2):
                    if i < len(att):
                        att_max(i)
                        att_weights(i)
                    if i >= 2:
                        att_store(i - 2)

                settled()
                for hd in range(HEADS):
                    name = f"gm {l}.{hd}"
                    filled(name)
                    step(nc.vector.scalar_tensor_tensor(ret_o[:, hd, 0:nx], bank(name)[:, 0:nx], -1.0 / P,
                                                        ret_o[:, hd, 0:nx], ALU.mult, ALU.add),
                         f"gd {l}.{hd}", "emptied " + name)
                name = f"lm {l}"
                filled(name)
                for t in range(BT):
                    step(nc.vector.scalar_tensor_tensor(f_br[:, t, 0:nx], bank(name)[:, 0:nx], -1.0 / BW,
                                                        f_br[:, t, 0:nx], ALU.mult, ALU.add),
                         f"ld {l}.{t}", *(["emptied " + name] if t == BT - 1 else []))
                for hd in range(HEADS):
                    inverse(f"gv {l}.{hd}", nx)
                    step(nc.vector.scalar_tensor_tensor(ret_o[:, hd, 0:nx], ret_o[:, hd, 0:nx],
                                                        param("gn_w", 2)[:, l, hd:hd + 1], stat2[:, 0:nx],
                                                        ALU.mult, ALU.mult), f"gn {l}.{hd}")
                inverse(f"lv {l}", nx)
                for t in range(BT):
                    step(nc.vector.tensor_tensor(f_br[:, t, 0:nx], f_br[:, t, 0:nx], stat2[:, 0:nx], ALU.mult),
                         f"ln {l}.{t}")
                zs = [(a, n) for a in ("ret", "att", "cf") for n in range(BT)]
                for i, (a, n) in enumerate(zs):
                    dve.wait_ge(*scalar.did(f"{a}_z {l}.{n}"))
                    if a == "cf":
                        dve.wait_ge(*scalar.did(f"ln {l}.{n}"))
                    elif a == "ret":
                        after(f"gn {l}.{n}")
                    else:
                        after(f"att_o {l}.{len(att) - 1}")
                    step(nc.vector.tensor_tensor(branch[a][:, n, 0:nx], branch[a][:, n, 0:nx], act_t[i % 4][:, 0:nx],
                                                 ALU.mult), f"branch {l}.{a}.{n}")
                settled()
                m = 0
                for b in MERGE_ORDER:
                    for n in range(KT):
                        dve.wait_ge(*scalar.did(f"gate {l}.{m}"))
                        name = f"br {l}.{b}.{n}"
                        filled(name)
                        if b == MERGE_ORDER[0]:
                            step(nc.vector.tensor_tensor(merged[:, n, 0:nx], bank(name)[:, 0:nx], act_t[m % 4][:, 0:nx],
                                                         ALU.mult), f"gated {l}.{m}", f"merged {l}.{b}.{n}", "emptied " + name)
                        else:
                            if m >= KT + 4:
                                after(f"added {l}.{m - 4}")
                            step(nc.vector.tensor_tensor(dve_t[m % 4][:, 0:nx], bank(name)[:, 0:nx], act_t[m % 4][:, 0:nx],
                                                         ALU.mult), f"gated {l}.{m}", "emptied " + name)
                            after(f"gated {l}.{m}")
                            after(f"merged {l}.{MERGE_ORDER[MERGE_ORDER.index(b) - 1]}.{n}")
                            step(nc.vector.tensor_tensor(merged[:, n, 0:nx], merged[:, n, 0:nx], dve_t[m % 4][:, 0:nx],
                                                         ALU.add), f"merged {l}.{b}.{n}", f"added {l}.{m}")
                        m += 1
                for n in range(KT):
                    name = f"out {l}.{n}"
                    filled(name)
                    for g in groups:
                        sl = slice(S * g, S * g + S)
                        step(nc.vector.scalar_tensor_tensor(xT[:, n, sl], bank(name)[:, sl], mod1[l][:, 16 + n, g:g + 1],
                                                            xT[:, n, sl], ALU.mult, ALU.add),
                             *([f"x out {l}.{n}", "emptied " + name] if g == groups[-1] else []))

            inverse("fin", S)
            for k in range(KT):
                step(nc.vector.scalar_tensor_tensor(xT[:, k, 0:S], xT[:, k, 0:S], param("fin_w")[:, k:k + 1],
                                                    stat2[:, 0:S], ALU.mult, ALU.mult), f"x fin.{k}")

            def post(tag, l, q):
                inverse(f"ys {tag}", S)
                for k in range(KT):
                    step(nc.vector.scalar_tensor_tensor(yT[:, k, :], yT[:, k, :], gain2[l][:, q, k:k + 1], stat2[:, 0:S],
                                                        ALU.mult, ALU.mult), f"yn {tag}.{k}")
                for k in range(KT):
                    after(f"yn {tag}.{k}")
                    step(nc.vector.tensor_tensor(xT[:, k, 0:S], xT[:, k, 0:S], yT[:, k, :], ALU.add), f"x {tag}.{k}")

            def ffn(l):
                normed(f"n3 {l}", S)
                dve.wait_ge(*scalar.did(f"h n3 {l}.{KT - 1}"))
                fw = param("ff_w", 2, FF_K)
                m = 0
                for i in range(11):
                    for nm in ("ffg", "ffv"):
                        for j in range(2):
                            n = 2 * i + j
                            c = n + (FT if nm == "ffv" else 0)
                            name = f"{nm} {l}.{n}"
                            dve.wait_ge(*scalar.did(f"tap {name}"))
                            src, acc = bank(name), act_t[m % 4]
                            dst = dve_t[n % 4][:, 0:S] if nm == "ffg" else dve_t[n % 4][:, S:2 * S]
                            step(nc.vector.scalar_tensor_tensor(acc[:, 1:S], src[:, 0:S - 1], fw[:, l, 1, c:c + 1],
                                                                acc[:, 1:S], ALU.mult, ALU.add), f"tap1 {name}")
                            after(f"tap1 {name}")
                            if n >= 4 and nm == "ffv":
                                after(f"ff_act {l}.{n - 4}")
                            step(nc.vector.tensor_copy(dst[:, 0:2], acc[:, 0:2]))
                            step(nc.vector.scalar_tensor_tensor(dst[:, 2:S], src[:, 0:S - 2], fw[:, l, 0, c:c + 1],
                                                                acc[:, 2:S], ALU.mult, ALU.add),
                                 f"conv {name}", f"ff_free {l}.{m}", "emptied " + name)
                            m += 1
                    for j in range(2):
                        n = 2 * i + j
                        dve.wait_ge(*scalar.did(f"gelu {l}.{n}"))
                        after(f"conv ffv {l}.{n}")
                        step(nc.vector.tensor_tensor(ff_act[:, n, :], act_t[n % 4][:, S:2 * S], dve_t[n % 4][:, S:2 * S],
                                                     ALU.mult), f"ff_act {l}.{n}")
                post(f"ffn {l}", l, 3)

            settled()
            modulation2(0)
            normed("n2 0", S)
            step(nc.vector.memset(xb_pad[:, :, 0:RG_K - 1], 0.0), "xb z")
            after("xb z")
            rw, rb = param("rg_w", RG_K), param("rg_b")
            for k in range(RG_K):
                for n in range(KT):
                    src = xb_pad[:, n, k:k + S]
                    if k == 0:
                        dve.wait_ge(*scalar.did(f"xb {n}"))
                        step(nc.vector.tensor_scalar(xc[:, n, :], src, rw[:, k, n:n + 1], rb[:, n:n + 1],
                                                     ALU.mult, ALU.add), f"xc0 {n}")
                    else:
                        after(f"xc{k - 1} {n}")
                        step(nc.vector.scalar_tensor_tensor(xc[:, n, :], src, rw[:, k, n:n + 1], xc[:, n, :],
                                                            ALU.mult, ALU.add),
                             f"xc{k} {n}", *([f"xc {n}"] if k == RG_K - 1 else []))
            for n in range(KT):
                dve.wait_ge(*scalar.did(f"ig {n}"))
                step(nc.vector.tensor_tensor(ix[:, n, :], ix[:, n, :], xc[:, n, :], ALU.mult), f"ix {n}")
            for n in range(KT):
                dve.wait_ge(*scalar.did(f"a {n}"))
                step(nc.vector.tensor_tensor(a2[:, n, :], rr[:, n, :], rr[:, n, :], ALU.mult), f"a2 {n}")
            for n in range(KT):
                after(f"a2 {n}")
                step(nc.vector.scalar_tensor_tensor(tt_[:, n, :], a2[:, n, :], 1.0, tt_[:, n, :], ALU.add, ALU.mult),
                     f"one_a2 {n}")
            for n in range(KT):
                dve.wait_ge(*scalar.did(f"mult {n}"))
                after(f"ix {n}")
                step(nc.vector.tensor_tensor(ix[:, n, :], ix[:, n, :], tt_[:, n, :], ALU.mult), f"u_rg {n}")
            for n in range(KT):
                after(f"u_rg {n}")
                step(nc.vector.tensor_tensor_scan(a2[:, n, :], rr[:, n, :], ix[:, n, :], 0.0, ALU.mult, ALU.add), f"hs {n}")
            dve.wait_ge(*tensor.did(f"filled rgx2 {KT - 1}"))
            for n in range(KT):
                after(f"hs {n}")
                dve.wait_ge(*scalar.did(f"gel {n}"))
                step(nc.vector.tensor_tensor(xc[:, n, :], a2[:, n, :], gel[:, n, :], ALU.mult), f"rg_y {n}")
            post("rg", 0, 1)
            ffn(0)
            modulation2(1)

            settled()
            normed("n2 1", S)
            for hd in range(GLA_H):
                name = f"alpha {hd}"
                dve.wait_ge(*scalar.did(f"le {hd}"))
                step(nc.vector.tensor_scalar(la[:, hd, :], bank(name)[:, 0:S], param("gla_b")[:, hd:hd + 1], 0.0,
                                             ALU.add, ALU.min), f"la {hd}", "emptied " + name)
            for hd in range(GLA_H):
                dve.wait_ge(*scalar.did(f"le3 {hd}"))
                after(f"la {hd}")
                step(nc.vector.tensor_tensor(la[:, hd, :], la[:, hd, :], le[:, hd, :], ALU.subtract), f"lb {hd}")
            for hd in range(GLA_H):
                after(f"lb {hd}")
                step(nc.vector.tensor_tensor_scan(gg[:, hd, :], ones, la[:, hd, :], 0.0, ALU.mult, ALU.add), f"gg {hd}")
            after(f"gg {GLA_H - 1}")
            flat = carve(8192 + 4 * 1024, GLA_H * S)
            half_of = (1, 2, 4, 8, 16, 32, 64, 128)
            level_order = [(7 + i) % 8 for i in range(8)]

            def halves(ap, s):
                return ap.rearrange("p (b two s) -> p b two s", two=2, s=s)

            for i in level_order:
                s = half_of[i]
                g, d = halves(flat, s), halves(lv[:, i, :], s)
                nb = g.shape[1]
                ref = g[:, :, 0, s - 1:s].broadcast_to([P, nb, s])
                step(nc.vector.tensor_tensor(d[:, :, 1, :], g[:, :, 1, :], ref, ALU.subtract))
                step(nc.vector.tensor_tensor(d[:, :, 0, :], ref, g[:, :, 0, :], ALU.subtract), f"ldiff {i}")
            qf, kf = carve(8192, GLA_H * S), carve(8192 + 1024, GLA_H * S)
            dve.wait_ge(*scalar.did(f"gk {GLA_H - 1}"))
            for i in level_order:
                s = half_of[i]
                d = halves(lv[:, i, :], s)
                dve.wait_ge(*scalar.did(f"lexp {i}"))
                step(nc.vector.tensor_tensor(d[:, :, 1, :], d[:, :, 1, :], halves(qf, s)[:, :, 1, :], ALU.mult))
                step(nc.vector.tensor_tensor(d[:, :, 0, :], d[:, :, 0, :], halves(kf, s)[:, :, 0, :], ALU.mult), f"lv {i}")
            lpf = carve(13312, 8 * P)
            dve.wait_ge(late_landed, 32)
            for n in range(GLA_H * ST):
                hd, t = n // ST, n % ST
                for half in range(2):
                    name = f"lev {n}.{half}"
                    filled(name)
                    if n:
                        after(f"attT {n - 1}")
                    step(nc.vector.tensor_tensor(lpf[:, 512 * half:512 * half + 512], bank(name)[:],
                                                 level[:, 512 * half:512 * half + 512], ALU.mult),
                         f"lpr {n}.{half}", "emptied " + name)
                after(f"lpr {n}.1")
                step(nc.vector.tensor_reduce(attT[:, hd, t, P * t:P * t + P], lprod.rearrange("p l i -> p i l"),
                                             AX_X, ALU.add), f"attT {n}")
            for hd in range(GLA_H):
                inverse(f"gs {hd}", S)
                for e in range(2):
                    n = 2 * hd + e
                    step(nc.vector.scalar_tensor_tensor(gla_o[:, n, :], gla_o[:, n, :], param("gla_g")[:, e:e + 1],
                                                        stat2[:, 0:S], ALU.mult, ALU.mult), f"gon {n}")
                for e in range(2):
                    n = 2 * hd + e
                    dve.wait_ge(*scalar.did(f"r_sil {n}"))
                    after(f"gon {n}")
                    step(nc.vector.tensor_tensor(gla_o[:, n, :], gla_o[:, n, :], r_sil[:, n, :], ALU.mult), f"gla_y {n}")
            post("gla", 1, 1)
            ffn(1)

    return dict(tensor=tensor.now, vector=vector.now, scalar=scalar.now)


WEIGHTS = ("w_mod", "w_in", "w_branch", "w_out", "ada_w_2", "ffn_w_up_2", "ffn_w_down_2", "rg_w_in_2", "rg_wa_2",
           "rg_wx_2", "rg_w_out_2", "gla_w_in_2", "gla_w_out_2", "gla_w_alpha_2")


def shape_tables():
    p, i = np.arange(P), np.arange(S)
    out = {"ident": np.eye(P), "ones": np.ones((P, S)), "eps": np.full((P, 1), EPS)}
    turn = np.zeros((P, P))
    half = ATT_DH // 2
    for m in range(P):
        r = m % ATT_DH
        turn[m + half if r < half else m - half, m] = -1.0 if r < half else 1.0
    out["turn"] = turn
    freqs = ATT_DH // 4
    inv = (np.float32(10000.0) ** (-np.arange(freqs, dtype=np.float32) / np.float32(freqs))).astype(np.float32)
    row, col = (i // 64).astype(np.float32), (i % 64).astype(np.float32)
    angle = np.concatenate([inv[:, None] * row[None], inv[:, None] * col[None]], 0).astype(np.float32)
    angle = np.tile(angle, (P // half, 1))
    out["cos"], out["sin"] = np.cos(angle), np.sin(angle)
    j = p[:, None, None] + P * np.arange(ST)[None, :, None]
    dist = i[None, None, :] - j
    out["behind"] = np.maximum(dist, 0).reshape(P, -1)
    out["ahead"] = np.maximum(-dist, 0).reshape(P, -1)
    out["q_pos"] = np.tile(np.concatenate([i + 1, S - i])[None], (P, 1))
    pos = p[:, None] + P * np.arange(ST)[None]
    out["k_pos"] = np.concatenate([S - 1 - pos, pos], 1)
    q, k = p[:, None], p[None, :]
    out["band"] = np.concatenate([np.where(k <= q, 0.0, -1e30), np.where(k >= q, 0.0, -1e30)], 1)
    masks = []
    for s in LEVELS:
        a, b = p[:, None], p[None, :]
        masks.append((a // (2 * s) == b // (2 * s)) & (a % (2 * s) < s) & (b % (2 * s) >= s))
    masks.append(np.eye(P, dtype=bool))
    level = np.concatenate([m.astype(np.float32) for m in masks], 1)
    return np.concatenate([out[n].reshape(P, -1).astype(np.float32) for n in TABLES], 1), level


def pack_params(a):
    def cols(v):
        v = np.asarray(v)
        v = v.reshape(v.shape[:-1] + (v.shape[-1] // P, P))
        return np.moveaxis(v, -1, 0).reshape(P, -1)

    def rows(v):
        return np.broadcast_to(np.asarray(v).reshape(1, -1), (P, np.asarray(v).size))

    c_vec = np.stack([cols(a["c"][0]), cols(a["c_ctx"]), cols(a["c_2"][0])], 2).reshape(P, -1)
    wz = np.asarray(a["gla_w_in_2"])[0][:, 3072:3088].reshape(KT, P, 16).transpose(1, 0, 2).reshape(P, -1)
    parts = dict(norm_w=cols(a["norm_w"]), gn_w=cols(a["ret_gn_w"]), sc_w=cols(a["sc_conv_w"]), cf_w=cols(a["cf_conv_w"]),
                 cf_b=cols(a["cf_conv_b"]), ln_w=cols(a["cf_ln_w"]), ln_b=cols(a["cf_ln_b"]), sink=rows(a["att_sink"]),
                 b_mod=cols(a["b_mod"]), fin_w=cols(a["final_norm_w"]), decay=rows(a["ret_decay"]),
                 lam=cols(a["rg_lambda_2"]), c_vec=c_vec, ada_b=cols(a["ada_b_2"]), norm_g=cols(a["norm_g_2"]),
                 ff_w=cols(a["ffn_conv_w_2"]), ff_b=cols(a["ffn_conv_b_2"]), rg_w=cols(a["rg_conv_w_2"]),
                 rg_b=cols(a["rg_conv_b_2"]), rg_ba=cols(a["rg_ba_2"]), rg_bx=cols(a["rg_bx_2"]),
                 gla_b=cols(a["gla_b_alpha_2"]), gla_g=cols(a["gla_norm_g_2"]), gla_z=wz)
    for n, v in parts.items():
        assert v.shape == (P, PARAMS[n]), (n, v.shape)
    return np.ascontiguousarray(np.concatenate([parts[n] for n in PARAMS], 1))


def kernel(**inputs):
    import concourse.bacc as _bacc
    from concourse.bass_utils import run_bass_kernel_spmd as _run

    arrays = {n: np.ascontiguousarray(np.asarray(inputs[n])) for n in WEIGHTS}
    arrays["x"] = np.ascontiguousarray(np.asarray(inputs["x"])[0].T)
    arrays["ctx"] = np.ascontiguousarray(np.asarray(inputs["ctx"])[0].T)
    arrays["params"] = pack_params(inputs)
    arrays["tables"], arrays["level"] = shape_tables()

    def build(counts):
        nc = _bacc.Bacc("TRN2", target_bir_lowering=False, num_devices=1)
        io = {n: nc.dram_tensor(f"in_{n}", a.shape, F32, kind="ExternalInput").ap() for n, a in arrays.items()}
        io["out"] = nc.dram_tensor("out", (D, S), F32, kind="ExternalOutput").ap()
        return nc, program(nc, io, counts)

    _, counts = build(None)
    nc, again = build(counts)
    assert again == counts
    r = _run(nc, [{f"in_{n}": a for n, a in arrays.items()}], core_ids=[0])
    return np.ascontiguousarray(np.asarray(r.results[0]["out"]).T)[None]
```

```python
from contextlib import ExitStack

import numpy as np
import concourse.bass as bass
from concourse import mybir

F32 = mybir.dt.float32
F32R = mybir.dt.float32r
ACT = mybir.ActivationFunctionType
ALU = mybir.AluOpType
AX_X = mybir.AxisListType.X

P = 128
D = 1024
KT = D // P
S = 256
ST = S // P
BW = 512
BT = BW // P
HEADS = 4
ATT_DH = 64
ATT_SCALE = ATT_DH ** -0.5
K_SCALE = 128 ** -0.5
SC_K, CF_K, FF_K, RG_K = 3, 31, 3, 4
PAD = CF_K // 2
D_FF = 2816
FT = D_FF // P
GLA_H = 4
GLA_DK = 128
EPS = 1e-6
LEVELS = (1, 2, 4, 8, 16, 32, 64)
RING = 3
PARTS = 3
AHEAD = 2
SLAB = 2048
BANKS = 8

IN_COL = dict(ret_q=0, ret_k=512, ret_v=1024, ret_z=1536, sc_b=2048, sc_c=2560, sc_x=3072, sc_z=3584,
              cf_a=4096, cf_g=4608, cf_z=5120, att_q=5632, att_kv=6144, att_z=6400, gates=6912)
BRANCHES = dict(ret=0, sc=1, cf=2, att=3)
MERGE_ORDER = ("sc", "ret", "att", "cf")

PARAMS = dict(norm_w=2 * 8, gn_w=2 * 4, sc_w=2 * 4 * SC_K, cf_w=2 * 4 * CF_K, cf_b=2 * 4, ln_w=2 * 4, ln_b=2 * 4,
              sink=2 * 8, b_mod=2 * 24, fin_w=8, decay=16, lam=8, c_vec=24,
              ada_b=2 * 48, norm_g=2 * 4 * 8, ff_w=2 * FF_K * 44, ff_b=2 * 44,
              rg_w=RG_K * 8, rg_b=8, rg_ba=8, rg_bx=8, gla_b=4, gla_g=2, gla_z=8 * 16)
TABLES = dict(ident=P, ones=P, turn=P, cos=S, sin=S, ahead=2 * S, behind=2 * S, q_pos=2 * S, k_pos=4,
              band=2 * P, eps=1)
LATE = 8 * P


def offsets(sizes):
    at, out = 0, {}
    for name, n in sizes.items():
        out[name] = (at, n)
        at += n
    return out, at


PARAM_AT, N_PARAM = offsets(PARAMS)
TABLE_AT, N_TABLE = offsets(TABLES)


class Steps:

    def __init__(self, sem, known):
        self.sem, self.known, self.n, self.now = sem, known, 0, {}

    def does(self, *names):
        self.n += 1
        for name in names:
            assert name not in self.now, name
            self.now[name] = self.n
        return self.sem, 1

    def did(self, name):
        if name in self.now:
            return self.sem, self.now[name]
        return self.sem, (self.known[name] if self.known is not None else 1)


def program(nc, io, counts):
    ctx = ExitStack()
    with ctx:
        def sbuf(name, cols, dtype=F32):
            return ctx.enter_context(nc.sbuf_tensor(name, [P, cols], dtype))

        def sem(name):
            return ctx.enter_context(nc.semaphore(name))

        counts = counts or dict(tensor=None, vector=None, scalar=None)
        tensor = Steps(sem("tensor_done"), counts["tensor"])
        vector = Steps(sem("vector_done"), counts["vector"])
        scalar = Steps(sem("scalar_done"), counts["scalar"])

        def emptied(name):
            for e in (vector, scalar):
                if "emptied " + name in (e.known or {}):
                    return e.did("emptied " + name)
            return vector.sem, 1

        def used(slab):
            for e in (vector, tensor):
                if "used " + slab in (e.known or {}):
                    return e.did("used " + slab)
            return vector.sem, 1

        slab_landed = [sem(f"slab_landed{i}") for i in range(RING)]
        params_landed, tables_landed = sem("params_landed"), sem("tables_landed")
        x_landed, late_landed, out_landed = sem("x_landed"), sem("late_landed"), sem("out_landed")

        ring = [sbuf(f"ring{i}", SLAB) for i in range(RING)]
        params, tables = sbuf("params", N_PARAM), sbuf("tables", N_TABLE)
        xT = sbuf("xT", KT * 2 * S)[:].rearrange("p (t s) -> p t s", t=KT)
        h_hi, h_lo = (sbuf(n, KT * 2 * S, F32R)[:].rearrange("p (t s) -> p t s", t=KT) for n in ("h_hi", "h_lo"))
        w_hi, w_lo = ([sbuf(f"{n}{i}", KT * P, F32R)[:].rearrange("p (t n) -> p t n", t=KT) for i in range(PARTS)]
                      for n in ("w_hi", "w_lo"))

        def param(name, *dims):
            at, n = PARAM_AT[name]
            ap = params[:, at:at + n]
            if len(dims) == 1:
                return ap.rearrange("p (a b) -> p a b", a=dims[0])
            if len(dims) == 2:
                return ap.rearrange("p (a b c) -> p a b c", a=dims[0], b=dims[1])
            if len(dims) == 3:
                return ap.rearrange("p (a b c d) -> p a b c d", a=dims[0], b=dims[1], c=dims[2])
            return ap

        def table(name):
            at, n = TABLE_AT[name]
            return tables[:, at:at + n]

        ident, ones, turn = table("ident"), table("ones"), table("turn")
        ones_pp = ones
        eps = table("eps")
        at = TABLE_AT["ahead"][0]
        level = tables[:, at:at + LATE]
        gla_a = tables[0:16, at + LATE:at + LATE + 512]

        arena_cols = 18456
        arena = sbuf("arena", arena_cols)

        def carve(at, *dims):
            n = int(np.prod(dims))
            assert at + n <= arena_cols, (at, dims)
            ap = arena[:, at:at + n]
            if len(dims) == 2:
                return ap.rearrange("p (a b) -> p a b", a=dims[0])
            if len(dims) == 3:
                return ap.rearrange("p (a b c) -> p a b c", a=dims[0], b=dims[1])
            if len(dims) == 4:
                return ap.rearrange("p (a b c d) -> p a b c d", a=dims[0], b=dims[1], c=dims[2])
            return ap

        cx = carve(0, BT, 2, S + 2)
        u_pad = carve(0, BT, 2, S + 2 * PAD)
        k_wt = [carve(1024 * i, ST, HEADS, P) for i in range(2)]
        att_o = carve(0, BT, 2 * S)
        s_br = carve(2288, BT, 2 * S)
        f_br = carve(4336, BT, 2 * S)
        ret_q = ret_o = carve(6384, BT, 2 * S)
        ret_k, ret_v = carve(8432, BT, 2 * S), carve(10480, 2 * ST, BW)
        att_q = carve(12528, BT, 2 * S)
        z_sil = dict(ret=carve(8432, BT, 2 * S), att=carve(10480, BT, 2 * S), cf=carve(12528, BT, 2 * S))
        merged = carve(8432, KT, 2 * S)
        att_k, att_ks = carve(14576, 2 * S), carve(15088, 2 * S)
        att_v = carve(15600, 2 * ST, P)
        state = carve(16112, HEADS, 2, P)
        branch = dict(ret=ret_o, sc=s_br, cf=f_br, att=att_o)

        yT, sq8 = carve(0, KT, S), carve(2048, KT, S)
        xb_pad = carve(4096, KT, S + RG_K - 1)
        xc, gel, rr, tt_, ix, a2 = (carve(6168 + 2048 * i, KT, S) for i in range(6))
        lv = carve(0, 8, GLA_H * S)
        gla_o = carve(4096, KT, S)
        gq, gk, la, le, gg = (carve(8192 + 1024 * i, GLA_H, S) for i in range(5))
        lprod = carve(10240, 8, P)
        r_sil = carve(11264, KT, S)
        gv = carve(13312, ST, D)
        attT = carve(15360, GLA_H, ST, S)
        zT, scan_one = carve(17408, S), carve(17664, S)
        ff_act = carve(4096, FT, S)

        work = [sbuf(f"work{i}", 2 * S) for i in range(8)]
        act_t = work[0:4]
        dve_t = work[4:8]
        stat = sbuf("stat", 2 * S)
        stat2 = sbuf("stat2", 2 * S)
        exps = (act_t[0], act_t[1], stat, stat2)
        small = sbuf("small", 256)
        soft_m, soft_s = small[:, 0:8], small[:, 8:16]
        soft_e, soft_d = small[:, 16:24], small[:, 24:32]
        csil = small[:, 32:56].rearrange("p (t v) -> p t v", t=KT)
        soft_p = small[:, 56:80]
        k_decay = small[:, 80:112].rearrange("p (l d t h) -> p l d t h", l=2, d=2, t=2)
        nsink = small[:, 112:128].rearrange("p (l h) -> p l h", l=2)
        lp = [small[:, 128 + 24 * i:152 + 24 * i] for i in range(4)]
        log_g = small[:, 224:240].rearrange("p (l d h) -> p l d h", l=2, d=2)
        lam8, lam8n = small[:, 240:248], small[:, 248:256]
        rows = [sbuf(f"rows{i}", 2 * P) for i in range(2)]
        mods = sbuf("mods", 2 * 48 + 2 * 16 + 2 * 48 + 2 * 32)
        mod1 = [mods[:, 48 * l:48 * l + 48].rearrange("p (n v) -> p n v", v=2) for l in range(2)]
        gain1 = [mods[:, 96 + 16 * l:112 + 16 * l].rearrange("p (n v) -> p n v", v=2) for l in range(2)]
        mod2 = [mods[:, 128 + 48 * l:176 + 48 * l] for l in range(2)]
        gain2 = [mods[:, 224 + 32 * l:256 + 32 * l].rearrange("p (q t) -> p q t", q=4) for l in range(2)]

        psum = [ctx.enter_context(nc.psum_tensor(f"bank{i}", [P, 512], F32)) for i in range(BANKS)]
        bank_at = {}

        def bank(name):
            return psum[bank_at[name] % BANKS]

        stream, w_units, unit_of = [], [], {}

        def by_rows(w):
            return w.rearrange("(t p) n -> p t n", p=P)

        def cols(name, w, c0, n=256):
            src = by_rows(w)[:, :, c0:c0 + n]
            stream.append((name, src, (src.shape[1], n)))

        def split_cols(name, tiles, w, c0, run):
            for j, tile in enumerate(tiles):
                unit_of[tile] = len(w_units)
                w_units.append((len(stream), j, run))
            cols(name, w, c0)

        def section(l, name, i, run):
            tiles = (f"att_k {l}", f"att_v {l}") if name == "att_kv" else [f"{name} {l}.{2 * i + j}" for j in range(2)]
            split_cols(f"w {name} {l}.{i}", tiles, io["w_in"][l], IN_COL[name] + 256 * i, run)

        def split_until(tile):
            i = unit_of[tile]
            u = i
            for v in range(i + 1, min(i + AHEAD + 1, len(w_units))):
                before = w_units[v][0] - RING
                native = before >= 0 and stream[before][0].split(" ")[1] in ("branch", "out", "down", "rgo", "glao")
                if w_units[v][2] == w_units[i][2] and not (native and before > w_units[i][0]):
                    u = v
            return u

        mod_at = {"start": [("mod", 0, i) for i in range(8)],
                  "n1 1": [("ada", 0, i) for i in range(0, 7)],
                  "fin": [("ada", 0, 23)] + [("ada", 1, i) for i in range(0, 4)],
                  "n2 0": [("ada", 1, i) for i in range(4, 10)],
                  "rg": [("ada", 1, i) for i in range(10, 16)],
                  "post rg": [("ada", 1, i) for i in range(16, 20)],
                  "n3 0": [("ada", 1, i) for i in range(20, 24)]}
        merge_mods = [[("mod", 0, i) for i in range(8, 12)] + [("mod", 1, i) for i in range(12)],
                      [("ada", 0, i) for i in range(7, 23)]]

        def mod_slab(kind, l, i):
            cols(f"w {kind} {l}.{i}", io["w_mod" if kind == "mod" else "ada_w_2"][l], 256 * i)

        def mod_slabs(at):
            for m in mod_at[at]:
                mod_slab(*m)

        mod_slabs("start")
        for l in range(2):
            run = f"in {l}"
            for i in range(2):
                section(l, "sc_c", i, run)
                if l and i == 0:
                    mod_slabs("n1 1")
                section(l, "sc_x", i, run)
            for i in range(2):
                section(l, "cf_g", i, run)
                section(l, "cf_a", i, run)
            for a in ("ret_q", "ret_k", "ret_v", "att_q"):
                for i in range(2):
                    section(l, a, i, run)
            section(l, "att_kv", 0, run)
            for i in range(2):
                section(l, "sc_b", i, run)
                section(l, "sc_z", i, run)
            run = f"merge {l}"
            for a in ("ret_z", "att_z", "cf_z"):
                for i in range(2):
                    section(l, a, i, run)
            for b in MERGE_ORDER:
                for i in range(4):
                    split_cols(f"w gate {l}.{b}.{i}", [f"gate {l}.{b}.{2 * i + j}" for j in range(2)], io["w_in"][l],
                               IN_COL["gates"] + D * BRANCHES[b] + 256 * i, run)
                    mod_slab(*merge_mods[l][4 * MERGE_ORDER.index(b) + i])
                    cols(f"w branch {l}.{b}.{i}", io["w_branch"][l, BRANCHES[b]], 256 * i)
            for i in range(4):
                cols(f"w out {l}.{i}", io["w_out"][l], 256 * i)

        def ffn_slabs(l):
            for i in range(11):
                for nm, c0 in (("ffg", 0), ("ffv", D_FF)):
                    split_cols(f"w {nm} {l}.{i}", [f"{nm} {l}.{2 * i + j}" for j in range(2)], io["ffn_w_up_2"][l],
                               c0 + 256 * i, f"ffn {l}")
                    if l == 0 and i == 0 and nm == "ffg":
                        mod_slabs("n3 0")
            down = by_rows(io["ffn_w_down_2"][l])
            for c in range(4):
                for k0 in range(0, FT, 8):
                    n = min(8, FT - k0)
                    stream.append((f"w down {l}.{c}.{k0}", down[:, k0:k0 + n, 256 * c:256 * c + 256], (n, 256)))

        mod_slabs("fin")
        for nm, c0 in (("rgx", D), ("rgg", 0)):
            for i in range(4):
                split_cols(f"w {nm} {i}", [f"{nm} {2 * i + j}" for j in range(2)], io["rg_w_in_2"][0], c0 + 256 * i, "rg")
                if nm == "rgx" and i == 0:
                    mod_slabs("n2 0")
        for n in ("a", "x"):
            stream.append((f"w rg{n}", io[f"rg_w{n}_2"][0].rearrange("g (t p) n -> p (g t) n", p=P), (8, 256)))
        mod_slabs("rg")
        for i in range(4):
            cols(f"w rgo {i}", io["rg_w_out_2"][0], 256 * i)
        mod_slabs("post rg")
        ffn_slabs(0)
        for n, c0, k in (("q", 0, 2), ("k", 512, 2), ("v", 1024, 4), ("r", 2048, 4)):
            for i in range(k):
                split_cols(f"w gla{n} {i}", [f"gla{n} {2 * i + j}" for j in range(2)], io["gla_w_in_2"][0],
                           c0 + 256 * i, "gla")
        for i in range(4):
            cols(f"w glao {i}", io["gla_w_out_2"][0], 256 * i)
        ffn_slabs(1)

        def mod_turns(at, n):
            last = len(mod_at[at])
            return [b for b in ((n - 2, n - 1) if n == last else (n - 2,)) if b >= 0]

        def mod_col(at, b, j):
            return 256 + 4 * (b % 2) + 2 * j

        def acc_of(m):
            l = next(l for l in range(2) if m in merge_mods[l])
            return (stat, stat2)[merge_mods[l].index(m) % 2]

        slab_of = {name: n for n, (name, _, _) in enumerate(stream)}

        def slot_of(n):
            a, b = stream[n][2]
            return ring[n % RING][:, 0:a * b].rearrange("p (a b) -> p a b", a=a)

        block = ctx.enter_context(nc.Block())

        @block.tensor
        def _(pe):
            state_ = dict(bank=0)

            def take(name):
                n = slab_of[name]
                pe.wait_ge(slab_landed[n % RING], 16 * (n // RING + 1))
                return slot_of(n)

            def open_bank(name):
                n = state_["bank"]
                state_["bank"] += 1
                bank_at[name] = n
                if n >= BANKS:
                    pe.wait_ge(*emptied(order[n - BANKS]))
                order.append(name)
                return psum[n % BANKS]

            order = []

            def tile(name, w, c0, rhs, n, free=None):
                out = open_bank(name)
                nk = w.shape[1]
                for k in range(nk):
                    m = pe.matmul(out[:, 0:n], w[:, k, c0:c0 + P], rhs(k), start=k == 0, stop=k == nk - 1)
                m.then_inc(*tensor.does("filled " + name, *([f"used {free}"] if free else [])))

            def unit(name):
                u = unit_of[name]
                pe.wait_ge(*scalar.did(f"hi {u}"))
                pe.wait_ge(*vector.did(f"lo {u}"))
                return w_hi[u % PARTS], w_lo[u % PARTS], f"used unit {u}"

            def project(name, n):
                hi, lo, used_unit = unit(name)
                out = open_bank(name)
                for k in range(KT):
                    pe.matmul(out[:, 0:n], hi[:, k, :], h_hi[:, k, 0:n], start=k == 0, stop=False)
                    pe.matmul(out[:, 0:n], hi[:, k, :], h_lo[:, k, 0:n], start=False, stop=False)
                    m = pe.matmul(out[:, 0:n], lo[:, k, :], h_hi[:, k, 0:n], start=False, stop=k == KT - 1)
                m.then_inc(*tensor.does("filled " + name, used_unit))

            def turn_tokens(name, src, tiles):
                pe.wait_ge(*scalar.did("rows " + name))
                out = open_bank("turned " + name)
                for t in range(tiles):
                    m = pe.transpose(out[:, P * t:P * t + P], src[:, P * t:P * t + P], ident)
                m.then_inc(*tensor.does("filled turned " + name))

            def mod_contract(m):
                kind, l, i = m
                name = f"{kind} {l}.{i}"
                acc = acc_of(m)
                pe.wait_ge(*vector.did("acc " + name))
                out = open_bank("sum " + name)
                for j in range(2):
                    for c in range(2):
                        o = 2 * j + c if kind == "mod" else j
                        ins = pe.matmul(out[:, o:o + 1], acc[:, 2 * P * c + P * j:2 * P * c + P * j + P], ones[:, 0:1],
                                        start=kind == "mod" or c == 0, stop=kind == "mod" or c == 1)
                ins.then_inc(*tensor.does("filled sum " + name))

            def mod_step(at, n):
                todo = mod_at[at]
                name = "%s %d.%d" % todo[n] if n < len(todo) else "end " + at
                w = take("w " + name) if n < len(todo) else None
                out = open_bank("row " + name)
                if w is not None:
                    vecs = csil[:, :, 0:2] if todo[n][0] == "mod" else csil[:, :, 2:3]
                    for k in range(KT):
                        m = pe.matmul(out[0:vecs.shape[2], 0:256], vecs[:, k, :], w[:, k, :],
                                      start=k == 0, stop=k == KT - 1)
                for b in mod_turns(at, n):
                    kind, l, i = todo[b]
                    nv = 2 if kind == "mod" else 1
                    pe.wait_ge(*scalar.did(f"row {kind} {l}.{i}"))
                    for j in range(2):
                        c = mod_col(at, b, j)
                        m = pe.transpose(out[:, c:c + nv], rows[b % 2][0:nv, P * j:P * j + P], ident[0:nv, 0:nv])
                m.then_inc(*tensor.does("filled row " + name, *(["used w " + name] if w is not None else [])))

            def modulations(at):
                if mod_at[at]:
                    for n in range(len(mod_at[at]) + 1):
                        mod_step(at, n)

            def sum_squares(name, n, tiles):
                out = open_bank(name)
                for k in range(tiles):
                    pe.wait_ge(*scalar.did(f"sq {name}.{k}"))
                    m = pe.matmul(out[:, 0:n], ones_pp, squares(name, k, n), start=k == 0, stop=k == tiles - 1)
                    m.then_inc(*tensor.does(f"summed {name}.{k}", *(["filled " + name] if k == tiles - 1 else [])))

            def squares(name, k, n):
                return act_t[k % 4][:, 0:n]

            def h_ready(name):
                for k in range(KT):
                    pe.wait_ge(*scalar.did(f"h_hi {name}.{k}"))
                    pe.wait_ge(*vector.did(f"h_lo {name}.{k}"))

            pe.wait_ge(params_landed, 16)
            pe.wait_ge(tables_landed, 16)
            pe.wait_ge(*scalar.did("csil"))

            for l in range(2):
                nx = 2 * S if l == 0 else S
                groups = (0, 1) if l == 0 else (0,)
                if l == 0:
                    modulations("start")
                sum_squares(f"n1 {l}", 2 * S, KT)
                if l:
                    modulations("n1 1")
                h_ready(f"n1 {l}")
                for a, b in (("sc_c", "sc_x"), ("cf_g", "cf_a")):
                    for i in range(2):
                        for n in (a, b):
                            for j in range(2):
                                project(f"{n} {l}.{2 * i + j}", nx)
                for n in range(BT):
                    project(f"ret_q {l}.{n}", nx)
                for n in range(BT):
                    project(f"ret_k {l}.{n}", 2 * S)
                for n in range(BT):
                    project(f"ret_v {l}.{n}", 2 * S)
                    if n:
                        turn_tokens(f"ret_v {l}.{n - 1}", act_t[(n - 1) % 2], 2 * ST)
                for n in range(BT):
                    project(f"att_q {l}.{n}", nx)
                    if n == 0:
                        turn_tokens(f"ret_v {l}.{BT - 1}", act_t[(BT - 1) % 2], 2 * ST)
                project(f"att_k {l}", 2 * S)
                project(f"att_v {l}", 2 * S)
                for i in range(2):
                    for n in ("sc_b", "sc_z"):
                        for j in range(2):
                            project(f"{n} {l}.{2 * i + j}", nx)
                            if (n, i, j) == ("sc_b", 0, 0):
                                turn_tokens(f"att_v {l}", act_t[0], 2 * ST)

                for t in range(BT + 1):
                    src = att_q[:, t, 0:S] if t < BT else att_k[:, 0:S]
                    pe.wait_ge(*scalar.did(f"att_q {l}.{t}" if t < BT else f"att_k {l}"))
                    out = open_bank(f"turn {l}.{t}")
                    pe.matmul(out[:, 0:S], turn, src, start=True, stop=True)\
                        .then_inc(*tensor.does(f"filled turn {l}.{t}"))

                for t in range(ST):
                    out = open_bank(f"kT {l}.{t}")
                    for hd in range(HEADS):
                        pe.wait_ge(*scalar.did(f"ret_k {l}.{hd}"))
                        m = pe.transpose(out[:, P * hd:P * hd + P], ret_k[:, hd, S + P * t:S + P * t + P], ident)
                    m.then_inc(*tensor.does(f"filled kT {l}.{t}"))
                pe.wait_ge(*scalar.did(f"ret_v {l}.{BT - 1}"))
                for hd in range(HEADS):
                    out = open_bank(f"state {l}.{hd}")
                    for d in range(2):
                        pe.wait_ge(*vector.did(f"k_wt {l}.{ST - 1}.{d}"))
                        for t in range(ST):
                            m = pe.matmul(out[:, P * d:P * d + P], k_wt[d][:, t, hd, :],
                                          ret_v[:, ST + t, P * hd:P * hd + P], start=t == 0, stop=t == ST - 1)
                    m.then_inc(*tensor.does(f"filled state {l}.{hd}"))

                units = [(hd, g) for hd in range(HEADS) for g in groups]

                def ret_scores(hd, g):
                    name = f"rs {l}.{hd}.{g}"
                    pe.wait_ge(*scalar.did(f"ret_q {l}.{hd}"))
                    out = open_bank(name)
                    for j in range(ST):
                        m = pe.matmul(out[:, S * j:S * j + S], ret_k[:, hd, S * g + P * j:S * g + P * j + P],
                                      ret_q[:, hd, S * g:S * g + S], start=True, stop=True)
                    m.then_inc(*tensor.does("filled " + name))

                def ret_out(hd, g):
                    name = f"ro {l}.{hd}.{g}"
                    pe.wait_ge(*vector.did(f"ret_p {l}.{hd}.{g}"))
                    p_t = dve_t[2 + units.index((hd, g)) % 2]
                    out = open_bank(name)
                    for j in range(ST):
                        m = pe.matmul(out[:, 0:S], ret_v[:, ST * g + j, P * hd:P * hd + P], p_t[:, S * j:S * j + S],
                                      start=j == 0, stop=g == 1 and j == ST - 1)
                    if g == 0:
                        pe.wait_ge(*scalar.did(f"state {l}.{hd}"))
                        pe.wait_ge(*vector.did(f"q_wt {l}.{hd}"))
                        for d in range(2):
                            m = pe.matmul(out[:, 0:S], state[:, hd, d, :], dve_t[hd % 2][:, S * d:S * d + S],
                                          start=False, stop=d == 1)
                    m.then_inc(*tensor.does("filled " + name))

                for n, (hd, g) in enumerate(units):
                    ret_scores(hd, g)
                    if n:
                        ret_out(*units[n - 1])
                ret_out(*units[-1])

                att = [(g, t, q) for g in groups for t in range(BT) for q in range(ST)]

                def att_scores(i):
                    g, t, q = att[i]
                    keys = 0 if g == 0 else S
                    for s in range(2):
                        name = f"as {l}.{i}.{s}"
                        rows = slice(64 * s, 64 * s + 64)
                        k_src = att_k if s == t // 2 else att_ks
                        out = open_bank(name)
                        pe.matmul(out[:, 0:2 * S - keys], att_q[rows, t, S * g + P * q:S * g + P * q + P],
                                  k_src[rows, keys:2 * S], start=True, stop=True)\
                            .then_inc(*tensor.does("filled " + name))

                def gate_of(i):
                    every = len(att) // (2 * BT)
                    n = i // every
                    return (("ret", "att")[n // BT], l, n % BT) if i % every == 0 and n < 2 * BT else None

                def att_turn(i):
                    g, t, q = att[i]
                    for s in range(2):
                        name = f"at {l}.{i}.{s}"
                        pe.wait_ge(*vector.did(f"att_p {l}.{i}.{s}"))
                        out = open_bank(name)
                        for b in range(4 - 2 * g):
                            m = pe.transpose(out[:, P * b:P * b + P], dve_t[2 * (i % 2) + s][:, P * b:P * b + P], ident)
                        m.then_inc(*tensor.does("filled " + name))

                def att_out(i):
                    g, t, q = att[i]
                    name = f"ao {l}.{i}"
                    out = open_bank(name)
                    for s in range(2):
                        pe.wait_ge(*scalar.did(f"att_t {l}.{i}.{s}"))
                        nb = 4 - 2 * g
                        c = 64 * (t // 2)
                        for b in range(nb):
                            m = pe.matmul(out[64 * s:64 * s + 64, 0:P], att_v[:, 2 * g + b, c:c + 64],
                                          act_t[2 + s][:, P * b:P * b + P], start=b == 0, stop=b == nb - 1)
                    m.then_inc(*tensor.does("filled " + name))

                pe.wait_ge(*vector.did(f"att_q roped {l}.{BT - 1}"))
                pe.wait_ge(*vector.did(f"att_ks {l}"))
                pe.wait_ge(*scalar.did(f"att_v {l}"))
                att_scores(0)
                for i in range(len(att) + 2):
                    if i + 1 < len(att):
                        att_scores(i + 1)
                    if gate_of(i):
                        project("%s_z %d.%d" % gate_of(i), nx)
                    if i >= 2:
                        att_out(i - 2)
                    if 1 <= i <= len(att):
                        att_turn(i - 1)

                for hd in range(HEADS):
                    pe.wait_ge(*scalar.did(f"ret_o {l}.{hd}.{groups[-1]}"))
                    name = f"gm {l}.{hd}"
                    out = open_bank(name)
                    pe.matmul(out[:, 0:nx], ones_pp, ret_o[:, hd, 0:nx], start=True, stop=True)\
                        .then_inc(*tensor.does("filled " + name))
                name = f"lm {l}"
                out = open_bank(name)
                for t in range(BT):
                    pe.wait_ge(*vector.did(f"conv {l}.{t}"))
                    m = pe.matmul(out[:, 0:nx], ones_pp, f_br[:, t, 0:nx], start=t == 0, stop=t == BT - 1)
                m.then_inc(*tensor.does("filled " + name))
                for n in range(2):
                    project(f"cf_z {l}.{n}", nx)
                for hd in range(HEADS):
                    name = f"gv {l}.{hd}"
                    pe.wait_ge(*scalar.did(f"sq {name}"))
                    pe.matmul(open_bank(name)[:, 0:nx], ones_pp, act_t[hd][:, 0:nx], start=True, stop=True)\
                        .then_inc(*tensor.does("filled " + name))
                for n in range(2, BT):
                    project(f"cf_z {l}.{n}", nx)
                sum_squares(f"lv {l}", nx, BT)

                for b in MERGE_ORDER:
                    for t in range(BT):
                        pe.wait_ge(*vector.did(f"branch {l}.{b}.{t}"))
                    for i in range(4):
                        for j in range(2):
                            n = 2 * i + j
                            project(f"gate {l}.{b}.{n}", nx)
                            if j == 0:
                                wb = take(f"w branch {l}.{b}.{i}")
                            else:
                                mod_contract(merge_mods[l][4 * MERGE_ORDER.index(b) + i])
                            tile(f"br {l}.{b}.{n}", wb, P * j, lambda k: branch[b][:, k, 0:nx], nx,
                                 f"w branch {l}.{b}.{i}" if j else None)
                for k in range(KT):
                    pe.wait_ge(*vector.did(f"merged {l}.{MERGE_ORDER[-1]}.{k}"))
                for i in range(4):
                    w = take(f"w out {l}.{i}")
                    for j in range(2):
                        tile(f"out {l}.{2 * i + j}", w, P * j, lambda k: merged[:, k, 0:nx], nx,
                             f"w out {l}.{i}" if j else None)

            sum_squares("fin", S, KT)
            modulations("fin")

            def ffn(l):
                sum_squares(f"n3 {l}", S, KT)
                if l == 0:
                    modulations("n3 0")
                h_ready(f"n3 {l}")
                for i in range(11):
                    for nm in ("ffg", "ffv"):
                        for j in range(2):
                            project(f"{nm} {l}.{2 * i + j}", S)
                for c in range(4):
                    names = [f"y ffn {l}.{2 * c + j}" for j in range(2)]
                    outs = [open_bank(name) for name in names]
                    for k0 in range(0, FT, 8):
                        w = take(f"w down {l}.{c}.{k0}")
                        last = k0 + 8 >= FT
                        for j in range(2):
                            for k in range(w.shape[1]):
                                if c == 0 and j == 0:
                                    pe.wait_ge(*vector.did(f"ff_act {l}.{k0 + k}"))
                                m = pe.matmul(outs[j][:, 0:S], w[:, k, P * j:P * j + P], ff_act[:, k0 + k, :],
                                              start=k0 + k == 0, stop=k0 + k == FT - 1)
                            done = ["filled " + names[j]] if last else []
                            if j:
                                done.append(f"used w down {l}.{c}.{k0}")
                            if done:
                                m.then_inc(*tensor.does(*done))
                post(f"ffn {l}")

            def post(tag):
                out = open_bank(f"ys {tag}")
                for k in range(KT):
                    pe.wait_ge(*scalar.did(f"y {tag}.{k}"))
                    m = pe.matmul(out[:, 0:S], ones_pp, sq8[:, k, :], start=k == 0, stop=k == KT - 1)
                m.then_inc(*tensor.does(f"filled ys {tag}"))

            sum_squares("n2 0", S, KT)
            modulations("n2 0")
            h_ready("n2 0")
            for nm in ("rgx", "rgg"):
                for n in range(KT):
                    project(f"{nm} {n}", S)
            for nm in ("rga", "rgx2"):
                slab = "w rga" if nm == "rga" else "w rgx"
                w = take(slab)
                for n in range(KT):
                    gblk, j = n // 2, n % 2
                    out = open_bank(f"{nm} {n}")
                    for i in range(2):
                        pe.wait_ge(*vector.did(f"xc {2 * gblk + i}"))
                        m = pe.matmul(out[:, 0:S], w[:, 2 * gblk + i, P * j:P * j + P], xc[:, 2 * gblk + i, :],
                                      start=i == 0, stop=i == 1)
                    m.then_inc(*tensor.does(f"filled {nm} {n}", *([f"used {slab}"] if n == KT - 1 else [])))
            modulations("rg")
            for k in range(KT):
                pe.wait_ge(*vector.did(f"rg_y {k}"))
            for i in range(4):
                w = take(f"w rgo {i}")
                for j in range(2):
                    tile(f"y rg.{2 * i + j}", w, P * j, lambda k: xc[:, k, :], S, f"w rgo {i}" if j else None)
            post("rg")
            modulations("post rg")
            ffn(0)

            sum_squares("n2 1", S, KT)
            h_ready("n2 1")
            wz, wa = param("gla_z", KT), gla_a
            out = open_bank("gla z")
            for k in range(KT):
                pe.matmul(out[0:16, 0:S], wz[:, k, :], h_hi[:, k, 0:S].bitcast(F32), start=k == 0, stop=False)
                m = pe.matmul(out[0:16, 0:S], wz[:, k, :], h_lo[:, k, 0:S].bitcast(F32), start=False, stop=k == KT - 1)
            m.then_inc(*tensor.does("filled gla z"))
            pe.wait_ge(*scalar.did("zT"))
            pe.wait_ge(late_landed, 32)
            for hd in range(GLA_H):
                out = open_bank(f"alpha {hd}")
                pe.matmul(out[:, 0:S], wa[:, P * hd:P * hd + P], zT[0:16, :], start=True, stop=True)\
                    .then_inc(*tensor.does(f"filled alpha {hd}"))
            for nm in ("q", "k"):
                for n in range(GLA_H):
                    project(f"gla{nm} {n}", S)
            for n in range(KT):
                project(f"glav {n}", S)
                if n:
                    turn_tokens(f"glav {n - 1}", act_t[(n - 1) % 2], ST)
            turn_tokens(f"glav {KT - 1}", act_t[(KT - 1) % 2], ST)
            for n in range(GLA_H * ST):
                hd, t = n // ST, n % ST
                sl = slice(S * hd + P * t, S * hd + P * t + P)
                for half in range(2):
                    name = f"lev {n}.{half}"
                    for q in range(4):
                        if n == 0:
                            pe.wait_ge(*vector.did(f"lv {4 * half + q}"))
                    out = open_bank(name)
                    for q in range(4):
                        i = 4 * half + q
                        if i < len(LEVELS):
                            m = pe.matmul(out[:, P * q:P * q + P], lv[:, i, sl], lv[:, i, sl], start=True, stop=True)
                        else:
                            m = pe.matmul(out[:, P * q:P * q + P], gk[:, hd, P * t:P * t + P],
                                          gq[:, hd, P * t:P * t + P], start=True, stop=True)
                    m.then_inc(*tensor.does("filled " + name))
                if t == 1:
                    out = open_bank(f"cross {hd}")
                    pe.matmul(out[:, 0:P], lv[:, 7, S * hd:S * hd + P], lv[:, 7, S * hd + P:S * hd + S],
                              start=True, stop=True).then_inc(*tensor.does(f"filled cross {hd}"))
                project(f"glar {n}", S)
            pe.wait_ge(*scalar.did("gv 7"))
            for hd in range(GLA_H):
                for j in range(ST):
                    pe.wait_ge(*vector.did(f"attT {ST * hd + j}"))
                pe.wait_ge(*scalar.did(f"cross {hd}"))
                for e in range(2):
                    name = f"go {2 * hd + e}"
                    out = open_bank(name)
                    c = 256 * hd + P * e
                    pe.matmul(out[:, 0:S], gv[:, 0, c:c + P], attT[:, hd, 0, :], start=True, stop=False)
                    pe.matmul(out[:, P:S], gv[:, 1, c:c + P], attT[:, hd, 1, P:S], start=False, stop=True)\
                        .then_inc(*tensor.does("filled " + name))
            for hd in range(GLA_H):
                out = open_bank(f"gs {hd}")
                for e in range(2):
                    pe.wait_ge(*scalar.did(f"go {2 * hd + e}"))
                    m = pe.matmul(out[:, 0:S], ones_pp, sq8[:, 2 * hd + e, :], start=e == 0, stop=e == 1)
                m.then_inc(*tensor.does(f"filled gs {hd}"))
            for k in range(KT):
                pe.wait_ge(*vector.did(f"gla_y {k}"))
            for i in range(4):
                w = take(f"w glao {i}")
                for j in range(2):
                    tile(f"y gla.{2 * i + j}", w, P * j, lambda k: gla_o[:, k, :], S, f"w glao {i}" if j else None)
            post("gla")
            ffn(1)

        @block.sync
        def _(sp):
            sp.dma_start(params[:], io["params"]).then_inc(params_landed, 16)
            sp.dma_start(tables[:], io["tables"]).then_inc(tables_landed, 16)
            for n, (name, src, _) in enumerate(stream):
                if name == "w rgo 0":
                    sp.wait_ge(*vector.did(f"expo 1.{HEADS - 1}"))
                    sp.wait_ge(*scalar.did(f"q_dec 1.{HEADS - 1}"))
                    sp.dma_start(level, io["level"]).then_inc(late_landed, 16)
                    sp.dma_start(gla_a, io["gla_w_alpha_2"][0]).then_inc(late_landed, 16)
                if n == RING:
                    sp.dma_start(xT[:, :, 0:S], by_rows(io["x"])).then_inc(x_landed, 16)
                    sp.dma_start(xT[:, :, S:2 * S], by_rows(io["ctx"])).then_inc(x_landed, 16)
                if n >= RING:
                    sp.wait_ge(*used(stream[n - RING][0]))
                sp.dma_start(slot_of(n), src).then_inc(slab_landed[n % RING], 16)
            for k in range(KT):
                sp.wait_ge(*vector.did(f"x ffn 1.{k}"))
                sp.dma_start(by_rows(io["out"])[:, k, :], xT[:, k, 0:S]).then_inc(out_landed, 16)
            sp.wait_ge(out_landed, 16 * KT)

        @block.scalar
        def _(act):
            def evacuate(name, dst, func=ACT.Copy, also=(), last=True, **kw):
                act.wait_ge(*tensor.did("filled " + name))
                names = list(also) + ([f"emptied {name}"] if last else [])
                src = bank(name)[0:dst.shape[0], 0:int(np.prod(dst.shape[1:]))]
                if len(dst.shape) == 3:
                    src = src.rearrange("p (a b) -> p a b", a=dst.shape[1])
                return nc.scalar.activation(dst, src, func, **kw)\
                    .then_inc(*scalar.does(*names))

            fed = dict(n=0)

            def split_to(last):
                while fed["n"] <= last:
                    u = fed["n"]
                    n, half, _ = w_units[u]
                    act.wait_ge(slab_landed[n % RING], 16 * (n // RING + 1))
                    if u >= PARTS:
                        act.wait_ge(*tensor.did(f"used unit {u - PARTS}"))
                    nc.scalar.activation(w_hi[u % PARTS], slot_of(n)[:, :, P * half:P * half + P], ACT.Copy)\
                        .then_inc(*scalar.does(f"hi {u}"))
                    fed["n"] += 1

            def first_units(tile):
                split_to(unit_of[tile] + 1)

            def projected(name, dst, func=ACT.Copy, also=(), **kw):
                split_to(split_until(name))
                return evacuate(name, dst, func, also, **kw)

            def square_all(name, n, tiles, src, ready=None):
                for k in range(tiles):
                    if ready:
                        act.wait_ge(*ready(k))
                    if k >= 4:
                        act.wait_ge(*tensor.did(f"summed {name}.{k - 4}"))
                    nc.scalar.activation(act_t[k % 4][:, 0:n], src(k), ACT.Square)\
                        .then_inc(*scalar.does(f"sq {name}.{k}"))

            def deviation(name, n, count):
                evacuate(name, stat[:, 0:n], ACT.Sqrt, [f"dev {name}"], scale=1.0 / count, bias=eps)

            def mod_row(at, n):
                todo = mod_at[at]
                name = "row %s %d.%d" % todo[n] if n < len(todo) else f"row end {at}"
                turned = mod_turns(at, n)
                if n < len(todo):
                    evacuate(name, rows[n % 2][0:2 if todo[n][0] == "mod" else 1, :], also=[name], last=not turned)
                else:
                    act.wait_ge(*tensor.did("filled " + name))
                for b in turned:
                    kind, l, i = todo[b]
                    for j in range(2):
                        c = 2 * i + j
                        if kind == "mod":
                            dst, bias = mod1[l][:, c, :], param("b_mod", 2)[:, l, c:c + 1]
                        else:
                            dst, bias = mod2[l][:, c:c + 1], param("ada_b", 2)[:, l, c:c + 1]
                        at_ = mod_col(at, b, j)
                        a = nc.scalar.activation(dst, bank(name)[:, at_:at_ + dst.shape[1]], ACT.Identity, bias=bias)
                if turned:
                    a.then_inc(*scalar.does("emptied " + name, *["col %s %d.%d" % todo[b] for b in turned]))

            def mod_cols(m):
                kind, l, i = m
                name = f"sum {kind} {l}.{i}"
                act.wait_ge(*tensor.did("filled " + name))
                for j in range(2):
                    c = 2 * i + j
                    if kind == "mod":
                        dst, bias = mod1[l][:, c, :], param("b_mod", 2)[:, l, c:c + 1]
                    else:
                        dst, bias = mod2[l][:, c:c + 1], param("ada_b", 2)[:, l, c:c + 1]
                    nv = dst.shape[1]
                    a = nc.scalar.activation(dst, bank(name)[:, nv * j:nv * j + nv], ACT.Identity, bias=bias)
                a.then_inc(*scalar.does("emptied " + name, f"col {kind} {l}.{i}"))

            def mod_rows(at):
                if mod_at[at]:
                    for n in range(len(mod_at[at]) + 1):
                        mod_row(at, n)

            def modulated(name, groups, shift, at=None):
                more = len(mod_at[at]) + 1 if at else 0
                for k in range(KT):
                    if k < more:
                        mod_row(at, k)
                    act.wait_ge(*vector.did(f"normed {name}.{k}"))
                    for g in groups:
                        a = nc.scalar.activation(h_hi[:, k, S * g:S * g + S], dve_t[k % 4][:, S * g:S * g + S],
                                                 ACT.Identity, bias=shift(k, g))
                    a.then_inc(*scalar.does(f"h_hi {name}.{k}"))
                assert more <= KT

            act.wait_ge(params_landed, 16)
            act.wait_ge(tables_landed, 16)
            nc.scalar.activation(small[:, 32:56], param("c_vec"), ACT.Silu).then_inc(*scalar.does("csil"))
            at = PARAM_AT["decay"][0]
            both = params[:, at:at + 24]
            nc.scalar.activation(lp[0], both, ACT.Abs).then_inc(*scalar.does("lp abs"))
            act.wait_ge(*scalar.did("lp abs"))
            nc.scalar.activation(lp[1], lp[0], ACT.Exp, scale=-1.0).then_inc(*scalar.does("lp exp"))
            act.wait_ge(*vector.did("k_exps"))
            nc.scalar.activation(small[:, 80:112], small[:, 80:112], ACT.Exp).then_inc(*scalar.does("k_decay"))

            for l in range(2):
                nx = 2 * S if l == 0 else S
                groups = (0, 1) if l == 0 else (0,)
                if l == 0:
                    mod_rows("start")
                    act.wait_ge(x_landed, 32)
                first_units(f"sc_c {l}.0")
                square_all(f"n1 {l}", 2 * S, KT, lambda k: xT[:, k, :],
                           (lambda k: vector.did(f"x out 0.{k}")) if l else None)
                deviation(f"n1 {l}", 2 * S, D)
                modulated(f"n1 {l}", (0, 1), lambda k, g: mod1[l][:, k, g:g + 1], "n1 1" if l else None)
                for n in range(BT):
                    split_to(split_until(f"sc_c {l}.{n}"))
                    if n >= 2:
                        act.wait_ge(*vector.did(f"cx {l}.{n - 2}"))
                    evacuate(f"sc_c {l}.{n}", act_t[n % 2][:, 0:nx], also=[f"sc_c {l}.{n}"])
                for n in range(BT):
                    split_to(split_until(f"cf_g {l}.{n}"))
                    if n >= 2:
                        act.wait_ge(*vector.did(f"u {l}.{n - 2}"))
                    evacuate(f"cf_g {l}.{n}", act_t[2 + n % 2][:, 0:nx], ACT.Sigmoid, [f"cf_g {l}.{n}"])
                for n in range(BT):
                    projected(f"ret_q {l}.{n}", ret_q[:, n, 0:nx], also=[f"ret_q {l}.{n}"])
                for n in range(BT):
                    projected(f"ret_k {l}.{n}", ret_k[:, n, :], also=[f"ret_k {l}.{n}"], scale=K_SCALE)
                act.wait_ge(*vector.did(f"cx {l}.{BT - 1}"))

                def turned_v(n):
                    evacuate(f"turned ret_v {l}.{n}", ret_v[:, :, P * n:P * n + P], also=[f"ret_v {l}.{n}"])

                for n in range(BT):
                    projected(f"ret_v {l}.{n}", act_t[n % 2][:], also=[f"rows ret_v {l}.{n}"])
                    if n:
                        turned_v(n - 1)
                for n in range(BT):
                    projected(f"att_q {l}.{n}", att_q[:, n, 0:nx], also=[f"att_q {l}.{n}"])
                    if n == 0:
                        turned_v(BT - 1)
                projected(f"att_k {l}", att_k, also=[f"att_k {l}"])
                projected(f"att_v {l}", act_t[0][:], also=[f"rows att_v {l}"])
                split_to(split_until(f"sc_b {l}.0"))
                evacuate(f"turned att_v {l}", att_v, also=[f"att_v {l}"])
                for n in range(BT):
                    split_to(split_until(f"sc_z {l}.{n}"))
                    if n >= 2:
                        act.wait_ge(*vector.did(f"branch {l}.sc.{n - 2}"))
                    evacuate(f"sc_z {l}.{n}", act_t[n % 2][:, 0:nx], ACT.Silu, [f"sc_z {l}.{n}"])

                for hd in range(HEADS):
                    evacuate(f"state {l}.{hd}", state[:, hd, :, :], also=[f"state {l}.{hd}"])
                units = [(hd, g) for hd in range(HEADS) for g in groups]

                def ret_evacuate(hd, g):
                    evacuate(f"ro {l}.{hd}.{g}", ret_o[:, hd, S * g:S * g + S], also=[f"ret_o {l}.{hd}.{g}"])

                for n, (hd, g) in enumerate(units):
                    if g == 0:
                        if hd >= 2:
                            act.wait_ge(*vector.did(f"q_wt {l}.{hd - 2}"))
                        for d in range(2):
                            a = nc.scalar.activation(act_t[hd % 2][:, S * d:S * d + S],
                                                     table("q_pos")[:, S * d:S * d + S], ACT.Exp,
                                                     scale=log_g[:, l, d, hd:hd + 1])
                        a.then_inc(*scalar.does(f"q_dec {l}.{hd}"))
                        act.wait_ge(*vector.did(f"expo {l}.{hd}"))
                        nc.scalar.activation(act_t[2 + hd % 2][:], stat2[:], ACT.Exp)\
                            .then_inc(*scalar.does(f"decay {l}.{hd}"))
                    if n:
                        ret_evacuate(*units[n - 1])
                ret_evacuate(*units[-1])

                att = [(g, t, q) for g in groups for t in range(BT) for q in range(ST)]

                def att_turned(i):
                    nb = 4 - 2 * att[i][0]
                    for s in range(2):
                        if i >= 1:
                            act.wait_ge(*tensor.did(f"filled ao {l}.{i - 1}"))
                        evacuate(f"at {l}.{i}.{s}", act_t[2 + s][:, 0:P * nb], also=[f"att_t {l}.{i}.{s}"])

                def gate_of(i):
                    every = len(att) // (2 * BT)
                    n = i // every
                    return (("ret", "att")[n // BT], l, n % BT) if i % every == 0 and n < 2 * BT else None

                first_units(f"ret_z {l}.0")
                for i in range(len(att) + 1):
                    if i < len(att):
                        g, t, q = att[i]
                        n = 2 * S - S * g
                        o = 2 * (i % 2)
                        act.wait_ge(*vector.did(f"att_m {l}.{i}"))
                        for s in range(2):
                            if i >= 2:
                                act.wait_ge(*vector.did(f"att_p {l}.{i - 2}.{s}"))
                            name = f"as {l}.{i}.{s}"
                            nc.scalar.activation(exps[o + s][:, 0:n], bank(name)[:, 0:n], ACT.Exp, scale=ATT_SCALE,
                                                 bias=soft_m[:, o + s:o + s + 1], accum_out=soft_s[:, o + s:o + s + 1])\
                                .then_inc(*scalar.does(f"att_e {l}.{i}.{s}", "emptied " + name))
                        act.wait_ge(*vector.did(f"att_sk {l}.{i}"))
                        nc.scalar.activation(soft_e[:, o:o + 2], soft_d[:, o:o + 2], ACT.Exp)\
                            .then_inc(*scalar.does(f"att_se {l}.{i}"))
                    if gate_of(i):
                        a, _, n = gate_of(i)
                        projected(f"{a}_z {l}.{n}", z_sil[a][:, n, 0:nx], also=[f"{a}_z raw {l}.{n}"])
                    if i >= 1:
                        att_turned(i - 1)

                def gates(a, ns):
                    for n in ns:
                        projected(f"{a}_z {l}.{n}", z_sil[a][:, n, 0:nx], ACT.Silu, [f"{a}_z {l}.{n}"])

                split_to(split_until(f"att_z {l}.{BT - 1}"))
                for hd in range(HEADS):
                    act.wait_ge(*vector.did(f"gd {l}.{hd}"))
                    nc.scalar.activation(act_t[hd][:, 0:nx], ret_o[:, hd, 0:nx], ACT.Square)\
                        .then_inc(*scalar.does(f"sq gv {l}.{hd}"))
                gates("cf", range(2))
                for hd in range(HEADS):
                    name = f"gv {l}.{hd}"
                    evacuate(name, act_t[hd][:, 0:nx], ACT.Sqrt, [f"dev {name}"], scale=1.0 / P, bias=eps)
                for k in range(BT):
                    act.wait_ge(*vector.did(f"rinv gv {l}.{k}"))
                    act.wait_ge(*vector.did(f"ld {l}.{k}"))
                    nc.scalar.activation(act_t[k][:, 0:nx], f_br[:, k, 0:nx], ACT.Square)\
                        .then_inc(*scalar.does(f"sq lv {l}.{k}"))
                gates("cf", range(2, BT))
                deviation(f"lv {l}", nx, BW)
                for a in ("ret", "att"):
                    for n in range(BT):
                        act.wait_ge(*scalar.did(f"{a}_z raw {l}.{n}"))
                        nc.scalar.activation(z_sil[a][:, n, 0:nx], z_sil[a][:, n, 0:nx], ACT.Silu)\
                            .then_inc(*scalar.does(f"{a}_z {l}.{n}"))
                for n in range(BT):
                    act.wait_ge(*vector.did(f"ln {l}.{n}"))
                    nc.scalar.activation(f_br[:, n, 0:nx], f_br[:, n, 0:nx], ACT.Silu,
                                         scale=param("ln_w", 2)[:, l, n:n + 1], bias=param("ln_b", 2)[:, l, n:n + 1])\
                        .then_inc(*scalar.does(f"ln {l}.{n}"))
                m = 0
                for b in MERGE_ORDER:
                    for n in range(KT):
                        split_to(split_until(f"gate {l}.{b}.{n}"))
                        if m >= 4:
                            act.wait_ge(*vector.did(f"gated {l}.{m - 4}"))
                        evacuate(f"gate {l}.{b}.{n}", act_t[m % 4][:, 0:nx], ACT.Sigmoid, [f"gate {l}.{m}"])
                        m += 1
                        if n % 2:
                            mod_cols(merge_mods[l][m // 2 - 1])

            square_all("fin", S, KT, lambda k: xT[:, k, 0:S], lambda k: vector.did(f"x out 1.{k}"))
            deviation("fin", S, D)
            mod_rows("fin")

            def pre_norm(name, ready, l, q, first, at=None):
                first_units(first)
                square_all(name, S, KT, lambda k: xT[:, k, 0:S], ready)
                deviation(name, S, D)
                modulated(name, (0,), lambda k, g: mod2[l][:, 12 * q + k:12 * q + k + 1], at)

            def post(tag):
                for k in range(KT):
                    name = f"y {tag}.{k}"
                    act.wait_ge(*tensor.did("filled " + name))
                    nc.scalar.activation(yT[:, k, :], bank(name)[:, 0:S], ACT.Copy)
                    nc.scalar.activation(sq8[:, k, :], bank(name)[:, 0:S], ACT.Square)\
                        .then_inc(*scalar.does(name, "emptied " + name))
                deviation(f"ys {tag}", S, D)

            def ffn(l, ready):
                pre_norm(f"n3 {l}", ready, l, 2, f"ffg {l}.0", None if l else "n3 0")
                fw, fb = param("ff_w", 2, FF_K), param("ff_b", 2)
                m = 0
                for i in range(11):
                    for nm in ("ffg", "ffv"):
                        for j in range(2):
                            n = 2 * i + j
                            c = n + (FT if nm == "ffv" else 0)
                            name = f"{nm} {l}.{n}"
                            split_to(split_until(name))
                            if m >= 4:
                                act.wait_ge(*vector.did(f"ff_free {l}.{m - 4}"))
                            evacuate(name, act_t[m % 4][:, 0:S], ACT.Identity, [f"tap {name}"], last=False,
                                     scale=fw[:, l, FF_K - 1, c:c + 1], bias=fb[:, l, c:c + 1])
                            m += 1
                    for j in range(2):
                        n = 2 * i + j
                        act.wait_ge(*vector.did(f"conv ffg {l}.{n}"))
                        if n >= 4:
                            act.wait_ge(*vector.did(f"ff_act {l}.{n - 4}"))
                        nc.scalar.activation(act_t[n % 4][:, S:2 * S], dve_t[n % 4][:, 0:S], ACT.Gelu_apprx_tanh)\
                            .then_inc(*scalar.does(f"gelu {l}.{n}"))
                post(f"ffn {l}")

            pre_norm("n2 0", lambda k: vector.did(f"x fin.{k}"), 0, 0, "rgx 0", "n2 0")
            for n in range(KT):
                projected(f"rgx {n}", xb_pad[:, n, RG_K - 1:], also=[f"xb {n}"])
            for n in range(KT):
                projected(f"rgg {n}", gel[:, n, :], ACT.Gelu_apprx_tanh, [f"gel {n}"])
            for n in range(KT):
                evacuate(f"rga {n}", rr[:, n, :], ACT.Sigmoid, [f"rr {n}"], bias=param("rg_ba")[:, n:n + 1])
            for n in range(KT):
                evacuate(f"rgx2 {n}", ix[:, n, :], ACT.Sigmoid, [f"ig {n}"], bias=param("rg_bx")[:, n:n + 1])
            for n in range(KT):
                nc.scalar.activation(tt_[:, n, :], rr[:, n, :], ACT.Tanh, scale=lam8[:, n:n + 1])
                nc.scalar.activation(rr[:, n, :], rr[:, n, :], ACT.Exp, scale=lam8n[:, n:n + 1])\
                    .then_inc(*scalar.does(f"a {n}"))
            mod_rows("rg")
            for n in range(KT):
                act.wait_ge(*vector.did(f"one_a2 {n}"))
                nc.scalar.activation(tt_[:, n, :], tt_[:, n, :], ACT.Sqrt).then_inc(*scalar.does(f"mult {n}"))
            post("rg")
            mod_rows("post rg")
            ffn(0, lambda k: vector.did(f"x rg.{k}"))

            pre_norm("n2 1", lambda k: vector.did(f"x ffn 0.{k}"), 1, 0, "glaq 0")
            evacuate("gla z", zT[0:16, :], also=["zT"])
            for hd in range(GLA_H):
                evacuate(f"alpha {hd}", le[:, hd, :], ACT.Abs, [f"le {hd}"], last=False,
                         bias=param("gla_b")[:, hd:hd + 1])
            for hd in range(GLA_H):
                act.wait_ge(*scalar.did(f"le {hd}"))
                nc.scalar.activation(le[:, hd, :], le[:, hd, :], ACT.Exp, scale=-1.0)\
                    .then_inc(*scalar.does(f"le2 {hd}"))
            for hd in range(GLA_H):
                act.wait_ge(*scalar.did(f"le2 {hd}"))
                nc.scalar.activation(le[:, hd, :], le[:, hd, :], ACT.Ln, bias=ones[:, 0:1])\
                    .then_inc(*scalar.does(f"le3 {hd}"))
            for n in range(GLA_H):
                projected(f"glaq {n}", gq[:, n, :], also=[f"gq {n}"], scale=GLA_DK ** -0.5)
            for n in range(GLA_H):
                projected(f"glak {n}", gk[:, n, :], also=[f"gk {n}"])
            for i in range(8):
                projected(f"glav {i}", act_t[i % 2][:, 0:S], also=[f"rows glav {i}"])
                if i:
                    evacuate(f"turned glav {i - 1}", gv[:, :, P * i - P:P * i], also=[f"gv {i - 1}"])
                j = (7 + i) % 8
                act.wait_ge(*vector.did(f"ldiff {j}"))
                nc.scalar.activation(lv[:, j, :], lv[:, j, :], ACT.Exp, scale=1.0 / 16.0)\
                    .then_inc(*scalar.does(f"lexp {j}"))
            evacuate(f"turned glav {KT - 1}", gv[:, :, D - P:D], also=[f"gv {KT - 1}"])
            for n in range(GLA_H * ST):
                split_to(split_until(f"glar {n}"))
                if n % 2:
                    evacuate(f"cross {n // 2}", attT[:, n // 2, 0, P:S], also=[f"cross {n // 2}"])
                evacuate(f"glar {n}", r_sil[:, n, :], ACT.Silu, [f"r_sil {n}"])
            for n in range(KT):
                name = f"go {n}"
                act.wait_ge(*tensor.did("filled " + name))
                nc.scalar.activation(gla_o[:, n, :], bank(name)[:, 0:S], ACT.Copy)
                nc.scalar.activation(sq8[:, n, :], bank(name)[:, 0:S], ACT.Square)\
                    .then_inc(*scalar.does(name, "emptied " + name))
            for hd in range(GLA_H):
                if hd:
                    act.wait_ge(*vector.did(f"rinv gs {hd - 1}"))
                deviation(f"gs {hd}", S, 2 * P)
            post("gla")
            ffn(1, lambda k: vector.did(f"x gla.{k}"))

        @block.vector
        def _(dve):
            def step(ins, *names):
                ins.then_inc(*vector.does(*names))

            def after(name):
                dve.wait_ge(*vector.did(name))

            def filled(name):
                dve.wait_ge(*tensor.did("filled " + name))

            def settled():
                dve.wait_ge(vector.sem, vector.n)

            def inverse(name, n):
                settled()
                dve.wait_ge(*scalar.did(f"dev {name}"))
                step(nc.vector.reciprocal(stat2[:, 0:n], stat[:, 0:n]), f"rinv {name}")
                after(f"rinv {name}")

            def normed(name, groups, gain, shift):
                inverse(name, S * len(groups))
                for k in range(KT + 2):
                    if k < KT:
                        if k >= 4:
                            after(f"h_lo {name}.{k - 4}")
                        for g in groups:
                            sl = slice(S * g, S * g + S)
                            ins = nc.vector.scalar_tensor_tensor(dve_t[k % 4][:, sl], xT[:, k, sl], gain(k, g),
                                                                 stat2[:, sl], ALU.mult, ALU.mult)
                            step(ins, *([f"normed {name}.{k}"] if g == groups[-1] else []))
                    if k >= 2:
                        i = k - 2
                        dve.wait_ge(*scalar.did(f"h_hi {name}.{i}"))
                        after(f"normed {name}.{i}")
                        for g in groups:
                            sl = slice(S * g, S * g + S)
                            ins = nc.vector.scalar_tensor_tensor(h_lo[:, i, sl], dve_t[i % 4][:, sl], shift(i, g),
                                                                 h_hi[:, i, sl].bitcast(F32), ALU.add, ALU.subtract)
                            step(ins, *([f"h_lo {name}.{i}"] if g == groups[-1] else []))

            def normed2(name, l, q):
                normed(name, (0,), lambda k, g: gain2[l][:, q, k:k + 1],
                       lambda k, g: mod2[l][:, 12 * q + k:12 * q + k + 1])

            fed = dict(n=0)

            def split_to(last):
                while fed["n"] <= last:
                    u = fed["n"]
                    n, half, _ = w_units[u]
                    dve.wait_ge(*scalar.did(f"hi {u}"))
                    if u >= PARTS:
                        dve.wait_ge(*tensor.did(f"used unit {u - PARTS}"))
                    step(nc.vector.tensor_tensor(w_lo[u % PARTS], slot_of(n)[:, :, P * half:P * half + P],
                                                 w_hi[u % PARTS].bitcast(F32), ALU.subtract),
                         f"lo {u}", *(["used " + stream[n][0]] if half else []))
                    fed["n"] += 1

            def split_for(tile):
                split_to(split_until(tile))

            def first_units(tile):
                split_to(unit_of[tile] + 1)

            def bcast(ap, n):
                return ap.unsqueeze(2).broadcast_to([ap.shape[0], ap.shape[1], n])

            dve.wait_ge(params_landed, 16)
            dve.wait_ge(tables_landed, 16)
            at = PARAM_AT["decay"][0]
            both = params[:, at:at + 24]
            dve.wait_ge(*scalar.did("lp exp"))
            step(nc.vector.tensor_scalar(lp[0], lp[1], 2.0, None, ALU.add), "lp0")
            after("lp0")
            step(nc.vector.reciprocal(lp[2], lp[0]), "lp1")
            after("lp1")
            step(nc.vector.tensor_tensor(lp[1], lp[1], lp[2], ALU.mult), "lp2")
            after("lp2")
            step(nc.vector.tensor_tensor(lp[2], lp[1], lp[1], ALU.mult), "lp3")
            after("lp3")
            step(nc.vector.tensor_scalar(lp[3], lp[2], 1.0 / 15, 1.0 / 13, ALU.mult, ALU.add), "lp4")
            for i, d in enumerate((11, 9, 7, 5, 3, 1)):
                after(f"lp{4 + 2 * i}")
                step(nc.vector.tensor_tensor(lp[3], lp[3], lp[2], ALU.mult), f"lp{5 + 2 * i}")
                after(f"lp{5 + 2 * i}")
                step(nc.vector.tensor_scalar(lp[3], lp[3], 1.0 / d, None, ALU.add), f"lp{6 + 2 * i}")
            after("lp16")
            step(nc.vector.scalar_tensor_tensor(lp[3], lp[1], 2.0, lp[3], ALU.mult, ALU.mult), "lp17")
            step(nc.vector.tensor_scalar(lp[0], both, -1.0, 0.0, ALU.mult, ALU.max), "lp18")
            after("lp18")
            step(nc.vector.tensor_tensor(soft_p, lp[0], lp[3], ALU.add), "soft_p")
            after("soft_p")
            step(nc.vector.tensor_scalar(small[:, 224:240], soft_p[:, 0:16], -1.0, None, ALU.mult), "log_g")
            step(nc.vector.tensor_scalar(lam8, soft_p[:, 16:24], 8.0, None, ALU.mult), "lam8")
            step(nc.vector.tensor_scalar(lam8n, soft_p[:, 16:24], -8.0, None, ALU.mult), "lam8n")
            step(nc.vector.tensor_scalar(small[:, 112:128], param("sink"), -1.0, None, ALU.mult), "nsink")
            after("log_g")
            for l in range(2):
                for d in range(2):
                    for t in range(ST):
                        ins = nc.vector.tensor_scalar(k_decay[:, l, d, t, :], log_g[:, l, d, :],
                                                      table("k_pos")[:, 2 * d + t:2 * d + t + 1], None, ALU.mult)
                        step(ins, *(["k_exps"] if (l, d, t) == (1, 1, 1) else []))

            def mod_accumulate(m):
                kind, l, i = m
                name = f"{kind} {l}.{i}"
                n = slab_of["w " + name]
                w, acc = slot_of(n), acc_of(m)
                dve.wait_ge(slab_landed[n % RING], 16 * (n // RING + 1))
                at = merge_mods[0].index(m) if m in merge_mods[0] else merge_mods[1].index(m)
                if at >= 2:
                    ll = 0 if m in merge_mods[0] else 1
                    filled("sum %s %d.%d" % merge_mods[ll][at - 2])
                todo = [(k, c, c) for k in range(KT) for c in range(2)] if kind == "mod" else \
                    [(k, k % 2, 2) for k in range(KT)]
                before = {}
                for k, c, v in todo:
                    dst, src, scale = acc[:, 2 * P * c:2 * P * c + 2 * P], w[:, k, :], csil[:, k, v:v + 1]
                    done = [f"acc {name}.{k}.{c}"]
                    if (k, c, v) == todo[-1]:
                        done += ["acc " + name, "used w " + name]
                    if c in before:
                        after(before[c])
                        step(nc.vector.scalar_tensor_tensor(dst, src, scale, dst, ALU.mult, ALU.add), *done)
                    else:
                        step(nc.vector.tensor_scalar(dst, src, scale, None, ALU.mult), *done)
                    before[c] = done[0]

            def modulation1(l):
                dve.wait_ge(*scalar.did(f"col mod {l}.7"))
                step(nc.vector.scalar_tensor_tensor(gain1[l], mod1[l][:, 8:16, :], 1.0,
                                                    bcast(param("norm_w", 2)[:, l, :], 2), ALU.add, ALU.mult),
                     f"gain1 {l}")

            def modulation2(l):
                dve.wait_ge(*scalar.did(f"col ada {l}.23"))
                g = param("norm_g", 2, 4)
                for q in range(2):
                    c = 24 * q
                    step(nc.vector.scalar_tensor_tensor(gain2[l][:, 2 * q, :], mod2[l][:, c + 8:c + 16], 1.0,
                                                        g[:, l, 2 * q, :], ALU.add, ALU.mult))
                    step(nc.vector.tensor_tensor(gain2[l][:, 2 * q + 1, :], mod2[l][:, c + 16:c + 24],
                                                 g[:, l, 2 * q + 1, :], ALU.mult), *([f"gain2 {l}"] if q else []))

            dve.wait_ge(x_landed, 32)
            for l in range(2):
                nx = 2 * S if l == 0 else S
                groups = (0, 1) if l == 0 else (0,)
                ng = len(groups)
                settled()
                first_units(f"sc_c {l}.0")
                modulation1(l)
                step(nc.vector.memset(cx[:, :, 0:ng, 0:1], 0.0), f"cx z0 {l}")
                step(nc.vector.memset(cx[:, :, 0:ng, S + 1:S + 2], 0.0), f"cx z1 {l}")
                after(f"gain1 {l}")
                normed(f"n1 {l}", (0, 1), lambda k, g: gain1[l][:, k, g:g + 1], lambda k, g: mod1[l][:, k, g:g + 1])

                def grouped(ap):
                    return ap.rearrange("p (g s) -> p g s", g=ng)

                settled()
                for n in range(BT):
                    split_for(f"sc_x {l}.{n}")
                    dve.wait_ge(*scalar.did(f"sc_c {l}.{n}"))
                    name = f"sc_x {l}.{n}"
                    filled(name)
                    step(nc.vector.tensor_tensor(cx[:, n, 0:ng, 1:S + 1], grouped(bank(name)[:, 0:nx]),
                                                 grouped(act_t[n % 2][:, 0:nx]), ALU.mult),
                         f"cx {l}.{n}", "emptied " + name)
                sw = param("sc_w", 2, SC_K)
                for k in range(SC_K):
                    for n in range(BT):
                        src, dst = cx[:, n, 0:ng, k:k + S], grouped(s_br[:, n, 0:nx])
                        if k == 0:
                            after(f"cx {l}.{n}")
                            step(nc.vector.tensor_scalar(dst, src, sw[:, l, k, n:n + 1], None, ALU.mult),
                                 f"sc {l}.{n}.{k}")
                        else:
                            after(f"sc {l}.{n}.{k - 1}")
                            step(nc.vector.scalar_tensor_tensor(dst, src, sw[:, l, k, n:n + 1], dst, ALU.mult, ALU.add),
                                 f"sc {l}.{n}.{k}")
                settled()
                step(nc.vector.memset(u_pad[:, :, 0:ng, 0:PAD], 0.0), f"u z0 {l}")
                step(nc.vector.memset(u_pad[:, :, 0:ng, PAD + S:], 0.0), f"u z1 {l}")
                for n in range(BT):
                    split_for(f"cf_a {l}.{n}")
                    dve.wait_ge(*scalar.did(f"cf_g {l}.{n}"))
                    name = f"cf_a {l}.{n}"
                    filled(name)
                    step(nc.vector.tensor_tensor(u_pad[:, n, 0:ng, PAD:PAD + S], grouped(bank(name)[:, 0:nx]),
                                                 grouped(act_t[2 + n % 2][:, 0:nx]), ALU.mult),
                         f"u {l}.{n}", "emptied " + name)
                cw, cb = param("cf_w", 2, CF_K), param("cf_b", 2)
                after(f"u z1 {l}")
                for k in range(CF_K):
                    for n in range(BT):
                        if (BT * k + n) % 6 == 5:
                            split_to(min(fed["n"], unit_of[f"sc_z {l}.0"]))
                        src, dst = u_pad[:, n, 0:ng, k:k + S], grouped(f_br[:, n, 0:nx])
                        name = f"cf {l}.{n}.{k}" if k < CF_K - 1 else f"conv {l}.{n}"
                        if k == 0:
                            after(f"u {l}.{n}")
                            step(nc.vector.tensor_scalar(dst, src, cw[:, l, k, n:n + 1], cb[:, l, n:n + 1],
                                                         ALU.mult, ALU.add), name)
                        else:
                            after(f"cf {l}.{n}.{k - 1}")
                            step(nc.vector.scalar_tensor_tensor(dst, src, cw[:, l, k, n:n + 1], dst, ALU.mult, ALU.add),
                                 name)
                settled()
                for n in range(BT):
                    name = f"sc_b {l}.{n}"
                    split_for(f"sc_z {l}.{n}")
                    filled(name)
                    step(nc.vector.tensor_tensor(s_br[:, n, 0:nx], bank(name)[:, 0:nx], s_br[:, n, 0:nx], ALU.mult),
                         f"sb {l}.{n}", "emptied " + name)
                    dve.wait_ge(*scalar.did(f"sc_z {l}.{n}"))
                    after(f"sb {l}.{n}")
                    step(nc.vector.tensor_tensor(s_br[:, n, 0:nx], s_br[:, n, 0:nx], act_t[n % 2][:, 0:nx], ALU.mult),
                         f"branch {l}.sc.{n}")
                settled()
                for t in range(BT + 1):
                    q = att_q[:, t, 0:S] if t < BT else att_k[:, 0:S]
                    name = f"turn {l}.{t}"
                    filled(name)
                    if t >= 2:
                        after(f"roped {l}.{t - 2}")
                    step(nc.vector.tensor_tensor(dve_t[t % 2][:, 0:S], bank(name)[:, 0:S], table("sin"), ALU.mult),
                         f"rope0 {l}.{t}", "emptied " + name)
                    step(nc.vector.tensor_tensor(q, q, table("cos"), ALU.mult), f"rope1 {l}.{t}")
                    after(f"rope1 {l}.{t}")
                    step(nc.vector.tensor_tensor(q, q, dve_t[t % 2][:, 0:S], ALU.add),
                         f"roped {l}.{t}", *([f"att_q roped {l}.{t}"] if t < BT else []))
                after(f"roped {l}.{BT}")
                step(nc.vector.tensor_copy(att_ks[0:64, :], att_k[64:P, :]))
                step(nc.vector.tensor_copy(att_ks[64:P, :], att_k[0:64, :]), f"att_ks {l}")

                settled()
                dve.wait_ge(*scalar.did("k_decay"))
                for t in range(ST):
                    name = f"kT {l}.{t}"
                    filled(name)
                    for d in range(2):
                        step(nc.vector.tensor_tensor(k_wt[d][:, t, :, :], bank(name)[:].rearrange("p (h n) -> p h n", h=HEADS),
                                                     bcast(k_decay[:, l, d, t, :], P), ALU.mult),
                             f"k_wt {l}.{t}.{d}", *(["emptied " + name] if d else []))
                units = [(hd, g) for hd in range(HEADS) for g in groups]
                for n, (hd, g) in enumerate(units):
                    if g == 0:
                        if hd:
                            dve.wait_ge(*scalar.did(f"decay {l}.{hd - 1}"))
                        step(nc.vector.tensor_scalar(stat2[:], table("ahead"), log_g[:, l, 1, hd:hd + 1], None, ALU.mult),
                             f"expo0 {l}.{hd}")
                        after(f"expo0 {l}.{hd}")
                        step(nc.vector.scalar_tensor_tensor(stat2[:], table("behind"), log_g[:, l, 0, hd:hd + 1], stat2[:],
                                                            ALU.mult, ALU.add), f"expo {l}.{hd}")
                        dve.wait_ge(*scalar.did(f"q_dec {l}.{hd}"))
                        if hd >= 2:
                            dve.wait_ge(*tensor.did(f"filled ro {l}.{hd - 2}.0"))
                        dve.wait_ge(*scalar.did(f"ret_q {l}.{hd}"))
                        for d in range(2):
                            ins = nc.vector.tensor_tensor(dve_t[hd % 2][:, S * d:S * d + S], ret_q[:, hd, 0:S],
                                                          act_t[hd % 2][:, S * d:S * d + S], ALU.mult)
                            step(ins, *([f"q_wt {l}.{hd}"] if d else []))
                        dve.wait_ge(*scalar.did(f"decay {l}.{hd}"))
                    name = f"rs {l}.{hd}.{g}"
                    filled(name)
                    if n >= 2:
                        dve.wait_ge(*tensor.did("filled ro %d.%d.%d" % (l, *units[n - 2])))
                    step(nc.vector.tensor_tensor(dve_t[2 + n % 2][:], bank(name)[:], act_t[2 + hd % 2][:], ALU.mult),
                         f"ret_p {l}.{hd}.{g}", "emptied " + name)

                settled()
                att = [(g, t, q) for g in groups for t in range(BT) for q in range(ST)]

                def att_max(i):
                    g, t, q = att[i]
                    o = 2 * (i % 2)
                    for s in range(2):
                        name = f"as {l}.{i}.{s}"
                        filled(name)
                        if g == 0:
                            c = P * (1 - q)
                            step(nc.vector.tensor_tensor(bank(name)[:, c:c + P], bank(name)[:, c:c + P],
                                                         table("band")[:, P * q:P * q + P], ALU.add), f"band {l}.{i}.{s}")
                    for s in range(2):
                        if g == 0:
                            after(f"band {l}.{i}.{s}")
                        step(nc.vector.tensor_reduce(soft_m[:, 4 + s:5 + s], bank(f"as {l}.{i}.{s}")[:, 0:2 * S - S * g],
                                                     AX_X, ALU.max), f"rowmax {l}.{i}.{s}")
                    after(f"rowmax {l}.{i}.1")
                    if i >= 2:
                        dve.wait_ge(*scalar.did(f"att_se {l}.{i - 2}"))
                    step(nc.vector.scalar_tensor_tensor(soft_m[:, o:o + 2], soft_m[:, 4:6], -ATT_SCALE,
                                                        nsink[:, l, 2 * t:2 * t + 2], ALU.mult, ALU.min), f"att_m {l}.{i}")
                    after(f"att_m {l}.{i}")
                    step(nc.vector.tensor_tensor(soft_d[:, o:o + 2], soft_m[:, o:o + 2],
                                                 param("sink", 2)[:, l, 2 * t:2 * t + 2], ALU.add), f"att_sk {l}.{i}")

                def att_weights(i):
                    g, t, q = att[i]
                    o = 2 * (i % 2)
                    n = 2 * S - S * g
                    dve.wait_ge(*scalar.did(f"att_se {l}.{i}"))
                    step(nc.vector.tensor_tensor(soft_s[:, 4:6], soft_s[:, o:o + 2], soft_e[:, o:o + 2], ALU.add),
                         f"att_d0 {l}.{i}")
                    after(f"att_d0 {l}.{i}")
                    if i:
                        after(f"att_p {l}.{i - 1}.1")
                    step(nc.vector.reciprocal(soft_e[:, 4:6], soft_s[:, 4:6]), f"att_d1 {l}.{i}")
                    after(f"att_d1 {l}.{i}")
                    for s in range(2):
                        if i >= 2:
                            dve.wait_ge(*tensor.did(f"filled at {l}.{i - 2}.{s}"))
                        step(nc.vector.tensor_scalar(dve_t[2 * (i % 2) + s][:, 0:n], exps[o + s][:, 0:n],
                                                     soft_e[:, 4 + s:5 + s], None, ALU.mult), f"att_p {l}.{i}.{s}")

                def att_store(i):
                    g, t, q = att[i]
                    name = f"ao {l}.{i}"
                    filled(name)
                    step(nc.vector.tensor_copy(att_o[:, t, S * g + P * q:S * g + P * q + P], bank(name)[:, 0:P]),
                         f"att_o {l}.{i}", "emptied " + name)

                dve.wait_ge(*tensor.did("filled ro %d.%d.%d" % (l, *units[-1])))
                first_units(f"ret_z {l}.0")
                every = len(att) // (2 * BT)
                for i in range(len(att) + 3):
                    if i < len(att):
                        att_max(i)
                        if i % every == 0:
                            n = i // every
                            split_for("%s_z %d.%d" % (("ret", "att")[n // BT], l, n % BT))
                    if 1 <= i <= len(att):
                        att_weights(i - 1)
                    if i >= 3:
                        att_store(i - 3)

                settled()
                split_for(f"att_z {l}.{BT - 1}")
                for hd in range(HEADS):
                    name = f"gm {l}.{hd}"
                    filled(name)
                    step(nc.vector.scalar_tensor_tensor(ret_o[:, hd, 0:nx], bank(name)[:, 0:nx], -1.0 / P,
                                                        ret_o[:, hd, 0:nx], ALU.mult, ALU.add),
                         f"gd {l}.{hd}", "emptied " + name)
                name = f"lm {l}"
                filled(name)
                for t in range(BT):
                    step(nc.vector.scalar_tensor_tensor(f_br[:, t, 0:nx], bank(name)[:, 0:nx], -1.0 / BW,
                                                        f_br[:, t, 0:nx], ALU.mult, ALU.add),
                         f"ld {l}.{t}", *(["emptied " + name] if t == BT - 1 else []))

                def gate_branch(a, n):
                    dve.wait_ge(*scalar.did(f"{a}_z {l}.{n}"))
                    step(nc.vector.tensor_tensor(branch[a][:, n, 0:nx], branch[a][:, n, 0:nx], z_sil[a][:, n, 0:nx],
                                                 ALU.mult), f"branch {l}.{a}.{n}")

                split_for(f"cf_z {l}.0")
                for hd in range(HEADS):
                    dve.wait_ge(*scalar.did(f"dev gv {l}.{hd}"))
                    step(nc.vector.reciprocal(dve_t[hd][:, 0:nx], act_t[hd][:, 0:nx]), f"rinv gv {l}.{hd}")
                split_for(f"cf_z {l}.1")
                for hd in range(HEADS):
                    after(f"rinv gv {l}.{hd}")
                    step(nc.vector.scalar_tensor_tensor(ret_o[:, hd, 0:nx], ret_o[:, hd, 0:nx],
                                                        param("gn_w", 2)[:, l, hd:hd + 1], dve_t[hd][:, 0:nx],
                                                        ALU.mult, ALU.mult), f"gn {l}.{hd}")
                for n in range(2, BT):
                    split_for(f"cf_z {l}.{n}")
                inverse(f"lv {l}", nx)
                for t in range(BT):
                    step(nc.vector.tensor_tensor(f_br[:, t, 0:nx], f_br[:, t, 0:nx], stat2[:, 0:nx], ALU.mult),
                         f"ln {l}.{t}")
                for n in range(BT):
                    after(f"gn {l}.{n}")
                    gate_branch("ret", n)
                for n in range(BT):
                    gate_branch("att", n)
                for n in range(BT):
                    dve.wait_ge(*scalar.did(f"ln {l}.{n}"))
                    gate_branch("cf", n)
                settled()
                m = 0
                for b in MERGE_ORDER:
                    for n in range(KT):
                        if n % 2 == 0:
                            mod_accumulate(merge_mods[l][m // 2])
                        split_for(f"gate {l}.{b}.{n}")
                        dve.wait_ge(*scalar.did(f"gate {l}.{m}"))
                        name = f"br {l}.{b}.{n}"
                        filled(name)
                        if b == MERGE_ORDER[0]:
                            step(nc.vector.tensor_tensor(merged[:, n, 0:nx], bank(name)[:, 0:nx], act_t[m % 4][:, 0:nx],
                                                         ALU.mult), f"gated {l}.{m}", f"merged {l}.{b}.{n}", "emptied " + name)
                        else:
                            if m >= KT + 4:
                                after(f"added {l}.{m - 4}")
                            step(nc.vector.tensor_tensor(dve_t[m % 4][:, 0:nx], bank(name)[:, 0:nx], act_t[m % 4][:, 0:nx],
                                                         ALU.mult), f"gated {l}.{m}", "emptied " + name)
                            after(f"gated {l}.{m}")
                            after(f"merged {l}.{MERGE_ORDER[MERGE_ORDER.index(b) - 1]}.{n}")
                            step(nc.vector.tensor_tensor(merged[:, n, 0:nx], merged[:, n, 0:nx], dve_t[m % 4][:, 0:nx],
                                                         ALU.add), f"merged {l}.{b}.{n}", f"added {l}.{m}")
                        m += 1
                dve.wait_ge(*scalar.did(f"col mod {l}.11"))
                for n in range(KT):
                    name = f"out {l}.{n}"
                    filled(name)
                    for g in groups:
                        sl = slice(S * g, S * g + S)
                        step(nc.vector.scalar_tensor_tensor(xT[:, n, sl], bank(name)[:, sl], mod1[l][:, 16 + n, g:g + 1],
                                                            xT[:, n, sl], ALU.mult, ALU.add),
                             *([f"x out {l}.{n}", "emptied " + name] if g == groups[-1] else []))

            inverse("fin", S)
            for k in range(KT):
                step(nc.vector.scalar_tensor_tensor(xT[:, k, 0:S], xT[:, k, 0:S], param("fin_w")[:, k:k + 1],
                                                    stat2[:, 0:S], ALU.mult, ALU.mult), f"x fin.{k}")

            def post(tag, l, q):
                inverse(f"ys {tag}", S)
                for k in range(KT):
                    step(nc.vector.scalar_tensor_tensor(yT[:, k, :], yT[:, k, :], gain2[l][:, q, k:k + 1], stat2[:, 0:S],
                                                        ALU.mult, ALU.mult), f"yn {tag}.{k}")
                for k in range(KT):
                    after(f"yn {tag}.{k}")
                    step(nc.vector.tensor_tensor(xT[:, k, 0:S], xT[:, k, 0:S], yT[:, k, :], ALU.add), f"x {tag}.{k}")

            def ffn(l):
                first_units(f"ffg {l}.0")
                normed2(f"n3 {l}", l, 2)
                settled()
                fw = param("ff_w", 2, FF_K)
                m = 0
                for i in range(11):
                    for nm in ("ffg", "ffv"):
                        for j in range(2):
                            n = 2 * i + j
                            c = n + (FT if nm == "ffv" else 0)
                            name = f"{nm} {l}.{n}"
                            split_for(name)
                            dve.wait_ge(*scalar.did(f"tap {name}"))
                            src, acc = bank(name), act_t[m % 4]
                            dst = dve_t[n % 4][:, 0:S] if nm == "ffg" else dve_t[n % 4][:, S:2 * S]
                            step(nc.vector.scalar_tensor_tensor(acc[:, 1:S], src[:, 0:S - 1], fw[:, l, 1, c:c + 1],
                                                                acc[:, 1:S], ALU.mult, ALU.add), f"tap1 {name}")
                            after(f"tap1 {name}")
                            if n >= 4 and nm == "ffv":
                                after(f"ff_act {l}.{n - 4}")
                            step(nc.vector.tensor_copy(dst[:, 0:2], acc[:, 0:2]))
                            step(nc.vector.scalar_tensor_tensor(dst[:, 2:S], src[:, 0:S - 2], fw[:, l, 0, c:c + 1],
                                                                acc[:, 2:S], ALU.mult, ALU.add),
                                 f"conv {name}", f"ff_free {l}.{m}", "emptied " + name)
                            m += 1
                    for j in range(2):
                        n = 2 * i + j
                        dve.wait_ge(*scalar.did(f"gelu {l}.{n}"))
                        after(f"conv ffv {l}.{n}")
                        step(nc.vector.tensor_tensor(ff_act[:, n, :], act_t[n % 4][:, S:2 * S], dve_t[n % 4][:, S:2 * S],
                                                     ALU.mult), f"ff_act {l}.{n}")
                post(f"ffn {l}", l, 3)

            settled()
            first_units("rgx 0")
            modulation2(0)
            settled()
            normed2("n2 0", 0, 0)
            step(nc.vector.memset(xb_pad[:, :, 0:RG_K - 1], 0.0), "xb z")
            after("xb z")
            rw, rb = param("rg_w", RG_K), param("rg_b")
            for n in range(KT):
                split_for(f"rgx {n}")
                dve.wait_ge(*scalar.did(f"xb {n}"))
                for k in range(RG_K):
                    src = xb_pad[:, n, k:k + S]
                    if k == 0:
                        step(nc.vector.tensor_scalar(xc[:, n, :], src, rw[:, k, n:n + 1], rb[:, n:n + 1],
                                                     ALU.mult, ALU.add), f"xc0 {n}")
                    else:
                        after(f"xc{k - 1} {n}")
                        step(nc.vector.scalar_tensor_tensor(xc[:, n, :], src, rw[:, k, n:n + 1], xc[:, n, :],
                                                            ALU.mult, ALU.add),
                             f"xc{k} {n}", *([f"xc {n}"] if k == RG_K - 1 else []))
            for n in range(KT):
                split_for(f"rgg {n}")
            for n in range(KT):
                dve.wait_ge(*scalar.did(f"ig {n}"))
                step(nc.vector.tensor_tensor(ix[:, n, :], ix[:, n, :], xc[:, n, :], ALU.mult), f"ix {n}")
            for n in range(KT):
                dve.wait_ge(*scalar.did(f"a {n}"))
                step(nc.vector.tensor_tensor(a2[:, n, :], rr[:, n, :], rr[:, n, :], ALU.mult), f"a2 {n}")
            for n in range(KT):
                after(f"a2 {n}")
                step(nc.vector.scalar_tensor_tensor(tt_[:, n, :], a2[:, n, :], 1.0, tt_[:, n, :], ALU.add, ALU.mult),
                     f"one_a2 {n}")
            for n in range(KT):
                dve.wait_ge(*scalar.did(f"mult {n}"))
                after(f"ix {n}")
                step(nc.vector.tensor_tensor(ix[:, n, :], ix[:, n, :], tt_[:, n, :], ALU.mult), f"u_rg {n}")
            for n in range(KT):
                after(f"u_rg {n}")
                step(nc.vector.tensor_tensor_scan(a2[:, n, :], rr[:, n, :], ix[:, n, :], 0.0, ALU.mult, ALU.add), f"hs {n}")
            dve.wait_ge(*tensor.did(f"filled rgx2 {KT - 1}"))
            for n in range(KT):
                after(f"hs {n}")
                dve.wait_ge(*scalar.did(f"gel {n}"))
                step(nc.vector.tensor_tensor(xc[:, n, :], a2[:, n, :], gel[:, n, :], ALU.mult), f"rg_y {n}")
            post("rg", 0, 1)
            ffn(0)
            modulation2(1)
            settled()

            settled()
            first_units("glaq 0")
            step(nc.vector.memset(scan_one, 1.0), "scan_one")
            normed2("n2 1", 1, 0)
            split_for("glaq 0")
            for hd in range(GLA_H):
                name = f"alpha {hd}"
                dve.wait_ge(*scalar.did(f"le {hd}"))
                step(nc.vector.tensor_scalar(la[:, hd, :], bank(name)[:, 0:S], param("gla_b")[:, hd:hd + 1], 0.0,
                                             ALU.add, ALU.min), f"la {hd}", "emptied " + name)
            for hd in range(GLA_H):
                dve.wait_ge(*scalar.did(f"le3 {hd}"))
                after(f"la {hd}")
                step(nc.vector.tensor_tensor(la[:, hd, :], la[:, hd, :], le[:, hd, :], ALU.subtract), f"lb {hd}")
            for hd in range(GLA_H):
                after(f"lb {hd}")
                step(nc.vector.tensor_tensor_scan(gg[:, hd, :], scan_one, la[:, hd, :], 0.0, ALU.mult, ALU.add), f"gg {hd}")
            after(f"gg {GLA_H - 1}")
            flat = carve(8192 + 4 * 1024, GLA_H * S)
            half_of = (1, 2, 4, 8, 16, 32, 64, 128)
            level_order = [(7 + i) % 8 for i in range(8)]

            def halves(ap, s):
                return ap.rearrange("p (b two s) -> p b two s", two=2, s=s)

            for n, i in enumerate(level_order):
                split_to(unit_of["glaq 0"] + 3 + n)
                s = half_of[i]
                g, d = halves(flat, s), halves(lv[:, i, :], s)
                nb = g.shape[1]
                ref = g[:, :, 0, s - 1:s].broadcast_to([P, nb, s])
                step(nc.vector.tensor_tensor(d[:, :, 1, :], g[:, :, 1, :], ref, ALU.subtract))
                step(nc.vector.tensor_tensor(d[:, :, 0, :], ref, g[:, :, 0, :], ALU.subtract), f"ldiff {i}")
            qf, kf = carve(8192, GLA_H * S), carve(8192 + 1024, GLA_H * S)
            dve.wait_ge(*scalar.did(f"gk {GLA_H - 1}"))
            for n, i in enumerate(level_order):
                split_to(min(unit_of["glaq 0"] + 11 + n, unit_of["glar 1"]))
                s = half_of[i]
                d = halves(lv[:, i, :], s)
                dve.wait_ge(*scalar.did(f"lexp {i}"))
                step(nc.vector.tensor_tensor(d[:, :, 1, :], d[:, :, 1, :], halves(qf, s)[:, :, 1, :], ALU.mult))
                step(nc.vector.tensor_tensor(d[:, :, 0, :], d[:, :, 0, :], halves(kf, s)[:, :, 0, :], ALU.mult), f"lv {i}")
            lpf = carve(10240, 8 * P)
            dve.wait_ge(late_landed, 32)
            for n in range(GLA_H * ST):
                hd, t = n // ST, n % ST
                split_for(f"glar {n}")
                for half in range(2):
                    name = f"lev {n}.{half}"
                    filled(name)
                    if n:
                        after(f"attT {n - 1}")
                    step(nc.vector.tensor_tensor(lpf[:, 512 * half:512 * half + 512], bank(name)[:],
                                                 level[:, 512 * half:512 * half + 512], ALU.mult),
                         f"lpr {n}.{half}", "emptied " + name)
                after(f"lpr {n}.1")
                step(nc.vector.tensor_reduce(attT[:, hd, t, P * t:P * t + P], lprod.rearrange("p l i -> p i l"),
                                             AX_X, ALU.add), f"attT {n}")
            for hd in range(GLA_H):
                inverse(f"gs {hd}", S)
                for e in range(2):
                    n = 2 * hd + e
                    step(nc.vector.scalar_tensor_tensor(gla_o[:, n, :], gla_o[:, n, :], param("gla_g")[:, e:e + 1],
                                                        stat2[:, 0:S], ALU.mult, ALU.mult), f"gon {n}")
                for e in range(2):
                    n = 2 * hd + e
                    dve.wait_ge(*scalar.did(f"r_sil {n}"))
                    after(f"gon {n}")
                    step(nc.vector.tensor_tensor(gla_o[:, n, :], gla_o[:, n, :], r_sil[:, n, :], ALU.mult), f"gla_y {n}")
            post("gla", 1, 1)
            ffn(1)

    return dict(tensor=tensor.now, vector=vector.now, scalar=scalar.now)


WEIGHTS = ("w_mod", "w_in", "w_branch", "w_out", "ada_w_2", "ffn_w_up_2", "ffn_w_down_2", "rg_w_in_2", "rg_wa_2",
           "rg_wx_2", "rg_w_out_2", "gla_w_in_2", "gla_w_out_2", "gla_w_alpha_2")


def shape_tables():
    p, i = np.arange(P), np.arange(S)
    out = {"ident": np.eye(P), "ones": np.ones((P, P)), "eps": np.full((P, 1), EPS)}
    turn = np.zeros((P, P))
    half = ATT_DH // 2
    for m in range(P):
        r = m % ATT_DH
        turn[m + half if r < half else m - half, m] = -1.0 if r < half else 1.0
    out["turn"] = turn
    freqs = ATT_DH // 4
    inv = (np.float32(10000.0) ** (-np.arange(freqs, dtype=np.float32) / np.float32(freqs))).astype(np.float32)
    row, col = (i // 64).astype(np.float32), (i % 64).astype(np.float32)
    angle = np.concatenate([inv[:, None] * row[None], inv[:, None] * col[None]], 0).astype(np.float32)
    angle = np.tile(angle, (P // half, 1))
    out["cos"], out["sin"] = np.cos(angle), np.sin(angle)
    j = p[:, None, None] + P * np.arange(ST)[None, :, None]
    dist = i[None, None, :] - j
    out["behind"] = np.maximum(dist, 0).reshape(P, -1)
    out["ahead"] = np.maximum(-dist, 0).reshape(P, -1)
    out["q_pos"] = np.tile(np.concatenate([i + 1, S - i])[None], (P, 1))
    pos = p[:, None] + P * np.arange(ST)[None]
    out["k_pos"] = np.concatenate([S - 1 - pos, pos], 1)
    q, k = p[:, None], p[None, :]
    out["band"] = np.concatenate([np.where(k <= q, 0.0, -1e30), np.where(k >= q, 0.0, -1e30)], 1)
    masks = []
    for s in LEVELS:
        a, b = p[:, None], p[None, :]
        masks.append((a // (2 * s) == b // (2 * s)) & (a % (2 * s) < s) & (b % (2 * s) >= s))
    masks.append(np.eye(P, dtype=bool))
    level = np.concatenate([m.astype(np.float32) for m in masks], 1)
    return np.concatenate([out[n].reshape(P, -1).astype(np.float32) for n in TABLES], 1), level


def pack_params(a):
    def cols(v):
        v = np.asarray(v)
        v = v.reshape(v.shape[:-1] + (v.shape[-1] // P, P))
        return np.moveaxis(v, -1, 0).reshape(P, -1)

    def rows(v):
        return np.broadcast_to(np.asarray(v).reshape(1, -1), (P, np.asarray(v).size))

    c_vec = np.stack([cols(a["c"][0]), cols(a["c_ctx"]), cols(a["c_2"][0])], 2).reshape(P, -1)
    wz = np.asarray(a["gla_w_in_2"])[0][:, 3072:3088].reshape(KT, P, 16).transpose(1, 0, 2).reshape(P, -1)
    parts = dict(norm_w=cols(a["norm_w"]), gn_w=cols(a["ret_gn_w"]), sc_w=cols(a["sc_conv_w"]), cf_w=cols(a["cf_conv_w"]),
                 cf_b=cols(a["cf_conv_b"]), ln_w=cols(a["cf_ln_w"]), ln_b=cols(a["cf_ln_b"]), sink=rows(a["att_sink"]),
                 b_mod=cols(a["b_mod"]), fin_w=cols(a["final_norm_w"]), decay=rows(a["ret_decay"]),
                 lam=cols(a["rg_lambda_2"]), c_vec=c_vec, ada_b=cols(a["ada_b_2"]), norm_g=cols(a["norm_g_2"]),
                 ff_w=cols(a["ffn_conv_w_2"]), ff_b=cols(a["ffn_conv_b_2"]), rg_w=cols(a["rg_conv_w_2"]),
                 rg_b=cols(a["rg_conv_b_2"]), rg_ba=cols(a["rg_ba_2"]), rg_bx=cols(a["rg_bx_2"]),
                 gla_b=cols(a["gla_b_alpha_2"]), gla_g=cols(a["gla_norm_g_2"]), gla_z=wz)
    for n, v in parts.items():
        assert v.shape == (P, PARAMS[n]), (n, v.shape)
    return np.ascontiguousarray(np.concatenate([parts[n] for n in PARAMS], 1))


def kernel(**inputs):
    import concourse.bacc as _bacc
    from concourse.bass_utils import run_bass_kernel_spmd as _run

    arrays = {n: np.ascontiguousarray(np.asarray(inputs[n])) for n in WEIGHTS}
    arrays["x"] = np.ascontiguousarray(np.asarray(inputs["x"])[0].T)
    arrays["ctx"] = np.ascontiguousarray(np.asarray(inputs["ctx"])[0].T)
    arrays["params"] = pack_params(inputs)
    arrays["tables"], arrays["level"] = shape_tables()

    def build(counts):
        nc = _bacc.Bacc("TRN2", target_bir_lowering=False, num_devices=1)
        io = {n: nc.dram_tensor(f"in_{n}", a.shape, F32, kind="ExternalInput").ap() for n, a in arrays.items()}
        io["out"] = nc.dram_tensor("out", (D, S), F32, kind="ExternalOutput").ap()
        return nc, program(nc, io, counts)

    _, counts = build(None)
    nc, again = build(counts)
    assert again == counts
    r = _run(nc, [{f"in_{n}": a for n, a in arrays.items()}], core_ids=[0])
    return np.ascontiguousarray(np.asarray(r.results[0]["out"]).T)[None]
```

```python
from contextlib import ExitStack

import numpy as np
import concourse.bass as bass
from concourse import mybir

F32 = mybir.dt.float32
F32R = mybir.dt.float32r
ACT = mybir.ActivationFunctionType
ALU = mybir.AluOpType
AX_X = mybir.AxisListType.X

P = 128
D = 1024
KT = D // P
S = 256
ST = S // P
BW = 512
BT = BW // P
HEADS = 4
ATT_DH = 64
ATT_SCALE = ATT_DH ** -0.5
K_SCALE = 128 ** -0.5
SC_K, CF_K, FF_K, RG_K = 3, 31, 3, 4
PAD = CF_K // 2
D_FF = 2816
FT = D_FF // P
GLA_H = 4
GLA_DK = 128
EPS = 1e-6
LEVELS = (1, 2, 4, 8, 16, 32, 64)
RING = 3
PARTS = 3
AHEAD = 2
SLAB = 2048
BANKS = 8

IN_COL = dict(ret_q=0, ret_k=512, ret_v=1024, ret_z=1536, sc_b=2048, sc_c=2560, sc_x=3072, sc_z=3584,
              cf_a=4096, cf_g=4608, cf_z=5120, att_q=5632, att_kv=6144, att_z=6400, gates=6912)
BRANCHES = dict(ret=0, sc=1, cf=2, att=3)
MERGE_ORDER = ("sc", "ret", "att", "cf")

PARAMS = dict(norm_w=2 * 8, gn_w=2 * 4, sc_w=2 * 4 * SC_K, cf_w=2 * 4 * CF_K, cf_b=2 * 4, ln_w=2 * 4, ln_b=2 * 4,
              sink=2 * 8, b_mod=2 * 24, fin_w=8, decay=16, lam=8, c_vec=24,
              ada_b=2 * 48, norm_g=2 * 4 * 8, ff_w=2 * FF_K * 44, ff_b=2 * 44,
              rg_w=RG_K * 8, rg_b=8, rg_ba=8, rg_bx=8, gla_b=4, gla_g=2, gla_z=8 * 16)
TABLES = dict(ident=P, ones=P, turn=P, cos=S, sin=S, ahead=2 * S, behind=2 * S, q_pos=2 * S, k_pos=4,
              band=2 * P, eps=1)
LATE = 8 * P


def offsets(sizes):
    at, out = 0, {}
    for name, n in sizes.items():
        out[name] = (at, n)
        at += n
    return out, at


PARAM_AT, N_PARAM = offsets(PARAMS)
TABLE_AT, N_TABLE = offsets(TABLES)


class Steps:

    def __init__(self, sem, known):
        self.sem, self.known, self.n, self.now = sem, known, 0, {}

    def does(self, *names):
        self.n += 1
        for name in names:
            assert name not in self.now, name
            self.now[name] = self.n
        return self.sem, 1

    def did(self, name):
        if name in self.now:
            return self.sem, self.now[name]
        return self.sem, (self.known[name] if self.known is not None else 1)


def program(nc, io, counts):
    ctx = ExitStack()
    with ctx:
        def sbuf(name, cols, dtype=F32):
            return ctx.enter_context(nc.sbuf_tensor(name, [P, cols], dtype))

        def sem(name):
            return ctx.enter_context(nc.semaphore(name))

        counts = counts or dict(tensor=None, vector=None, scalar=None)
        tensor = Steps(sem("tensor_done"), counts["tensor"])
        vector = Steps(sem("vector_done"), counts["vector"])
        scalar = Steps(sem("scalar_done"), counts["scalar"])

        def emptied(name):
            for e in (vector, scalar):
                if "emptied " + name in (e.known or {}):
                    return e.did("emptied " + name)
            return vector.sem, 1

        def used(slab):
            for e in (vector, tensor):
                if "used " + slab in (e.known or {}):
                    return e.did("used " + slab)
            return vector.sem, 1

        slab_landed = [sem(f"slab_landed{i}") for i in range(RING)]
        acc_landed = [sem(f"acc_landed{i}") for i in range(2)]
        params_landed, tables_landed = sem("params_landed"), sem("tables_landed")
        x_landed, late_landed, out_landed = sem("x_landed"), sem("late_landed"), sem("out_landed")

        ring = [sbuf(f"ring{i}", SLAB) for i in range(RING)]
        params, tables = sbuf("params", N_PARAM), sbuf("tables", N_TABLE)
        xT = sbuf("xT", KT * 2 * S)[:].rearrange("p (t s) -> p t s", t=KT)
        h_hi, h_lo = (sbuf(n, KT * 2 * S, F32R)[:].rearrange("p (t s) -> p t s", t=KT) for n in ("h_hi", "h_lo"))
        w_hi, w_lo = ([sbuf(f"{n}{i}", KT * P, F32R)[:].rearrange("p (t n) -> p t n", t=KT) for i in range(PARTS)]
                      for n in ("w_hi", "w_lo"))

        def param(name, *dims):
            at, n = PARAM_AT[name]
            ap = params[:, at:at + n]
            if len(dims) == 1:
                return ap.rearrange("p (a b) -> p a b", a=dims[0])
            if len(dims) == 2:
                return ap.rearrange("p (a b c) -> p a b c", a=dims[0], b=dims[1])
            if len(dims) == 3:
                return ap.rearrange("p (a b c d) -> p a b c d", a=dims[0], b=dims[1], c=dims[2])
            return ap

        def table(name):
            at, n = TABLE_AT[name]
            return tables[:, at:at + n]

        ident, ones, turn = table("ident"), table("ones"), table("turn")
        ones_pp = ones
        eps = table("eps")
        at = TABLE_AT["ahead"][0]
        level = tables[:, at:at + LATE]
        gla_a = tables[0:16, at + LATE:at + LATE + 512]

        arena_cols = 18672
        with nc.sbuf_tensor("arena", [P, arena_cols], F32) as arena:
            pass
        arena_r = sbuf("arena_r", arena_cols, F32R)

        def carve(at, *dims):
            n = int(np.prod(dims))
            assert at + n <= arena_cols, (at, dims)
            ap = arena[:, at:at + n]
            if len(dims) == 2:
                return ap.rearrange("p (a b) -> p a b", a=dims[0])
            if len(dims) == 3:
                return ap.rearrange("p (a b c) -> p a b c", a=dims[0], b=dims[1])
            if len(dims) == 4:
                return ap.rearrange("p (a b c d) -> p a b c d", a=dims[0], b=dims[1], c=dims[2])
            return ap

        cx = carve(0, BT, 2, S + 2)
        u_pad = carve(0, BT, 2, S + 2 * PAD)
        k_wt = [carve(1024 * i, ST, HEADS, P) for i in range(2)]
        att_o = carve(0, BT, 2 * S)
        s_br = carve(2288, BT, 2 * S)
        f_br = carve(4336, BT, 2 * S)
        ret_q = ret_o = carve(6384, BT, 2 * S)
        ret_k, ret_v = carve(8432, BT, 2 * S), carve(10480, 2 * ST, BW)
        att_q = carve(12528, BT, 2 * S)
        z_sil = dict(ret=carve(8432, BT, 2 * S), att=carve(10480, BT, 2 * S), cf=carve(12528, BT, 2 * S))
        merged = carve(8432, KT, 2 * S)
        att_k, att_ks = carve(14576, 2 * S), carve(15088, 2 * S)
        att_v = carve(15600, 2 * ST, P)
        state = carve(16112, HEADS, 2, P)
        branch = dict(ret=ret_o, sc=s_br, cf=f_br, att=att_o)

        def out_at(l):
            return S if l else 0

        def parts_of(at):
            return arena_r[:, at:at + BT * 2 * S].rearrange("p (t s) -> p t s", t=BT)

        branch_hi = parts_of(16624)
        branch_lo = dict(ret=parts_of(6384), sc=parts_of(2288), cf=parts_of(4336), att=parts_of(0))

        def rows(at, n):
            c = (4096 if at in ("rg", "post rg", "n3 0") else 14576) + 2 * P * (n % 2)
            return arena[:, c:c + 2 * P]

        yT, sq8 = carve(0, KT, S), carve(2048, KT, S)
        xb_pad = carve(4096, KT, S + RG_K - 1)
        xc, gel, rr, tt_, ix, a2 = (carve(6168 + 2048 * i, KT, S) for i in range(6))
        lv = carve(0, 8, GLA_H * S)
        gla_o = carve(4096, KT, S)
        gq, gk, la, le, gg = (carve(8192 + 1024 * i, GLA_H, S) for i in range(5))
        lprod = carve(10240, 8, P)
        r_sil = carve(11264, KT, S)
        gv = carve(13312, ST, D)
        attT = carve(15360, GLA_H, ST, S)
        zT, scan_one = carve(17408, S), carve(17664, S)
        ff_act = carve(4096, FT, S)
        ff_hi, ff_lo = (arena_r[:, c:c + (FT - 2 * KT) * S].rearrange("p (t s) -> p t s", s=S)
                        for c in (9728, 9728 + (FT - 2 * KT) * S))

        def ff_part(h, n):
            if n >= 2 * KT:
                return (ff_hi if h is h_hi else ff_lo)[:, n - 2 * KT, :]
            return h[:, n, S:2 * S] if n < KT else h[:, n - KT, 0:S]

        work = [sbuf(f"work{i}", 2 * S) for i in range(8)]
        act_t = work[0:4]
        dve_t = work[4:8]
        stat = sbuf("stat", 2 * S)
        stat2 = sbuf("stat2", 2 * S)
        exps = (act_t[0], act_t[1], stat, stat2)
        small = sbuf("small", 256)
        soft_m, soft_s = small[:, 0:8], small[:, 8:16]
        soft_e, soft_d = small[:, 16:24], small[:, 24:32]
        csil = small[:, 32:56].rearrange("p (t v) -> p t v", t=KT)
        soft_p = small[:, 56:80]
        k_decay = small[:, 80:112].rearrange("p (l d t h) -> p l d t h", l=2, d=2, t=2)
        nsink = small[:, 112:128].rearrange("p (l h) -> p l h", l=2)
        lp = [small[:, 128 + 24 * i:152 + 24 * i] for i in range(4)]
        log_g = small[:, 224:240].rearrange("p (l d h) -> p l d h", l=2, d=2)
        lam8, lam8n = small[:, 240:248], small[:, 248:256]
        warm = sbuf("warm", 16)
        mods = sbuf("mods", 2 * 48 + 2 * 16 + 2 * 48 + 2 * 32)
        mod1 = [mods[:, 48 * l:48 * l + 48].rearrange("p (n v) -> p n v", v=2) for l in range(2)]
        gain1 = [mods[:, 96 + 16 * l:112 + 16 * l].rearrange("p (n v) -> p n v", v=2) for l in range(2)]
        mod2 = [mods[:, 128 + 48 * l:176 + 48 * l] for l in range(2)]
        gain2 = [mods[:, 224 + 32 * l:256 + 32 * l].rearrange("p (q t) -> p q t", q=4) for l in range(2)]

        psum = [ctx.enter_context(nc.psum_tensor(f"bank{i}", [P, 512], F32)) for i in range(BANKS)]
        bank_at = {}

        def bank(name):
            return psum[bank_at[name] % BANKS]

        stream, w_units, unit_of = [], [], {}

        def by_rows(w):
            return w.rearrange("(t p) n -> p t n", p=P)

        def cols(name, w, c0, n=256):
            src = by_rows(w)[:, :, c0:c0 + n]
            stream.append((name, src, (src.shape[1], n)))

        def split_cols(name, tiles, w, c0, run):
            for j, tile in enumerate(tiles):
                unit_of[tile] = len(w_units)
                w_units.append((len(stream), j, run))
            cols(name, w, c0)

        def section(l, name, i, run):
            tiles = (f"att_k {l}", f"att_v {l}") if name == "att_kv" else [f"{name} {l}.{2 * i + j}" for j in range(2)]
            split_cols(f"w {name} {l}.{i}", tiles, io["w_in"][l], IN_COL[name] + 256 * i, run)

        def split_until(tile):
            i = unit_of[tile]
            u = i
            for v in range(i + 1, min(i + AHEAD + 1, len(w_units))):
                if w_units[v][2] == w_units[i][2]:
                    u = v
            return u

        mod_at = {"start": [("mod", 0, i) for i in range(8)],
                  "n1 1": [("ada", 1, i) for i in range(5, 8)],
                  "fin": [("ada", 1, i) for i in range(8, 11)],
                  "n2 0": [("ada", 1, i) for i in range(11, 14)],
                  "rg": [("ada", 1, i) for i in range(14, 19)],
                  "post rg": [("ada", 1, i) for i in range(19, 22)],
                  "n3 0": [("ada", 1, i) for i in range(22, 24)]}
        pairs = KT // 2 * len(MERGE_ORDER)
        mods = [("mod", 0, i) for i in range(8, 12)] + [("mod", 1, i) for i in range(12)]
        adas = [("ada", 0, i) for i in range(24)] + [("ada", 1, i) for i in range(5)]
        merge_mods = [[[]] + [[mods[p], adas[p]] for p in range(pairs - 2)] + [mods[pairs - 2:]],
                      [[]] + [[m] for m in adas[pairs - 2:]]]
        acc_order = [m for layer in merge_mods for pair in layer for m in pair]

        def mod_slabs(at):
            for kind, l, i in mod_at[at]:
                cols(f"w {kind} {l}.{i}", io["w_mod" if kind == "mod" else "ada_w_2"][l], 256 * i)

        mod_slabs("start")
        for l in range(2):
            run = f"in {l}"
            for i in range(2):
                section(l, "sc_c", i, run)
                if l and i == 0:
                    mod_slabs("n1 1")
                section(l, "sc_x", i, run)
            for i in range(2):
                section(l, "cf_g", i, run)
                section(l, "cf_a", i, run)
            for a in ("ret_q", "ret_k", "ret_v", "att_q"):
                for i in range(2):
                    section(l, a, i, run)
            section(l, "att_kv", 0, run)
            for i in range(2):
                section(l, "sc_b", i, run)
                section(l, "sc_z", i, run)
            run = f"merge {l}"
            for a in ("ret_z", "att_z", "cf_z"):
                for i in range(2):
                    section(l, a, i, run)
            for b in MERGE_ORDER:
                for i in range(4):
                    split_cols(f"w gate {l}.{b}.{i}", [f"gate {l}.{b}.{2 * i + j}" for j in range(2)], io["w_in"][l],
                               IN_COL["gates"] + D * BRANCHES[b] + 256 * i, run)
                    split_cols(f"w branch {l}.{b}.{i}", [f"br {l}.{b}.{2 * i + j}" for j in range(2)],
                               io["w_branch"][l, BRANCHES[b]], 256 * i, run)
            for i in range(4):
                split_cols(f"w out {l}.{i}", [f"out {l}.{2 * i + j}" for j in range(2)], io["w_out"][l], 256 * i, run)

        def ffn_slabs(l):
            for i in range(11):
                for nm, c0 in (("ffg", 0), ("ffv", D_FF)):
                    split_cols(f"w {nm} {l}.{i}", [f"{nm} {l}.{2 * i + j}" for j in range(2)], io["ffn_w_up_2"][l],
                               c0 + 256 * i, f"ffn {l}")
                    if l == 0 and i == 0 and nm == "ffg":
                        mod_slabs("n3 0")
            down = by_rows(io["ffn_w_down_2"][l])
            for c in range(4):
                for k0 in range(0, FT, 8):
                    n = min(8, FT - k0)
                    for j in range(2):
                        unit_of[f"down {l}.{c}.{k0}.{j}"] = len(w_units)
                        w_units.append((len(stream), j, f"ffn {l}"))
                    stream.append((f"w down {l}.{c}.{k0}", down[:, k0:k0 + n, 256 * c:256 * c + 256], (n, 256)))

        mod_slabs("fin")
        def rg_slab(nm, i):
            split_cols(f"w {nm} {i}", [f"{nm} {2 * i + j}" for j in range(2)], io["rg_w_in_2"][0],
                       256 * i + (D if nm == "rgx" else 0), "rg")

        for i in range(4):
            rg_slab("rgx", i)
            if i == 0:
                mod_slabs("n2 0")
        rg_slab("rgg", 0)
        for n in ("a", "x"):
            stream.append((f"w rg{n}", io[f"rg_w{n}_2"][0].rearrange("g (t p) n -> p (g t) n", p=P), (8, 256)))
        for i in range(1, 4):
            rg_slab("rgg", i)
        mod_slabs("rg")
        for i in range(4):
            split_cols(f"w rgo {i}", [f"y rg.{2 * i + j}" for j in range(2)], io["rg_w_out_2"][0], 256 * i, "rgo")
        mod_slabs("post rg")
        ffn_slabs(0)
        for n, c0, k in (("q", 0, 2), ("k", 512, 2), ("v", 1024, 4), ("r", 2048, 4)):
            for i in range(k):
                split_cols(f"w gla{n} {i}", [f"gla{n} {2 * i + j}" for j in range(2)], io["gla_w_in_2"][0],
                           c0 + 256 * i, "gla")
        for i in range(4):
            split_cols(f"w glao {i}", [f"y gla.{2 * i + j}" for j in range(2)], io["gla_w_out_2"][0], 256 * i, "gla")
        ffn_slabs(1)

        def mod_turns(at, n):
            last = len(mod_at[at])
            return [b for b in ((n - 2, n - 1) if n == last else (n - 2,)) if b >= 0]

        def mod_col(at, b, j):
            return 256 + 4 * (b % 2) + 2 * j

        def pair_before(l, b, i):
            p = KT // 2 * MERGE_ORDER.index(b) + i
            return merge_mods[l][p - 1] if p else []

        def acc_of(m):
            return (stat, stat2)[acc_order.index(m) % 2]

        def acc_slot(m):
            return carve(12528 + SLAB * (acc_order.index(m) % 2), KT, 256)

        def acc_slab_landed(m):
            n = acc_order.index(m)
            return acc_landed[n % 2], 16 * (n // 2 + 1)

        slab_of = {name: n for n, (name, _, _) in enumerate(stream)}

        def slot_of(n):
            a, b = stream[n][2]
            return ring[n % RING][:, 0:a * b].rearrange("p (a b) -> p a b", a=a)

        def landed(n):
            return slab_landed[n % RING], 16 * (n // RING + 1)

        block = ctx.enter_context(nc.Block())

        @block.tensor
        def _(pe):
            state_ = dict(bank=0)

            def take(name):
                n = slab_of[name]
                pe.wait_ge(*landed(n))
                return slot_of(n)

            def open_bank(name):
                n = state_["bank"]
                state_["bank"] += 1
                bank_at[name] = n
                if n >= BANKS:
                    pe.wait_ge(*emptied(order[n - BANKS]))
                order.append(name)
                return psum[n % BANKS]

            order = []

            def unit(name):
                u = unit_of[name]
                pe.wait_ge(*scalar.did(f"hi {u}"))
                pe.wait_ge(*vector.did(f"lo {u}"))
                return w_hi[u % PARTS], w_lo[u % PARTS], f"used unit {u}"

            def part(h, s0):
                return lambda k, n: h[:, k, s0:s0 + n]

            def three_products(out, ws, k, hi, lo, start, stop):
                pe.matmul(out, ws[0][:, k, :], hi, start=start, stop=False)
                pe.matmul(out, ws[0][:, k, :], lo, start=False, stop=False)
                return pe.matmul(out, ws[1][:, k, :], hi, start=False, stop=stop)

            def both_parts(name):
                def ready(k):
                    pe.wait_ge(*scalar.did(f"hi {name}.{k}"))
                    pe.wait_ge(*vector.did(f"lo {name}.{k}"))
                return ready

            def project(name, n, hi=part(h_hi, 0), lo=part(h_lo, 0), ready=None, tiles=KT):
                w = unit(name)
                out = open_bank(name)
                for k in range(tiles):
                    if ready:
                        ready(k)
                    m = three_products(out[:, 0:n], w, k, hi(k, n), lo(k, n), k == 0, k == tiles - 1)
                m.then_inc(*tensor.does("filled " + name, w[2]))

            def turn_tokens(name, src, tiles):
                pe.wait_ge(*scalar.did("rows " + name))
                out = open_bank("turned " + name)
                for t in range(tiles):
                    m = pe.transpose(out[:, P * t:P * t + P], src[:, P * t:P * t + P], ident)
                m.then_inc(*tensor.does("filled turned " + name))

            def mod_contract(m):
                kind, l, i = m
                name = f"{kind} {l}.{i}"
                acc = acc_of(m)
                pe.wait_ge(*vector.did("acc " + name))
                out = open_bank("sum " + name)
                for j in range(2):
                    for c in range(2 if kind == "mod" else 1):
                        o = 2 * j + c if kind == "mod" else j
                        ins = pe.matmul(out[:, o:o + 1], acc[:, 2 * P * c + P * j:2 * P * c + P * j + P], ones[:, 0:1],
                                        start=True, stop=True)
                ins.then_inc(*tensor.does("filled sum " + name))

            def mod_step(at, n):
                todo = mod_at[at]
                name = "%s %d.%d" % todo[n] if n < len(todo) else "end " + at
                w = take("w " + name) if n < len(todo) else None
                out = open_bank("row " + name)
                if w is not None:
                    vecs = csil[:, :, 0:2] if todo[n][0] == "mod" else csil[:, :, 2:3]
                    for k in range(KT):
                        m = pe.matmul(out[0:vecs.shape[2], 0:256], vecs[:, k, :], w[:, k, :],
                                      start=k == 0, stop=k == KT - 1)
                for b in mod_turns(at, n):
                    kind, l, i = todo[b]
                    nv = 2 if kind == "mod" else 1
                    pe.wait_ge(*scalar.did(f"row {kind} {l}.{i}"))
                    for j in range(2):
                        c = mod_col(at, b, j)
                        m = pe.transpose(out[:, c:c + nv], rows(at, b)[0:nv, P * j:P * j + P], ident[0:nv, 0:nv])
                m.then_inc(*tensor.does("filled row " + name, *(["used w " + name] if w is not None else [])))

            def modulations(at, between=()):
                between = iter(between)
                for n in range(len(mod_at[at]) + 1):
                    if (at, n) == ("start", 2):
                        pe.wait_ge(tables_landed, 16)
                    mod_step(at, n)
                    if n in (3, 4):
                        for _ in range(4):
                            next(between, None)

            def sum_squares(name, n, tiles):
                out = open_bank(name)
                for k in range(tiles):
                    pe.wait_ge(*scalar.did(f"sq {name}.{k}"))
                    m = pe.matmul(out[:, 0:n], ones_pp, squares(name, k, n), start=k == 0, stop=k == tiles - 1)
                    m.then_inc(*tensor.does(f"summed {name}.{k}", *(["filled " + name] if k == tiles - 1 else [])))
                    yield

            def sum_all(name, n, tiles):
                for _ in sum_squares(name, n, tiles):
                    pass

            def squares(name, k, n):
                return act_t[k % 4][:, 0:n]

            pe.wait_ge(params_landed, 16)
            pe.wait_ge(*scalar.did("csil"))

            for l in range(2):
                nx = 2 * S if l == 0 else S
                groups = (0, 1) if l == 0 else (0,)
                if l == 0:
                    modulations("start", sum_squares("n1 0", 2 * S, KT))
                else:
                    sum_all("n1 1", 2 * S, KT)
                    modulations("n1 1")
                for a, b in (("sc_c", "sc_x"), ("cf_g", "cf_a")):
                    for i in range(2):
                        for n in (a, b):
                            for j in range(2):
                                first = (n, i, j) == ("sc_c", 0, 0)
                                project(f"{n} {l}.{2 * i + j}", nx, ready=both_parts(f"n1 {l}") if first else None)
                for n in range(BT):
                    project(f"ret_q {l}.{n}", nx)
                for n in range(BT):
                    project(f"ret_k {l}.{n}", 2 * S)
                for n in range(BT):
                    project(f"ret_v {l}.{n}", 2 * S)
                    if n:
                        turn_tokens(f"ret_v {l}.{n - 1}", act_t[(n - 1) % 2], 2 * ST)
                for n in range(BT):
                    project(f"att_q {l}.{n}", nx)
                    if n == 0:
                        turn_tokens(f"ret_v {l}.{BT - 1}", act_t[(BT - 1) % 2], 2 * ST)
                project(f"att_k {l}", 2 * S)
                project(f"att_v {l}", 2 * S)
                for i in range(2):
                    for n in ("sc_b", "sc_z"):
                        for j in range(2):
                            project(f"{n} {l}.{2 * i + j}", nx)
                            if (n, i, j) == ("sc_b", 0, 0):
                                turn_tokens(f"att_v {l}", act_t[0], 2 * ST)

                for t in range(ST):
                    out = open_bank(f"kT {l}.{t}")
                    for hd in range(HEADS):
                        pe.wait_ge(*scalar.did(f"ret_k {l}.{hd}"))
                        m = pe.transpose(out[:, P * hd:P * hd + P], ret_k[:, hd, S + P * t:S + P * t + P], ident)
                    m.then_inc(*tensor.does(f"filled kT {l}.{t}"))
                for t in range(BT + 1):
                    src = att_q[:, t, 0:S] if t < BT else att_k[:, 0:S]
                    pe.wait_ge(*scalar.did(f"att_q {l}.{t}" if t < BT else f"att_k {l}"))
                    out = open_bank(f"turn {l}.{t}")
                    pe.matmul(out[:, 0:S], turn, src, start=True, stop=True)\
                        .then_inc(*tensor.does(f"filled turn {l}.{t}"))

                pe.wait_ge(*scalar.did(f"ret_v {l}.{BT - 1}"))
                for hd in range(HEADS):
                    out = open_bank(f"state {l}.{hd}")
                    for d in range(2):
                        pe.wait_ge(*vector.did(f"k_wt {l}.{ST - 1}.{d}"))
                        for t in range(ST):
                            m = pe.matmul(out[:, P * d:P * d + P], k_wt[d][:, t, hd, :],
                                          ret_v[:, ST + t, P * hd:P * hd + P], start=t == 0, stop=t == ST - 1)
                    m.then_inc(*tensor.does(f"filled state {l}.{hd}"))

                units = [(hd, g) for hd in range(HEADS) for g in groups]

                def ret_scores(hd, g):
                    name = f"rs {l}.{hd}.{g}"
                    pe.wait_ge(*scalar.did(f"ret_q {l}.{hd}"))
                    out = open_bank(name)
                    for j in range(ST):
                        m = pe.matmul(out[:, S * j:S * j + S], ret_k[:, hd, S * g + P * j:S * g + P * j + P],
                                      ret_q[:, hd, S * g:S * g + S], start=True, stop=True)
                    m.then_inc(*tensor.does("filled " + name))

                def ret_out(hd, g):
                    name = f"ro {l}.{hd}.{g}"
                    pe.wait_ge(*vector.did(f"ret_p {l}.{hd}.{g}"))
                    p_t = dve_t[2 + units.index((hd, g)) % 2]
                    out = open_bank(name)
                    for j in range(ST):
                        m = pe.matmul(out[:, 0:S], ret_v[:, ST * g + j, P * hd:P * hd + P], p_t[:, S * j:S * j + S],
                                      start=j == 0, stop=g == 1 and j == ST - 1)
                    if g == 0:
                        pe.wait_ge(*scalar.did(f"state {l}.{hd}"))
                        pe.wait_ge(*vector.did(f"q_wt {l}.{hd}"))
                        for d in range(2):
                            m = pe.matmul(out[:, 0:S], state[:, hd, d, :], dve_t[hd % 2][:, S * d:S * d + S],
                                          start=False, stop=d == 1)
                    m.then_inc(*tensor.does("filled " + name))

                for n, (hd, g) in enumerate(units):
                    ret_scores(hd, g)
                    if n:
                        ret_out(*units[n - 1])
                ret_out(*units[-1])

                att = [(g, t, q) for g in groups for t in range(BT) for q in range(ST)]

                def att_scores(i):
                    g, t, q = att[i]
                    keys = 0 if g == 0 else S
                    for s in range(2):
                        name = f"as {l}.{i}.{s}"
                        rows = slice(64 * s, 64 * s + 64)
                        k_src = att_k if s == t // 2 else att_ks
                        out = open_bank(name)
                        pe.matmul(out[:, 0:2 * S - keys], att_q[rows, t, S * g + P * q:S * g + P * q + P],
                                  k_src[rows, keys:2 * S], start=True, stop=True)\
                            .then_inc(*tensor.does("filled " + name))

                def gate_of(i):
                    every = len(att) // (2 * BT)
                    n = i // every
                    return (("ret", "att")[n // BT], l, n % BT) if i % every == 0 and n < 2 * BT else None

                def att_turn(i):
                    g, t, q = att[i]
                    for s in range(2):
                        name = f"at {l}.{i}.{s}"
                        pe.wait_ge(*vector.did(f"att_p {l}.{i}.{s}"))
                        out = open_bank(name)
                        for b in range(4 - 2 * g):
                            m = pe.transpose(out[:, P * b:P * b + P], dve_t[2 * (i % 2) + s][:, P * b:P * b + P], ident)
                        m.then_inc(*tensor.does("filled " + name))

                def att_out(i):
                    g, t, q = att[i]
                    name = f"ao {l}.{i}"
                    out = open_bank(name)
                    for s in range(2):
                        pe.wait_ge(*scalar.did(f"att_t {l}.{i}.{s}"))
                        nb = 4 - 2 * g
                        c = 64 * (t // 2)
                        for b in range(nb):
                            m = pe.matmul(out[64 * s:64 * s + 64, 0:P], att_v[:, 2 * g + b, c:c + 64],
                                          act_t[2 + s][:, P * b:P * b + P], start=b == 0, stop=b == nb - 1)
                    m.then_inc(*tensor.does("filled " + name))

                pe.wait_ge(*vector.did(f"att_q roped {l}.{BT - 1}"))
                pe.wait_ge(*vector.did(f"att_ks {l}"))
                pe.wait_ge(*scalar.did(f"att_v {l}"))
                att_scores(0)
                for i in range(len(att) + 2):
                    if i + 1 < len(att):
                        att_scores(i + 1)
                    if gate_of(i):
                        project("%s_z %d.%d" % gate_of(i), nx)
                    if i >= 2:
                        att_out(i - 2)
                    if 1 <= i <= len(att):
                        att_turn(i - 1)

                for hd in range(HEADS):
                    pe.wait_ge(*scalar.did(f"ret_o {l}.{hd}.{groups[-1]}"))
                    name = f"gm {l}.{hd}"
                    out = open_bank(name)
                    pe.matmul(out[:, 0:nx], ones_pp, ret_o[:, hd, 0:nx], start=True, stop=True)\
                        .then_inc(*tensor.does("filled " + name))
                name = f"lm {l}"
                out = open_bank(name)
                for t in range(BT):
                    pe.wait_ge(*vector.did(f"conv {l}.{t}"))
                    m = pe.matmul(out[:, 0:nx], ones_pp, f_br[:, t, 0:nx], start=t == 0, stop=t == BT - 1)
                m.then_inc(*tensor.does("filled " + name))
                for n in range(2):
                    project(f"cf_z {l}.{n}", nx)
                for hd in range(HEADS):
                    name = f"gv {l}.{hd}"
                    pe.wait_ge(*scalar.did(f"sq {name}"))
                    pe.matmul(open_bank(name)[:, 0:nx], ones_pp, act_t[hd][:, 0:nx], start=True, stop=True)\
                        .then_inc(*tensor.does("filled " + name))
                for n in range(2, BT):
                    project(f"cf_z {l}.{n}", nx)
                sum_all(f"lv {l}", nx, BT)

                for b in MERGE_ORDER:
                    for i in range(4):
                        for m in pair_before(l, b, i):
                            mod_contract(m)
                        for j in range(2):
                            project(f"gate {l}.{b}.{2 * i + j}", nx)
                        for j in range(2):
                            project(f"br {l}.{b}.{2 * i + j}", nx, part(branch_hi, 0), part(branch_lo[b], 0),
                                    None if i or j else both_parts(f"br {l}.{b}"), BT)
                for m in merge_mods[l][-1]:
                    mod_contract(m)
                for n in range(KT):
                    project(f"out {l}.{n}", nx, part(h_hi, out_at(l)), part(h_lo, out_at(l)),
                            None if n else both_parts(f"merged {l}"))

            sum_all("fin", S, KT)
            modulations("fin")

            def ffn(l):
                sum_all(f"n3 {l}", S, KT)
                if l == 0:
                    modulations("n3 0")
                for i in range(11):
                    for nm in ("ffg", "ffv"):
                        for j in range(2):
                            first = (nm, i, j) == ("ffg", 0, 0)
                            project(f"{nm} {l}.{2 * i + j}", S, ready=both_parts(f"n3 {l}") if first else None)
                tag = f"ffn {l}"
                for c in range(4):
                    outs = [open_bank(f"y {tag}.{2 * c + j}") for j in range(2)]
                    for k0 in range(0, FT, 8):
                        for j in range(2):
                            parts = unit(f"down {l}.{c}.{k0}.{j}")
                            for k in range(k0, min(k0 + 8, FT)):
                                if c == 0 and j == 0:
                                    both_parts(f"ff {l}")(k)
                                m = three_products(outs[j][:, 0:S], parts, k - k0, ff_part(h_hi, k), ff_part(h_lo, k),
                                                   k == 0, k == FT - 1)
                            done = [f"filled y {tag}.{2 * c + j}"] if k == FT - 1 else []
                            m.then_inc(*tensor.does(parts[2], *done))
                    for j in range(2):
                        if c:
                            sum_y(tag, 2 * c - 2 + j)
                for j in range(2):
                    sum_y(tag, KT - 2 + j)

            post_bank = {}

            def sum_y(tag, k):
                if k == 0:
                    post_bank[tag] = open_bank(f"ys {tag}")
                pe.wait_ge(*scalar.did(f"y {tag}.{k}"))
                m = pe.matmul(post_bank[tag][:, 0:S], ones_pp, sq8[:, k, :], start=k == 0, stop=k == KT - 1)
                if k == KT - 1:
                    m.then_inc(*tensor.does(f"filled ys {tag}"))

            def block_out(tag, ready):
                for n in range(KT):
                    project(f"y {tag}.{n}", S, part(h_hi, S), part(h_lo, S), ready if n == 0 else None)
                    if n:
                        sum_y(tag, n - 1)
                sum_y(tag, KT - 1)

            sum_all("n2 0", S, KT)
            modulations("n2 0")
            for n in range(KT):
                project(f"rgx {n}", S, ready=None if n else both_parts("n2 0"))
            for n in range(2):
                project(f"rgg {n}", S)
            for nm in ("rga", "rgx2"):
                slab = "w rga" if nm == "rga" else "w rgx"
                w = take(slab)
                for n in range(KT):
                    gblk, j = n // 2, n % 2
                    out = open_bank(f"{nm} {n}")
                    for i in range(2):
                        pe.wait_ge(*vector.did(f"xc {2 * gblk + i}"))
                        m = pe.matmul(out[:, 0:S], w[:, 2 * gblk + i, P * j:P * j + P], xc[:, 2 * gblk + i, :],
                                      start=i == 0, stop=i == 1)
                    m.then_inc(*tensor.does(f"filled {nm} {n}", *([f"used {slab}"] if n == KT - 1 else [])))
            for n in range(2, KT):
                project(f"rgg {n}", S)
            modulations("rg")
            block_out("rg", both_parts("rg"))
            modulations("post rg")
            ffn(0)

            sum_all("n2 1", S, KT)
            wz, wa = param("gla_z", KT), gla_a
            out = open_bank("gla z")
            for k in range(KT):
                both_parts("n2 1")(k)
                pe.matmul(out[0:16, 0:S], wz[:, k, :], h_hi[:, k, 0:S].bitcast(F32), start=k == 0, stop=False)
                m = pe.matmul(out[0:16, 0:S], wz[:, k, :], h_lo[:, k, 0:S].bitcast(F32), start=False, stop=k == KT - 1)
            m.then_inc(*tensor.does("filled gla z"))
            pe.wait_ge(*scalar.did("zT"))
            pe.wait_ge(late_landed, 32)
            for hd in range(GLA_H):
                out = open_bank(f"alpha {hd}")
                pe.matmul(out[:, 0:S], wa[:, P * hd:P * hd + P], zT[0:16, :], start=True, stop=True)\
                    .then_inc(*tensor.does(f"filled alpha {hd}"))
            for nm in ("q", "k"):
                for n in range(GLA_H):
                    project(f"gla{nm} {n}", S)
            for n in range(KT):
                project(f"glav {n}", S)
                if n:
                    turn_tokens(f"glav {n - 1}", act_t[(n - 1) % 2], ST)
            turn_tokens(f"glav {KT - 1}", act_t[(KT - 1) % 2], ST)
            for n in range(GLA_H * ST):
                hd, t = n // ST, n % ST
                sl = slice(S * hd + P * t, S * hd + P * t + P)
                for half in range(2):
                    name = f"lev {n}.{half}"
                    for q in range(4):
                        if n == 0:
                            pe.wait_ge(*vector.did(f"lv {4 * half + q}"))
                    out = open_bank(name)
                    for q in range(4):
                        i = 4 * half + q
                        if i < len(LEVELS):
                            m = pe.matmul(out[:, P * q:P * q + P], lv[:, i, sl], lv[:, i, sl], start=True, stop=True)
                        else:
                            m = pe.matmul(out[:, P * q:P * q + P], gk[:, hd, P * t:P * t + P],
                                          gq[:, hd, P * t:P * t + P], start=True, stop=True)
                    m.then_inc(*tensor.does("filled " + name))
                if t == 1:
                    out = open_bank(f"cross {hd}")
                    pe.matmul(out[:, 0:P], lv[:, 7, S * hd:S * hd + P], lv[:, 7, S * hd + P:S * hd + S],
                              start=True, stop=True).then_inc(*tensor.does(f"filled cross {hd}"))
                if n % 2 == 0:
                    project(f"glar {n // 2}", S)
            def head_squares(hd):
                out = open_bank(f"gs {hd}")
                for e in range(2):
                    pe.wait_ge(*scalar.did(f"go {2 * hd + e}"))
                    m = pe.matmul(out[:, 0:S], ones_pp, sq8[:, 2 * hd + e, :], start=e == 0, stop=e == 1)
                m.then_inc(*tensor.does(f"filled gs {hd}"))

            pe.wait_ge(*scalar.did("gv 7"))
            for hd in range(GLA_H):
                for j in range(ST):
                    pe.wait_ge(*vector.did(f"attT {ST * hd + j}"))
                pe.wait_ge(*scalar.did(f"cross {hd}"))
                for e in range(2):
                    name = f"go {2 * hd + e}"
                    out = open_bank(name)
                    c = 256 * hd + P * e
                    pe.matmul(out[:, 0:S], gv[:, 0, c:c + P], attT[:, hd, 0, :], start=True, stop=False)
                    pe.matmul(out[:, P:S], gv[:, 1, c:c + P], attT[:, hd, 1, P:S], start=False, stop=True)\
                        .then_inc(*tensor.does("filled " + name))
                if hd:
                    head_squares(hd - 1)
            head_squares(GLA_H - 1)
            for n in range(KT // 2, KT):
                project(f"glar {n}", S)
            block_out("gla", both_parts("gla"))
            ffn(1)

        @block.sync
        def _(sp):
            sp.dma_start(params[:], io["params"]).then_inc(params_landed, 16)
            for n, (name, src, _) in enumerate(stream):
                if name == "w rgo 0":
                    sp.wait_ge(*vector.did(f"expo 1.{HEADS - 1}"))
                    sp.wait_ge(*scalar.did(f"q_dec 1.{HEADS - 1}"))
                    sp.dma_start(level, io["level"]).then_inc(late_landed, 16)
                    sp.dma_start(gla_a, io["gla_w_alpha_2"][0]).then_inc(late_landed, 16)
                if n == 2:
                    sp.dma_start(tables[:], io["tables"]).then_inc(tables_landed, 16)
                if n == RING + 1:
                    sp.dma_start(xT[:, :, 0:S], by_rows(io["x"])).then_inc(x_landed, 16)
                    sp.dma_start(xT[:, :, S:2 * S], by_rows(io["ctx"])).then_inc(x_landed, 16)
                if n >= RING:
                    sp.wait_ge(*used(stream[n - RING][0]))
                sp.dma_start(slot_of(n), src).then_inc(landed(n)[0], 16)
                if name.startswith("w branch"):
                    l, b, i = name.split(" ")[2].split(".")
                    l, pair = int(l), KT // 2 * MERGE_ORDER.index(b) + int(i)
                    for m in merge_mods[l][pair]:
                        at = acc_order.index(m)
                        if at >= 2 and acc_order[at - 2] in sum(merge_mods[l], []):
                            sp.wait_ge(*vector.did("acc used %s %d.%d" % acc_order[at - 2]))
                        else:
                            sp.wait_ge(*vector.did(f"branch {l}.cf.{BT - 1}"))
                        kind, ml, i = m
                        w = io["w_mod" if kind == "mod" else "ada_w_2"][ml]
                        sp.dma_start(acc_slot(m), by_rows(w)[:, :, 256 * i:256 * i + 256])\
                            .then_inc(acc_slab_landed(m)[0], 16)
            for k in range(KT):
                sp.wait_ge(*vector.did(f"x ffn 1.{k}"))
                sp.dma_start(by_rows(io["out"])[:, k, :], xT[:, k, 0:S]).then_inc(out_landed, 16)
            sp.wait_ge(out_landed, 16 * KT)

        @block.scalar
        def _(act):
            def evacuate(name, dst, func=ACT.Copy, also=(), last=True, **kw):
                act.wait_ge(*tensor.did("filled " + name))
                names = list(also) + ([f"emptied {name}"] if last else [])
                src = bank(name)[0:dst.shape[0], 0:int(np.prod(dst.shape[1:]))]
                if len(dst.shape) == 3:
                    src = src.rearrange("p (a b) -> p a b", a=dst.shape[1])
                return nc.scalar.activation(dst, src, func, **kw)\
                    .then_inc(*scalar.does(*names))

            fed = dict(n=0)

            def split_to(last):
                while fed["n"] <= last:
                    u = fed["n"]
                    n, half, _ = w_units[u]
                    act.wait_ge(*landed(n))
                    if u >= PARTS:
                        act.wait_ge(*tensor.did(f"used unit {u - PARTS}"))
                    src = slot_of(n)[:, :, P * half:P * half + P]
                    nc.scalar.activation(w_hi[u % PARTS][:, 0:src.shape[1], :], src, ACT.Copy)\
                        .then_inc(*scalar.does(f"hi {u}"))
                    fed["n"] += 1

            def first_units(tile):
                split_to(unit_of[tile] + 1)

            def projected(name, dst, func=ACT.Copy, also=(), **kw):
                split_to(split_until(name))
                return evacuate(name, dst, func, also, **kw)

            def square_all(name, n, tiles, src, ready=None, also=None):
                for k in range(tiles):
                    if ready:
                        act.wait_ge(*ready(k))
                    if k >= 4:
                        act.wait_ge(*tensor.did(f"summed {name}.{k - 4}"))
                    nc.scalar.activation(act_t[k % 4][:, 0:n], src(k), ACT.Square)\
                        .then_inc(*scalar.does(f"sq {name}.{k}"))
                    if also:
                        also(k)

            warmed = dict(n=0)

            def warm_sqrt(name):
                i = warmed["n"]
                nc.scalar.activation(warm[:, i:i + 1], eps, ACT.Sqrt).then_inc(*scalar.does(f"warm {name}"))
                warmed["n"] += 1

            def deviation(name, n, count):
                evacuate(name, stat[:, 0:n], ACT.Sqrt, [f"dev {name}"], scale=1.0 / count, bias=eps)

            def mod_row(at, n):
                todo = mod_at[at]
                name = "row %s %d.%d" % todo[n] if n < len(todo) else f"row end {at}"
                turned = mod_turns(at, n)
                if n < len(todo):
                    evacuate(name, rows(at, n)[0:2 if todo[n][0] == "mod" else 1, :], also=[name], last=not turned)
                else:
                    act.wait_ge(*tensor.did("filled " + name))
                for b in turned:
                    kind, l, i = todo[b]
                    for j in range(2):
                        c = 2 * i + j
                        if kind == "mod":
                            dst, bias = mod1[l][:, c, :], param("b_mod", 2)[:, l, c:c + 1]
                        else:
                            dst, bias = mod2[l][:, c:c + 1], param("ada_b", 2)[:, l, c:c + 1]
                        at_ = mod_col(at, b, j)
                        a = nc.scalar.activation(dst, bank(name)[:, at_:at_ + dst.shape[1]], ACT.Identity, bias=bias)
                if turned:
                    a.then_inc(*scalar.does("emptied " + name, *["col %s %d.%d" % todo[b] for b in turned]))

            def mod_cols(m):
                kind, l, i = m
                name = f"sum {kind} {l}.{i}"
                act.wait_ge(*tensor.did("filled " + name))
                for j in range(2):
                    c = 2 * i + j
                    if kind == "mod":
                        dst, bias = mod1[l][:, c, :], param("b_mod", 2)[:, l, c:c + 1]
                    else:
                        dst, bias = mod2[l][:, c:c + 1], param("ada_b", 2)[:, l, c:c + 1]
                    nv = dst.shape[1]
                    a = nc.scalar.activation(dst, bank(name)[:, nv * j:nv * j + nv], ACT.Identity, bias=bias)
                a.then_inc(*scalar.does("emptied " + name, f"col {kind} {l}.{i}"))

            def mod_rows(at):
                if mod_at[at]:
                    for n in range(len(mod_at[at]) + 1):
                        mod_row(at, n)

            def modulated(name, groups, shift, at=None):
                more = len(mod_at[at]) + 1 if at else 0
                for k in range(KT):
                    if k < more:
                        mod_row(at, k)
                    act.wait_ge(*vector.did(f"normed {name}.{k}"))
                    for g in groups:
                        a = nc.scalar.activation(h_hi[:, k, S * g:S * g + S], dve_t[k % 4][:, S * g:S * g + S],
                                                 ACT.Identity, bias=shift(k, g))
                    a.then_inc(*scalar.does(f"hi {name}.{k}"))
                assert more <= KT

            act.wait_ge(params_landed, 16)
            nc.scalar.activation(small[:, 32:56], param("c_vec"), ACT.Silu).then_inc(*scalar.does("csil"))
            at = PARAM_AT["decay"][0]
            both = params[:, at:at + 24]
            nc.scalar.activation(lp[0], both, ACT.Abs).then_inc(*scalar.does("lp abs"))
            act.wait_ge(*scalar.did("lp abs"))
            nc.scalar.activation(lp[1], lp[0], ACT.Exp, scale=-1.0).then_inc(*scalar.does("lp exp"))

            for l in range(2):
                nx = 2 * S if l == 0 else S
                groups = (0, 1) if l == 0 else (0,)
                if l == 0:
                    for n in range(4):
                        mod_row("start", n)
                    act.wait_ge(x_landed, 32)
                    act.wait_ge(tables_landed, 16)
                    square_all("n1 0", 2 * S, KT, lambda k: xT[:, k, :], None,
                               lambda k: mod_row("start", 4) if k == 3 else None)
                    deviation("n1 0", 2 * S, D)
                    for n in range(5, len(mod_at["start"]) + 1):
                        if n == len(mod_at["start"]):
                            first_units("sc_c 0.0")
                        mod_row("start", n)
                else:
                    first_units("sc_c 1.0")
                    square_all("n1 1", 2 * S, KT, lambda k: xT[:, k, :], lambda k: vector.did(f"x out 0.{k}"))
                    deviation("n1 1", 2 * S, D)
                modulated(f"n1 {l}", (0, 1), lambda k, g: mod1[l][:, k, g:g + 1], "n1 1" if l else None)
                if l == 0:
                    act.wait_ge(*vector.did("k_exps"))
                    nc.scalar.activation(small[:, 80:112], small[:, 80:112], ACT.Exp).then_inc(*scalar.does("k_decay"))
                for n in range(BT):
                    split_to(split_until(f"sc_c {l}.{n}"))
                    if n >= 2:
                        act.wait_ge(*vector.did(f"cx {l}.{n - 2}"))
                    evacuate(f"sc_c {l}.{n}", act_t[n % 2][:, 0:nx], also=[f"sc_c {l}.{n}"])
                for n in range(BT):
                    split_to(split_until(f"cf_g {l}.{n}"))
                    if n >= 2:
                        act.wait_ge(*vector.did(f"u {l}.{n - 2}"))
                    evacuate(f"cf_g {l}.{n}", act_t[2 + n % 2][:, 0:nx], ACT.Sigmoid, [f"cf_g {l}.{n}"])
                for n in range(BT):
                    projected(f"ret_q {l}.{n}", ret_q[:, n, 0:nx], also=[f"ret_q {l}.{n}"])
                for n in range(BT):
                    projected(f"ret_k {l}.{n}", ret_k[:, n, :], also=[f"ret_k {l}.{n}"], scale=K_SCALE)
                act.wait_ge(*vector.did(f"cx {l}.{BT - 1}"))

                def turned_v(n):
                    evacuate(f"turned ret_v {l}.{n}", ret_v[:, :, P * n:P * n + P], also=[f"ret_v {l}.{n}"])

                for n in range(BT):
                    projected(f"ret_v {l}.{n}", act_t[n % 2][:], also=[f"rows ret_v {l}.{n}"])
                    if n:
                        turned_v(n - 1)
                for n in range(BT):
                    projected(f"att_q {l}.{n}", att_q[:, n, 0:nx], also=[f"att_q {l}.{n}"])
                    if n == 0:
                        turned_v(BT - 1)
                projected(f"att_k {l}", att_k, also=[f"att_k {l}"])
                projected(f"att_v {l}", act_t[0][:], also=[f"rows att_v {l}"])
                split_to(split_until(f"sc_b {l}.0"))
                evacuate(f"turned att_v {l}", att_v, also=[f"att_v {l}"])
                for n in range(BT):
                    split_to(split_until(f"sc_z {l}.{n}"))
                    if n >= 2:
                        act.wait_ge(*vector.did(f"branch {l}.sc.{n - 2}"))
                    evacuate(f"sc_z {l}.{n}", act_t[n % 2][:, 0:nx], ACT.Silu, [f"sc_z {l}.{n}"])

                for hd in range(HEADS):
                    evacuate(f"state {l}.{hd}", state[:, hd, :, :], also=[f"state {l}.{hd}"])
                units = [(hd, g) for hd in range(HEADS) for g in groups]

                def ret_evacuate(hd, g):
                    evacuate(f"ro {l}.{hd}.{g}", ret_o[:, hd, S * g:S * g + S], also=[f"ret_o {l}.{hd}.{g}"])

                for n, (hd, g) in enumerate(units):
                    if g == 0:
                        if hd >= 2:
                            act.wait_ge(*vector.did(f"q_wt {l}.{hd - 2}"))
                        for d in range(2):
                            a = nc.scalar.activation(act_t[hd % 2][:, S * d:S * d + S],
                                                     table("q_pos")[:, S * d:S * d + S], ACT.Exp,
                                                     scale=log_g[:, l, d, hd:hd + 1])
                        a.then_inc(*scalar.does(f"q_dec {l}.{hd}"))
                        act.wait_ge(*vector.did(f"expo {l}.{hd}"))
                        nc.scalar.activation(act_t[2 + hd % 2][:], stat2[:], ACT.Exp)\
                            .then_inc(*scalar.does(f"decay {l}.{hd}"))
                    if n:
                        ret_evacuate(*units[n - 1])
                ret_evacuate(*units[-1])

                att = [(g, t, q) for g in groups for t in range(BT) for q in range(ST)]

                def att_turned(i):
                    nb = 4 - 2 * att[i][0]
                    for s in range(2):
                        if i >= 1:
                            act.wait_ge(*tensor.did(f"filled ao {l}.{i - 1}"))
                        evacuate(f"at {l}.{i}.{s}", act_t[2 + s][:, 0:P * nb], also=[f"att_t {l}.{i}.{s}"])

                def gate_of(i):
                    every = len(att) // (2 * BT)
                    n = i // every
                    return (("ret", "att")[n // BT], l, n % BT) if i % every == 0 and n < 2 * BT else None

                first_units(f"ret_z {l}.0")
                for i in range(len(att) + 1):
                    if i < len(att):
                        g, t, q = att[i]
                        n = 2 * S - S * g
                        o = 2 * (i % 2)
                        act.wait_ge(*vector.did(f"att_m {l}.{i}"))
                        for s in range(2):
                            if i >= 2:
                                act.wait_ge(*vector.did(f"att_p {l}.{i - 2}.{s}"))
                            name = f"as {l}.{i}.{s}"
                            nc.scalar.activation(exps[o + s][:, 0:n], bank(name)[:, 0:n], ACT.Exp, scale=ATT_SCALE,
                                                 bias=soft_m[:, o + s:o + s + 1], accum_out=soft_s[:, o + s:o + s + 1])\
                                .then_inc(*scalar.does(f"att_e {l}.{i}.{s}", "emptied " + name))
                        act.wait_ge(*vector.did(f"att_sk {l}.{i}"))
                        nc.scalar.activation(soft_e[:, o:o + 2], soft_d[:, o:o + 2], ACT.Exp)\
                            .then_inc(*scalar.does(f"att_se {l}.{i}"))
                    if gate_of(i):
                        a, _, n = gate_of(i)
                        projected(f"{a}_z {l}.{n}", z_sil[a][:, n, 0:nx], also=[f"{a}_z raw {l}.{n}"])
                    if i >= 1:
                        att_turned(i - 1)

                def gates(a, ns):
                    for n in ns:
                        projected(f"{a}_z {l}.{n}", z_sil[a][:, n, 0:nx], ACT.Silu, [f"{a}_z {l}.{n}"])

                def high_parts(b):
                    for t in range(BT):
                        act.wait_ge(*vector.did(f"branch {l}.{b}.{t}"))
                        nc.scalar.activation(branch_hi[:, t, 0:nx], branch[b][:, t, 0:nx], ACT.Copy)\
                            .then_inc(*scalar.does(f"hi br {l}.{b}.{t}"))

                high_parts(MERGE_ORDER[0])
                split_to(split_until(f"att_z {l}.{BT - 1}"))
                for hd in range(HEADS):
                    act.wait_ge(*vector.did(f"gd {l}.{hd}"))
                    nc.scalar.activation(act_t[hd][:, 0:nx], ret_o[:, hd, 0:nx], ACT.Square)\
                        .then_inc(*scalar.does(f"sq gv {l}.{hd}"))
                gates("cf", range(2))
                for hd in range(HEADS):
                    name = f"gv {l}.{hd}"
                    evacuate(name, act_t[hd][:, 0:nx], ACT.Sqrt, [f"dev {name}"], scale=1.0 / P, bias=eps)
                for k in range(BT):
                    act.wait_ge(*vector.did(f"rinv gv {l}.{k}"))
                    act.wait_ge(*vector.did(f"ld {l}.{k}"))
                    nc.scalar.activation(act_t[k][:, 0:nx], f_br[:, k, 0:nx], ACT.Square)\
                        .then_inc(*scalar.does(f"sq lv {l}.{k}"))
                gates("cf", range(2, BT))
                deviation(f"lv {l}", nx, BW)
                for a in ("ret", "att"):
                    for n in range(BT):
                        act.wait_ge(*scalar.did(f"{a}_z raw {l}.{n}"))
                        nc.scalar.activation(z_sil[a][:, n, 0:nx], z_sil[a][:, n, 0:nx], ACT.Silu)\
                            .then_inc(*scalar.does(f"{a}_z {l}.{n}"))
                for n in range(BT):
                    act.wait_ge(*vector.did(f"ln {l}.{n}"))
                    nc.scalar.activation(f_br[:, n, 0:nx], f_br[:, n, 0:nx], ACT.Silu,
                                         scale=param("ln_w", 2)[:, l, n:n + 1], bias=param("ln_b", 2)[:, l, n:n + 1])\
                        .then_inc(*scalar.does(f"ln {l}.{n}"))
                m = 0
                for b in MERGE_ORDER:
                    if b != MERGE_ORDER[0]:
                        act.wait_ge(*tensor.did(f"filled br {l}.{MERGE_ORDER[MERGE_ORDER.index(b) - 1]}.{KT - 1}"))
                        high_parts(b)
                    for n in range(KT):
                        if n % 2 == 0:
                            for acc in pair_before(l, b, n // 2):
                                mod_cols(acc)
                        split_to(split_until(f"gate {l}.{b}.{n}"))
                        if m >= 4:
                            act.wait_ge(*vector.did(f"gated {l}.{m - 4}"))
                        evacuate(f"gate {l}.{b}.{n}", act_t[m % 4][:, 0:nx], ACT.Sigmoid, [f"gate {l}.{m}"])
                        m += 1
                        if n % 2:
                            split_to(split_until(f"br {l}.{b}.{n}"))

                for acc in merge_mods[l][-1]:
                    mod_cols(acc)
                act.wait_ge(*tensor.did(f"filled gate {l}.{MERGE_ORDER[-1]}.{KT - 1}"))
                for k in range(KT):
                    act.wait_ge(*vector.did(f"merged {l}.{MERGE_ORDER[-1]}.{k}"))
                    nc.scalar.activation(h_hi[:, k, out_at(l):out_at(l) + nx], merged[:, k, 0:nx], ACT.Copy)\
                        .then_inc(*scalar.does(f"hi merged {l}.{k}"))
                for n in range(KT):
                    split_to(split_until(f"out {l}.{n}"))

            warm_sqrt("fin")
            square_all("fin", S, KT, lambda k: xT[:, k, 0:S], lambda k: vector.did(f"x out 1.{k}"))
            deviation("fin", S, D)
            mod_rows("fin")

            def pre_norm(name, ready, l, q, first, at=None):
                first_units(first)
                if name in ("n2 1", "n3 0", "n3 1"):
                    warm_sqrt(name)
                square_all(name, S, KT, lambda k: xT[:, k, 0:S], ready)
                deviation(name, S, D)
                modulated(name, (0,), lambda k, g: mod2[l][:, 12 * q + k:12 * q + k + 1], at)

            def store_y(tag, k):
                name = f"y {tag}.{k}"
                act.wait_ge(*tensor.did("filled " + name))
                nc.scalar.activation(yT[:, k, :], bank(name)[:, 0:S], ACT.Copy)
                nc.scalar.activation(sq8[:, k, :], bank(name)[:, 0:S], ACT.Square)\
                    .then_inc(*scalar.does(name, "emptied " + name))

            def block_out(tag, src, ready):
                first_units(f"y {tag}.0")
                for n in range(KT):
                    act.wait_ge(*vector.did(f"{ready} {n}"))
                    nc.scalar.activation(h_hi[:, n, S:2 * S], src[:, n, :], ACT.Copy).then_inc(*scalar.does(f"hi {tag}.{n}"))
                warm_sqrt(tag)
                for n in range(KT):
                    split_to(split_until(f"y {tag}.{n}"))
                    store_y(tag, n)
                deviation(f"ys {tag}", S, D)

            def ffn(l, ready):
                pre_norm(f"n3 {l}", ready, l, 2, f"ffg {l}.0", None if l else "n3 0")
                fw, fb = param("ff_w", 2, FF_K), param("ff_b", 2)
                m = 0
                for i in range(11):
                    for nm in ("ffg", "ffv"):
                        for j in range(2):
                            n = 2 * i + j
                            c = n + (FT if nm == "ffv" else 0)
                            name = f"{nm} {l}.{n}"
                            split_to(split_until(name))
                            if m >= 4:
                                act.wait_ge(*vector.did(f"ff_free {l}.{m - 4}"))
                            evacuate(name, act_t[m % 4][:, 0:S], ACT.Identity, [f"tap {name}"], last=False,
                                     scale=fw[:, l, FF_K - 1, c:c + 1], bias=fb[:, l, c:c + 1])
                            m += 1
                    for j in range(2):
                        n = 2 * i + j
                        act.wait_ge(*vector.did(f"conv ffg {l}.{n}"))
                        if n >= 4:
                            act.wait_ge(*vector.did(f"ff_act {l}.{n - 4}"))
                        nc.scalar.activation(act_t[n % 4][:, S:2 * S], dve_t[n % 4][:, 0:S], ACT.Gelu_apprx_tanh)\
                            .then_inc(*scalar.does(f"gelu {l}.{n}"))
                    for n in (2 * i - 2, 2 * i - 1):
                        if 0 <= n < KT:
                            ff_high(l, n)
                warm_sqrt(f"ffn {l}")
                act.wait_ge(*tensor.did(f"filled ffv {l}.{FT - 1}"))
                for n in range(KT, FT):
                    ff_high(l, n)
                for c in range(4):
                    for k0 in range(0, FT, 8):
                        split_to(unit_of[f"down {l}.{c}.{k0}.1"])
                    if c < 3:
                        split_to(unit_of[f"down {l}.{c + 1}.0.1"])
                    for j in range(2):
                        store_y(f"ffn {l}", 2 * c + j)
                deviation(f"ys ffn {l}", S, D)

            def ff_high(l, n):
                act.wait_ge(*vector.did(f"ff_act {l}.{n}"))
                nc.scalar.activation(ff_part(h_hi, n), ff_act[:, n, :], ACT.Copy).then_inc(*scalar.does(f"hi ff {l}.{n}"))

            pre_norm("n2 0", lambda k: vector.did(f"x fin.{k}"), 0, 0, "rgx 0", "n2 0")
            for n in range(KT):
                projected(f"rgx {n}", xb_pad[:, n, RG_K - 1:], also=[f"xb {n}"])
            def gel_out(n):
                projected(f"rgg {n}", gel[:, n, :], ACT.Gelu_apprx_tanh, [f"gel {n}"])

            for n in range(2):
                gel_out(n)
            for n in range(KT):
                evacuate(f"rga {n}", rr[:, n, :], ACT.Sigmoid, [f"rr {n}"], bias=param("rg_ba")[:, n:n + 1])
            for n in range(KT):
                evacuate(f"rgx2 {n}", ix[:, n, :], ACT.Sigmoid, [f"ig {n}"], bias=param("rg_bx")[:, n:n + 1])
            for n in range(KT):
                nc.scalar.activation(tt_[:, n, :], rr[:, n, :], ACT.Tanh, scale=lam8[:, n:n + 1])
                nc.scalar.activation(rr[:, n, :], rr[:, n, :], ACT.Exp, scale=lam8n[:, n:n + 1])\
                    .then_inc(*scalar.does(f"a {n}"))
                if n % 2 == 0:
                    split_to(unit_of["rgg 4"] + n // 2)
            for n in range(KT):
                act.wait_ge(*vector.did(f"one_a2 {n}"))
                nc.scalar.activation(tt_[:, n, :], tt_[:, n, :], ACT.Sqrt).then_inc(*scalar.does(f"mult {n}"))
            for n in range(2, KT):
                gel_out(n)
            mod_rows("rg")
            block_out("rg", xc, "rg_y")
            mod_rows("post rg")
            ffn(0, lambda k: vector.did(f"x rg.{k}"))

            pre_norm("n2 1", lambda k: vector.did(f"x ffn 0.{k}"), 1, 0, "glaq 0")
            split_to(split_until("glaq 0"))
            evacuate("gla z", zT[0:16, :], also=["zT"])
            for hd in range(GLA_H):
                evacuate(f"alpha {hd}", le[:, hd, :], ACT.Abs, [f"le {hd}"], last=False,
                         bias=param("gla_b")[:, hd:hd + 1])
            for hd in range(GLA_H):
                act.wait_ge(*scalar.did(f"le {hd}"))
                nc.scalar.activation(le[:, hd, :], le[:, hd, :], ACT.Exp, scale=-1.0)\
                    .then_inc(*scalar.does(f"le2 {hd}"))
            for hd in range(GLA_H):
                act.wait_ge(*scalar.did(f"le2 {hd}"))
                nc.scalar.activation(le[:, hd, :], le[:, hd, :], ACT.Ln, bias=ones[:, 0:1])\
                    .then_inc(*scalar.does(f"le3 {hd}"))
            for n in range(GLA_H):
                projected(f"glaq {n}", gq[:, n, :], also=[f"gq {n}"], scale=GLA_DK ** -0.5)
            for n in range(GLA_H):
                projected(f"glak {n}", gk[:, n, :], also=[f"gk {n}"])
            for i in range(8):
                projected(f"glav {i}", act_t[i % 2][:, 0:S], also=[f"rows glav {i}"])
                if i:
                    evacuate(f"turned glav {i - 1}", gv[:, :, P * i - P:P * i], also=[f"gv {i - 1}"])
                j = (7 + i) % 8
                act.wait_ge(*vector.did(f"ldiff {j}"))
                nc.scalar.activation(lv[:, j, :], lv[:, j, :], ACT.Exp, scale=1.0 / 16.0)\
                    .then_inc(*scalar.does(f"lexp {j}"))
            evacuate(f"turned glav {KT - 1}", gv[:, :, D - P:D], also=[f"gv {KT - 1}"])
            def r_out(n):
                projected(f"glar {n}", r_sil[:, n, :], ACT.Silu, [f"r_sil {n}"])

            for n in range(GLA_H * ST):
                if n % 2:
                    evacuate(f"cross {n // 2}", attT[:, n // 2, 0, P:S], also=[f"cross {n // 2}"])
                else:
                    r_out(n // 2)
            warm_sqrt("gs")
            for n in range(KT):
                name = f"go {n}"
                act.wait_ge(*tensor.did("filled " + name))
                nc.scalar.activation(gla_o[:, n, :], bank(name)[:, 0:S], ACT.Copy)
                nc.scalar.activation(sq8[:, n, :], bank(name)[:, 0:S], ACT.Square)\
                    .then_inc(*scalar.does(name, "emptied " + name))
            for hd in range(GLA_H):
                evacuate(f"gs {hd}", act_t[hd][:, 0:S], ACT.Sqrt, [f"dev gs {hd}"], scale=1.0 / (2 * P), bias=eps)
            for n in range(KT // 2, KT):
                r_out(n)
            block_out("gla", gla_o, "gla_y")
            ffn(1, lambda k: vector.did(f"x gla.{k}"))

        @block.vector
        def _(dve):
            def step(ins, *names):
                ins.then_inc(*vector.does(*names))

            def after(name):
                dve.wait_ge(*vector.did(name))

            def filled(name):
                dve.wait_ge(*tensor.did("filled " + name))

            def settled():
                dve.wait_ge(vector.sem, vector.n)

            def inverse(name, n):
                settled()
                dve.wait_ge(*scalar.did(f"dev {name}"))
                step(nc.vector.reciprocal(stat2[:, 0:n], stat[:, 0:n]), f"rinv {name}")
                after(f"rinv {name}")

            def normed(name, groups, gain, shift):
                for k in range(KT + 2):
                    if k < KT:
                        if k >= 4:
                            after(f"lo {name}.{k - 4}")
                        for g in groups:
                            sl = slice(S * g, S * g + S)
                            ins = nc.vector.scalar_tensor_tensor(dve_t[k % 4][:, sl], xT[:, k, sl], gain(k, g),
                                                                 stat2[:, sl], ALU.mult, ALU.mult)
                            step(ins, *([f"normed {name}.{k}"] if g == groups[-1] else []))
                    if k >= 2:
                        i = k - 2
                        dve.wait_ge(*scalar.did(f"hi {name}.{i}"))
                        after(f"normed {name}.{i}")
                        for g in groups:
                            sl = slice(S * g, S * g + S)
                            ins = nc.vector.scalar_tensor_tensor(h_lo[:, i, sl], dve_t[i % 4][:, sl], shift(i, g),
                                                                 h_hi[:, i, sl].bitcast(F32), ALU.add, ALU.subtract)
                            step(ins, *([f"lo {name}.{i}"] if g == groups[-1] else []))

            def normed2(name, l, q):
                inverse(name, S)
                normed(name, (0,), lambda k, g: gain2[l][:, q, k:k + 1],
                       lambda k, g: mod2[l][:, 12 * q + k:12 * q + k + 1])

            fed = dict(n=0)

            def split_to(last):
                while fed["n"] <= last:
                    u = fed["n"]
                    n, half, _ = w_units[u]
                    dve.wait_ge(*scalar.did(f"hi {u}"))
                    if u >= PARTS:
                        dve.wait_ge(*tensor.did(f"used unit {u - PARTS}"))
                    src = slot_of(n)[:, :, P * half:P * half + P]
                    nk = src.shape[1]
                    step(nc.vector.tensor_tensor(w_lo[u % PARTS][:, 0:nk, :], src,
                                                 w_hi[u % PARTS][:, 0:nk, :].bitcast(F32), ALU.subtract),
                         f"lo {u}", *(["used " + stream[n][0]] if half else []))
                    fed["n"] += 1

            def low_part(name, dst, src, hi):
                dve.wait_ge(*scalar.did("hi " + name))
                step(nc.vector.tensor_tensor(dst, src, hi.bitcast(F32), ALU.subtract), "lo " + name)

            def split_for(tile):
                split_to(split_until(tile))

            def first_units(tile):
                split_to(unit_of[tile] + 1)

            def bcast(ap, n):
                return ap.unsqueeze(2).broadcast_to([ap.shape[0], ap.shape[1], n])

            dve.wait_ge(params_landed, 16)
            dve.wait_ge(tables_landed, 16)
            at = PARAM_AT["decay"][0]
            both = params[:, at:at + 24]
            dve.wait_ge(*scalar.did("lp exp"))
            step(nc.vector.tensor_scalar(lp[0], lp[1], 2.0, None, ALU.add), "lp0")
            after("lp0")
            step(nc.vector.reciprocal(lp[2], lp[0]), "lp1")
            after("lp1")
            step(nc.vector.tensor_tensor(lp[1], lp[1], lp[2], ALU.mult), "lp2")
            after("lp2")
            step(nc.vector.tensor_tensor(lp[2], lp[1], lp[1], ALU.mult), "lp3")
            after("lp3")
            step(nc.vector.tensor_scalar(lp[3], lp[2], 1.0 / 15, 1.0 / 13, ALU.mult, ALU.add), "lp4")
            for i, d in enumerate((11, 9, 7, 5, 3, 1)):
                after(f"lp{4 + 2 * i}")
                step(nc.vector.tensor_tensor(lp[3], lp[3], lp[2], ALU.mult), f"lp{5 + 2 * i}")
                after(f"lp{5 + 2 * i}")
                step(nc.vector.tensor_scalar(lp[3], lp[3], 1.0 / d, None, ALU.add), f"lp{6 + 2 * i}")
            after("lp16")
            step(nc.vector.scalar_tensor_tensor(lp[3], lp[1], 2.0, lp[3], ALU.mult, ALU.mult), "lp17")
            step(nc.vector.tensor_scalar(lp[0], both, -1.0, 0.0, ALU.mult, ALU.max), "lp18")
            after("lp18")
            step(nc.vector.tensor_tensor(soft_p, lp[0], lp[3], ALU.add), "soft_p")
            after("soft_p")
            step(nc.vector.tensor_scalar(small[:, 224:240], soft_p[:, 0:16], -1.0, None, ALU.mult), "log_g")
            step(nc.vector.tensor_scalar(lam8, soft_p[:, 16:24], 8.0, None, ALU.mult), "lam8")
            step(nc.vector.tensor_scalar(lam8n, soft_p[:, 16:24], -8.0, None, ALU.mult), "lam8n")
            step(nc.vector.tensor_scalar(small[:, 112:128], param("sink"), -1.0, None, ALU.mult), "nsink")
            after("log_g")
            for l in range(2):
                for d in range(2):
                    for t in range(ST):
                        ins = nc.vector.tensor_scalar(k_decay[:, l, d, t, :], log_g[:, l, d, :],
                                                      table("k_pos")[:, 2 * d + t:2 * d + t + 1], None, ALU.mult)
                        step(ins, *(["k_exps"] if (l, d, t) == (1, 1, 1) else []))

            def mod_accumulate(m):
                kind, l, i = m
                name = f"{kind} {l}.{i}"
                w, acc = acc_slot(m), acc_of(m)
                dve.wait_ge(*acc_slab_landed(m))
                at = acc_order.index(m)
                if at >= 2:
                    filled("sum %s %d.%d" % acc_order[at - 2])
                todo = [(k, c, c) for k in range(KT) for c in range(2)] if kind == "mod" else \
                    [(k, k % 2, 2) for k in range(KT)]
                before = {}
                for k, c, v in todo:
                    dst, src, scale = acc[:, 2 * P * c:2 * P * c + 2 * P], w[:, k, :], csil[:, k, v:v + 1]
                    done = [f"acc {name}.{k}.{c}"]
                    if (k, c, v) == todo[-1]:
                        done += ["acc used " + name] + (["acc " + name] if kind == "mod" else [])
                    if c in before:
                        after(before[c])
                        step(nc.vector.scalar_tensor_tensor(dst, src, scale, dst, ALU.mult, ALU.add), *done)
                    else:
                        step(nc.vector.tensor_scalar(dst, src, scale, None, ALU.mult), *done)
                    before[c] = done[0]
                if kind == "ada":
                    after(before[0])
                    after(before[1])
                    step(nc.vector.tensor_tensor(acc[:, 0:2 * P], acc[:, 0:2 * P], acc[:, 2 * P:4 * P], ALU.add), "acc " + name)

            def modulation1(l):
                dve.wait_ge(*scalar.did(f"col mod {l}.7"))
                step(nc.vector.scalar_tensor_tensor(gain1[l], mod1[l][:, 8:16, :], 1.0,
                                                    bcast(param("norm_w", 2)[:, l, :], 2), ALU.add, ALU.mult),
                     f"gain1 {l}")

            def modulation2(l):
                dve.wait_ge(*scalar.did(f"col ada {l}.23"))
                g = param("norm_g", 2, 4)
                for q in range(2):
                    c = 24 * q
                    step(nc.vector.scalar_tensor_tensor(gain2[l][:, 2 * q, :], mod2[l][:, c + 8:c + 16], 1.0,
                                                        g[:, l, 2 * q, :], ALU.add, ALU.mult))
                    step(nc.vector.tensor_tensor(gain2[l][:, 2 * q + 1, :], mod2[l][:, c + 16:c + 24],
                                                 g[:, l, 2 * q + 1, :], ALU.mult), *([f"gain2 {l}"] if q else []))

            dve.wait_ge(x_landed, 32)
            for l in range(2):
                nx = 2 * S if l == 0 else S
                groups = (0, 1) if l == 0 else (0,)
                ng = len(groups)
                settled()
                if l:
                    first_units(f"sc_c {l}.0")
                inverse(f"n1 {l}", 2 * S)
                if l == 0:
                    first_units(f"sc_c {l}.0")
                modulation1(l)
                step(nc.vector.memset(cx[:, :, 0:ng, 0:1], 0.0), f"cx z0 {l}")
                step(nc.vector.memset(cx[:, :, 0:ng, S + 1:S + 2], 0.0), f"cx z1 {l}")
                after(f"gain1 {l}")
                normed(f"n1 {l}", (0, 1), lambda k, g: gain1[l][:, k, g:g + 1], lambda k, g: mod1[l][:, k, g:g + 1])

                def grouped(ap):
                    return ap.rearrange("p (g s) -> p g s", g=ng)

                settled()
                for n in range(BT):
                    split_for(f"sc_x {l}.{n}")
                    dve.wait_ge(*scalar.did(f"sc_c {l}.{n}"))
                    name = f"sc_x {l}.{n}"
                    filled(name)
                    step(nc.vector.tensor_tensor(cx[:, n, 0:ng, 1:S + 1], grouped(bank(name)[:, 0:nx]),
                                                 grouped(act_t[n % 2][:, 0:nx]), ALU.mult),
                         f"cx {l}.{n}", "emptied " + name)
                sw = param("sc_w", 2, SC_K)
                for k in range(SC_K):
                    for n in range(BT):
                        src, dst = cx[:, n, 0:ng, k:k + S], grouped(s_br[:, n, 0:nx])
                        if k == 0:
                            after(f"cx {l}.{n}")
                            step(nc.vector.tensor_scalar(dst, src, sw[:, l, k, n:n + 1], None, ALU.mult),
                                 f"sc {l}.{n}.{k}")
                        else:
                            after(f"sc {l}.{n}.{k - 1}")
                            step(nc.vector.scalar_tensor_tensor(dst, src, sw[:, l, k, n:n + 1], dst, ALU.mult, ALU.add),
                                 f"sc {l}.{n}.{k}")
                settled()
                step(nc.vector.memset(u_pad[:, :, 0:ng, 0:PAD], 0.0), f"u z0 {l}")
                step(nc.vector.memset(u_pad[:, :, 0:ng, PAD + S:], 0.0), f"u z1 {l}")
                for n in range(BT):
                    split_for(f"cf_a {l}.{n}")
                    dve.wait_ge(*scalar.did(f"cf_g {l}.{n}"))
                    name = f"cf_a {l}.{n}"
                    filled(name)
                    step(nc.vector.tensor_tensor(u_pad[:, n, 0:ng, PAD:PAD + S], grouped(bank(name)[:, 0:nx]),
                                                 grouped(act_t[2 + n % 2][:, 0:nx]), ALU.mult),
                         f"u {l}.{n}", "emptied " + name)
                cw, cb = param("cf_w", 2, CF_K), param("cf_b", 2)
                after(f"u z1 {l}")
                for k in range(CF_K):
                    for n in range(BT):
                        if (BT * k + n) % 6 == 5:
                            split_to(min(fed["n"], unit_of[f"sc_z {l}.0"]))
                        src, dst = u_pad[:, n, 0:ng, k:k + S], grouped(f_br[:, n, 0:nx])
                        name = f"cf {l}.{n}.{k}" if k < CF_K - 1 else f"conv {l}.{n}"
                        if k == 0:
                            after(f"u {l}.{n}")
                            step(nc.vector.tensor_scalar(dst, src, cw[:, l, k, n:n + 1], cb[:, l, n:n + 1],
                                                         ALU.mult, ALU.add), name)
                        else:
                            after(f"cf {l}.{n}.{k - 1}")
                            step(nc.vector.scalar_tensor_tensor(dst, src, cw[:, l, k, n:n + 1], dst, ALU.mult, ALU.add),
                                 name)
                settled()
                for n in range(BT):
                    name = f"sc_b {l}.{n}"
                    split_for(f"sc_z {l}.{n}")
                    filled(name)
                    step(nc.vector.tensor_tensor(s_br[:, n, 0:nx], bank(name)[:, 0:nx], s_br[:, n, 0:nx], ALU.mult),
                         f"sb {l}.{n}", "emptied " + name)
                    dve.wait_ge(*scalar.did(f"sc_z {l}.{n}"))
                    after(f"sb {l}.{n}")
                    step(nc.vector.tensor_tensor(s_br[:, n, 0:nx], s_br[:, n, 0:nx], act_t[n % 2][:, 0:nx], ALU.mult),
                         f"branch {l}.sc.{n}")
                settled()
                dve.wait_ge(*scalar.did("k_decay"))
                for t in range(ST):
                    name = f"kT {l}.{t}"
                    filled(name)
                    for d in range(2):
                        step(nc.vector.tensor_tensor(k_wt[d][:, t, :, :], bank(name)[:].rearrange("p (h n) -> p h n", h=HEADS),
                                                     bcast(k_decay[:, l, d, t, :], P), ALU.mult),
                             f"k_wt {l}.{t}.{d}", *(["emptied " + name] if d else []))
                settled()
                for t in range(BT + 1):
                    q = att_q[:, t, 0:S] if t < BT else att_k[:, 0:S]
                    name = f"turn {l}.{t}"
                    filled(name)
                    if t >= 2:
                        after(f"roped {l}.{t - 2}")
                    step(nc.vector.tensor_tensor(dve_t[t % 2][:, 0:S], bank(name)[:, 0:S], table("sin"), ALU.mult),
                         f"rope0 {l}.{t}", "emptied " + name)
                    step(nc.vector.tensor_tensor(q, q, table("cos"), ALU.mult), f"rope1 {l}.{t}")
                    after(f"rope1 {l}.{t}")
                    step(nc.vector.tensor_tensor(q, q, dve_t[t % 2][:, 0:S], ALU.add),
                         f"roped {l}.{t}", *([f"att_q roped {l}.{t}"] if t < BT else []))
                after(f"roped {l}.{BT}")
                step(nc.vector.tensor_copy(att_ks[0:64, :], att_k[64:P, :]))
                step(nc.vector.tensor_copy(att_ks[64:P, :], att_k[0:64, :]), f"att_ks {l}")

                units = [(hd, g) for hd in range(HEADS) for g in groups]
                for n, (hd, g) in enumerate(units):
                    if g == 0:
                        if hd:
                            dve.wait_ge(*scalar.did(f"decay {l}.{hd - 1}"))
                        step(nc.vector.tensor_scalar(stat2[:], table("ahead"), log_g[:, l, 1, hd:hd + 1], None, ALU.mult),
                             f"expo0 {l}.{hd}")
                        after(f"expo0 {l}.{hd}")
                        step(nc.vector.scalar_tensor_tensor(stat2[:], table("behind"), log_g[:, l, 0, hd:hd + 1], stat2[:],
                                                            ALU.mult, ALU.add), f"expo {l}.{hd}")
                        dve.wait_ge(*scalar.did(f"q_dec {l}.{hd}"))
                        if hd >= 2:
                            dve.wait_ge(*tensor.did(f"filled ro {l}.{hd - 2}.0"))
                        dve.wait_ge(*scalar.did(f"ret_q {l}.{hd}"))
                        for d in range(2):
                            ins = nc.vector.tensor_tensor(dve_t[hd % 2][:, S * d:S * d + S], ret_q[:, hd, 0:S],
                                                          act_t[hd % 2][:, S * d:S * d + S], ALU.mult)
                            step(ins, *([f"q_wt {l}.{hd}"] if d else []))
                        dve.wait_ge(*scalar.did(f"decay {l}.{hd}"))
                    name = f"rs {l}.{hd}.{g}"
                    filled(name)
                    if n >= 2:
                        dve.wait_ge(*tensor.did("filled ro %d.%d.%d" % (l, *units[n - 2])))
                    step(nc.vector.tensor_tensor(dve_t[2 + n % 2][:], bank(name)[:], act_t[2 + hd % 2][:], ALU.mult),
                         f"ret_p {l}.{hd}.{g}", "emptied " + name)

                settled()
                att = [(g, t, q) for g in groups for t in range(BT) for q in range(ST)]

                def att_max(i):
                    g, t, q = att[i]
                    o = 2 * (i % 2)
                    for s in range(2):
                        name = f"as {l}.{i}.{s}"
                        filled(name)
                        if g == 0:
                            c = P * (1 - q)
                            step(nc.vector.tensor_tensor(bank(name)[:, c:c + P], bank(name)[:, c:c + P],
                                                         table("band")[:, P * q:P * q + P], ALU.add), f"band {l}.{i}.{s}")
                    for s in range(2):
                        if g == 0:
                            after(f"band {l}.{i}.{s}")
                        step(nc.vector.tensor_reduce(soft_m[:, 4 + s:5 + s], bank(f"as {l}.{i}.{s}")[:, 0:2 * S - S * g],
                                                     AX_X, ALU.max), f"rowmax {l}.{i}.{s}")
                    after(f"rowmax {l}.{i}.1")
                    if i >= 2:
                        dve.wait_ge(*scalar.did(f"att_se {l}.{i - 2}"))
                    step(nc.vector.scalar_tensor_tensor(soft_m[:, o:o + 2], soft_m[:, 4:6], -ATT_SCALE,
                                                        nsink[:, l, 2 * t:2 * t + 2], ALU.mult, ALU.min), f"att_m {l}.{i}")
                    after(f"att_m {l}.{i}")
                    step(nc.vector.tensor_tensor(soft_d[:, o:o + 2], soft_m[:, o:o + 2],
                                                 param("sink", 2)[:, l, 2 * t:2 * t + 2], ALU.add), f"att_sk {l}.{i}")

                def att_weights(i):
                    g, t, q = att[i]
                    o = 2 * (i % 2)
                    n = 2 * S - S * g
                    dve.wait_ge(*scalar.did(f"att_se {l}.{i}"))
                    step(nc.vector.tensor_tensor(soft_s[:, 4:6], soft_s[:, o:o + 2], soft_e[:, o:o + 2], ALU.add),
                         f"att_d0 {l}.{i}")
                    after(f"att_d0 {l}.{i}")
                    if i:
                        after(f"att_p {l}.{i - 1}.1")
                    step(nc.vector.reciprocal(soft_e[:, 4:6], soft_s[:, 4:6]), f"att_d1 {l}.{i}")
                    after(f"att_d1 {l}.{i}")
                    for s in range(2):
                        if i >= 2:
                            dve.wait_ge(*tensor.did(f"filled at {l}.{i - 2}.{s}"))
                        step(nc.vector.tensor_scalar(dve_t[2 * (i % 2) + s][:, 0:n], exps[o + s][:, 0:n],
                                                     soft_e[:, 4 + s:5 + s], None, ALU.mult), f"att_p {l}.{i}.{s}")

                def att_store(i):
                    g, t, q = att[i]
                    name = f"ao {l}.{i}"
                    filled(name)
                    step(nc.vector.tensor_copy(att_o[:, t, S * g + P * q:S * g + P * q + P], bank(name)[:, 0:P]),
                         f"att_o {l}.{i}", "emptied " + name)

                dve.wait_ge(*tensor.did("filled ro %d.%d.%d" % (l, *units[-1])))
                first_units(f"ret_z {l}.0")
                every = len(att) // (2 * BT)
                for i in range(len(att) + 3):
                    if i < len(att):
                        att_max(i)
                        if i % every == 0:
                            n = i // every
                            split_for("%s_z %d.%d" % (("ret", "att")[n // BT], l, n % BT))
                    if 1 <= i <= len(att):
                        att_weights(i - 1)
                    if i >= 3:
                        att_store(i - 3)

                settled()
                split_for(f"att_z {l}.{BT - 1}")
                for hd in range(HEADS):
                    name = f"gm {l}.{hd}"
                    filled(name)
                    step(nc.vector.scalar_tensor_tensor(ret_o[:, hd, 0:nx], bank(name)[:, 0:nx], -1.0 / P,
                                                        ret_o[:, hd, 0:nx], ALU.mult, ALU.add),
                         f"gd {l}.{hd}", "emptied " + name)
                name = f"lm {l}"
                filled(name)
                for t in range(BT):
                    step(nc.vector.scalar_tensor_tensor(f_br[:, t, 0:nx], bank(name)[:, 0:nx], -1.0 / BW,
                                                        f_br[:, t, 0:nx], ALU.mult, ALU.add),
                         f"ld {l}.{t}", *(["emptied " + name] if t == BT - 1 else []))

                def gate_branch(a, n):
                    dve.wait_ge(*scalar.did(f"{a}_z {l}.{n}"))
                    step(nc.vector.tensor_tensor(branch[a][:, n, 0:nx], branch[a][:, n, 0:nx], z_sil[a][:, n, 0:nx],
                                                 ALU.mult), f"branch {l}.{a}.{n}")

                split_for(f"cf_z {l}.0")
                split_for(f"cf_z {l}.1")

                def low_parts(b):
                    for t in range(BT):
                        low_part(f"br {l}.{b}.{t}", branch_lo[b][:, t, 0:nx], branch[b][:, t, 0:nx],
                                 branch_hi[:, t, 0:nx])

                low_parts(MERGE_ORDER[0])
                for hd in range(HEADS):
                    dve.wait_ge(*scalar.did(f"dev gv {l}.{hd}"))
                    step(nc.vector.reciprocal(dve_t[hd][:, 0:nx], act_t[hd][:, 0:nx]), f"rinv gv {l}.{hd}")
                for hd in range(HEADS):
                    after(f"rinv gv {l}.{hd}")
                    step(nc.vector.scalar_tensor_tensor(ret_o[:, hd, 0:nx], ret_o[:, hd, 0:nx],
                                                        param("gn_w", 2)[:, l, hd:hd + 1], dve_t[hd][:, 0:nx],
                                                        ALU.mult, ALU.mult), f"gn {l}.{hd}")
                for n in range(2, BT):
                    split_for(f"cf_z {l}.{n}")
                inverse(f"lv {l}", nx)
                for t in range(BT):
                    step(nc.vector.tensor_tensor(f_br[:, t, 0:nx], f_br[:, t, 0:nx], stat2[:, 0:nx], ALU.mult),
                         f"ln {l}.{t}")
                for n in range(BT):
                    after(f"gn {l}.{n}")
                    gate_branch("ret", n)
                for n in range(BT):
                    gate_branch("att", n)
                split_for(f"gate {l}.{MERGE_ORDER[0]}.0")
                for n in range(BT):
                    dve.wait_ge(*scalar.did(f"ln {l}.{n}"))
                    gate_branch("cf", n)
                settled()
                m = 0
                for b in MERGE_ORDER:
                    for n in range(KT):
                        if n == 0 and b != MERGE_ORDER[0]:
                            low_parts(b)
                        if n % 2 == 0:
                            split_for(f"gate {l}.{b}.{n}")
                            for i, acc in enumerate(merge_mods[l][m // 2]):
                                mod_accumulate(acc)
                                if i == 0:
                                    split_for(f"gate {l}.{b}.{n + 1}")
                        split_for(f"br {l}.{b}.{n}")
                        dve.wait_ge(*scalar.did(f"gate {l}.{m}"))
                        name = f"br {l}.{b}.{n}"
                        filled(name)
                        if b == MERGE_ORDER[0]:
                            step(nc.vector.tensor_tensor(merged[:, n, 0:nx], bank(name)[:, 0:nx], act_t[m % 4][:, 0:nx],
                                                         ALU.mult), f"gated {l}.{m}", f"merged {l}.{b}.{n}", "emptied " + name)
                        else:
                            if m >= KT + 4:
                                after(f"added {l}.{m - 4}")
                            step(nc.vector.tensor_tensor(dve_t[m % 4][:, 0:nx], bank(name)[:, 0:nx], act_t[m % 4][:, 0:nx],
                                                         ALU.mult), f"gated {l}.{m}", "emptied " + name)
                            after(f"gated {l}.{m}")
                            after(f"merged {l}.{MERGE_ORDER[MERGE_ORDER.index(b) - 1]}.{n}")
                            step(nc.vector.tensor_tensor(merged[:, n, 0:nx], merged[:, n, 0:nx], dve_t[m % 4][:, 0:nx],
                                                         ALU.add), f"merged {l}.{b}.{n}", f"added {l}.{m}")
                        m += 1
                for k in range(KT):
                    low_part(f"merged {l}.{k}", h_lo[:, k, out_at(l):out_at(l) + nx], merged[:, k, 0:nx],
                             h_hi[:, k, out_at(l):out_at(l) + nx])
                dve.wait_ge(*scalar.did(f"col mod {l}.11"))
                for n in range(KT):
                    split_for(f"out {l}.{n}")
                    name = f"out {l}.{n}"
                    filled(name)
                    for g in groups:
                        sl = slice(S * g, S * g + S)
                        step(nc.vector.scalar_tensor_tensor(xT[:, n, sl], bank(name)[:, sl], mod1[l][:, 16 + n, g:g + 1],
                                                            xT[:, n, sl], ALU.mult, ALU.add),
                             *([f"x out {l}.{n}", "emptied " + name] if g == groups[-1] else []))

            inverse("fin", S)
            for k in range(KT):
                step(nc.vector.scalar_tensor_tensor(xT[:, k, 0:S], xT[:, k, 0:S], param("fin_w")[:, k:k + 1],
                                                    stat2[:, 0:S], ALU.mult, ALU.mult), f"x fin.{k}")

            def post(tag, l, q):
                inverse(f"ys {tag}", S)
                for n in range(KT + 1):
                    if n < KT:
                        step(nc.vector.scalar_tensor_tensor(yT[:, n, :], yT[:, n, :], gain2[l][:, q, n:n + 1],
                                                            stat2[:, 0:S], ALU.mult, ALU.mult), f"yn {tag}.{n}")
                    if n:
                        k = n - 1
                        after(f"yn {tag}.{k}")
                        step(nc.vector.tensor_tensor(xT[:, k, 0:S], xT[:, k, 0:S], yT[:, k, :], ALU.add), f"x {tag}.{k}")

            def block_parts(tag, src, l):
                first_units(f"y {tag}.0")
                for n in range(KT):
                    low_part(f"{tag}.{n}", h_lo[:, n, S:2 * S], src[:, n, :], h_hi[:, n, S:2 * S])
                split_to(unit_of[f"y {tag}.{KT - 1}"])
                post(tag, l, 1)

            def ffn(l):
                first_units(f"ffg {l}.0")
                normed2(f"n3 {l}", l, 2)
                settled()
                fw = param("ff_w", 2, FF_K)
                m = 0
                for i in range(11):
                    for nm in ("ffg", "ffv"):
                        for j in range(2):
                            n = 2 * i + j
                            c = n + (FT if nm == "ffv" else 0)
                            name = f"{nm} {l}.{n}"
                            split_for(name)
                            dve.wait_ge(*scalar.did(f"tap {name}"))
                            src, acc = bank(name), act_t[m % 4]
                            dst = dve_t[n % 4][:, 0:S] if nm == "ffg" else dve_t[n % 4][:, S:2 * S]
                            step(nc.vector.scalar_tensor_tensor(acc[:, 1:S], src[:, 0:S - 1], fw[:, l, 1, c:c + 1],
                                                                acc[:, 1:S], ALU.mult, ALU.add), f"tap1 {name}")
                            after(f"tap1 {name}")
                            if n >= 4 and nm == "ffv":
                                after(f"ff_act {l}.{n - 4}")
                            step(nc.vector.tensor_copy(dst[:, 0:2], acc[:, 0:2]))
                            step(nc.vector.scalar_tensor_tensor(dst[:, 2:S], src[:, 0:S - 2], fw[:, l, 0, c:c + 1],
                                                                acc[:, 2:S], ALU.mult, ALU.add),
                                 f"conv {name}", f"ff_free {l}.{m}", "emptied " + name)
                            m += 1
                    for j in range(2):
                        n = 2 * i + j
                        dve.wait_ge(*scalar.did(f"gelu {l}.{n}"))
                        after(f"conv ffv {l}.{n}")
                        step(nc.vector.tensor_tensor(ff_act[:, n, :], act_t[n % 4][:, S:2 * S], dve_t[n % 4][:, S:2 * S],
                                                     ALU.mult), f"ff_act {l}.{n}")
                    for n in (2 * i - 2, 2 * i - 1):
                        if 0 <= n < KT:
                            low_part(f"ff {l}.{n}", ff_part(h_lo, n), ff_act[:, n, :], ff_part(h_hi, n))
                split_to(unit_of[f"down {l}.0.0.1"])
                for n in range(KT, FT):
                    low_part(f"ff {l}.{n}", ff_part(h_lo, n), ff_act[:, n, :], ff_part(h_hi, n))
                split_to(unit_of[f"down {l}.3.{FT // 8 * 8}.1"])
                post(f"ffn {l}", l, 3)

            settled()
            first_units("rgx 0")
            modulation2(0)
            settled()
            normed2("n2 0", 0, 0)
            step(nc.vector.memset(xb_pad[:, :, 0:RG_K - 1], 0.0), "xb z")
            after("xb z")
            rw, rb = param("rg_w", RG_K), param("rg_b")
            for n in range(KT):
                split_for(f"rgx {n}")
                dve.wait_ge(*scalar.did(f"xb {n}"))
                for k in range(RG_K):
                    src = xb_pad[:, n, k:k + S]
                    if k == 0:
                        step(nc.vector.tensor_scalar(xc[:, n, :], src, rw[:, k, n:n + 1], rb[:, n:n + 1],
                                                     ALU.mult, ALU.add), f"xc0 {n}")
                    else:
                        after(f"xc{k - 1} {n}")
                        step(nc.vector.scalar_tensor_tensor(xc[:, n, :], src, rw[:, k, n:n + 1], xc[:, n, :],
                                                            ALU.mult, ALU.add),
                             f"xc{k} {n}", *([f"xc {n}"] if k == RG_K - 1 else []))
            split_for("rgg 1")
            for n in range(KT):
                dve.wait_ge(*scalar.did(f"ig {n}"))
                step(nc.vector.tensor_tensor(ix[:, n, :], ix[:, n, :], xc[:, n, :], ALU.mult), f"ix {n}")
            for n in range(KT):
                dve.wait_ge(*scalar.did(f"a {n}"))
                step(nc.vector.tensor_tensor(a2[:, n, :], rr[:, n, :], rr[:, n, :], ALU.mult), f"a2 {n}")
                if n % 2:
                    split_to(unit_of["rgg 4"] + n // 2)
            for n in range(KT):
                after(f"a2 {n}")
                step(nc.vector.scalar_tensor_tensor(tt_[:, n, :], a2[:, n, :], 1.0, tt_[:, n, :], ALU.add, ALU.mult),
                     f"one_a2 {n}")
            for n in range(KT):
                dve.wait_ge(*scalar.did(f"mult {n}"))
                after(f"ix {n}")
                step(nc.vector.tensor_tensor(ix[:, n, :], ix[:, n, :], tt_[:, n, :], ALU.mult), f"u_rg {n}")
            for n in range(KT):
                after(f"u_rg {n}")
                step(nc.vector.tensor_tensor_scan(a2[:, n, :], rr[:, n, :], ix[:, n, :], 0.0, ALU.mult, ALU.add), f"hs {n}")
            dve.wait_ge(*tensor.did(f"filled rgx2 {KT - 1}"))
            for n in range(KT):
                after(f"hs {n}")
                dve.wait_ge(*scalar.did(f"gel {n}"))
                step(nc.vector.tensor_tensor(xc[:, n, :], a2[:, n, :], gel[:, n, :], ALU.mult), f"rg_y {n}")
            block_parts("rg", xc, 0)
            ffn(0)
            modulation2(1)
            settled()

            settled()
            first_units("glaq 0")
            step(nc.vector.memset(scan_one, 1.0), "scan_one")
            normed2("n2 1", 1, 0)
            split_for("glaq 0")
            for hd in range(GLA_H):
                name = f"alpha {hd}"
                dve.wait_ge(*scalar.did(f"le {hd}"))
                step(nc.vector.tensor_scalar(la[:, hd, :], bank(name)[:, 0:S], param("gla_b")[:, hd:hd + 1], 0.0,
                                             ALU.add, ALU.min), f"la {hd}", "emptied " + name)
            for hd in range(GLA_H):
                dve.wait_ge(*scalar.did(f"le3 {hd}"))
                after(f"la {hd}")
                step(nc.vector.tensor_tensor(la[:, hd, :], la[:, hd, :], le[:, hd, :], ALU.subtract), f"lb {hd}")
            for hd in range(GLA_H):
                after(f"lb {hd}")
                step(nc.vector.tensor_tensor_scan(gg[:, hd, :], scan_one, la[:, hd, :], 0.0, ALU.mult, ALU.add), f"gg {hd}")
            after(f"gg {GLA_H - 1}")
            flat = carve(8192 + 4 * 1024, GLA_H * S)
            half_of = (1, 2, 4, 8, 16, 32, 64, 128)
            level_order = [(7 + i) % 8 for i in range(8)]

            def halves(ap, s):
                return ap.rearrange("p (b two s) -> p b two s", two=2, s=s)

            for n, i in enumerate(level_order):
                split_to(unit_of["glaq 0"] + 3 + n)
                s = half_of[i]
                g, d = halves(flat, s), halves(lv[:, i, :], s)
                nb = g.shape[1]
                ref = g[:, :, 0, s - 1:s].broadcast_to([P, nb, s])
                step(nc.vector.tensor_tensor(d[:, :, 1, :], g[:, :, 1, :], ref, ALU.subtract))
                step(nc.vector.tensor_tensor(d[:, :, 0, :], ref, g[:, :, 0, :], ALU.subtract), f"ldiff {i}")
            qf, kf = carve(8192, GLA_H * S), carve(8192 + 1024, GLA_H * S)
            dve.wait_ge(*scalar.did(f"gk {GLA_H - 1}"))
            for n, i in enumerate(level_order):
                split_to(min(unit_of["glaq 0"] + 11 + n, unit_of["glar 1"]))
                s = half_of[i]
                d = halves(lv[:, i, :], s)
                dve.wait_ge(*scalar.did(f"lexp {i}"))
                step(nc.vector.tensor_tensor(d[:, :, 1, :], d[:, :, 1, :], halves(qf, s)[:, :, 1, :], ALU.mult))
                step(nc.vector.tensor_tensor(d[:, :, 0, :], d[:, :, 0, :], halves(kf, s)[:, :, 0, :], ALU.mult), f"lv {i}")
            lpf = carve(10240, 8 * P)
            dve.wait_ge(late_landed, 32)
            for n in range(GLA_H * ST):
                hd, t = n // ST, n % ST
                if n % 2 == 0:
                    split_for(f"glar {n // 2}")
                for half in range(2):
                    name = f"lev {n}.{half}"
                    filled(name)
                    if n:
                        after(f"attT {n - 1}")
                    step(nc.vector.tensor_tensor(lpf[:, 512 * half:512 * half + 512], bank(name)[:],
                                                 level[:, 512 * half:512 * half + 512], ALU.mult),
                         f"lpr {n}.{half}", "emptied " + name)
                after(f"lpr {n}.1")
                step(nc.vector.tensor_reduce(attT[:, hd, t, P * t:P * t + P], lprod.rearrange("p l i -> p i l"),
                                             AX_X, ALU.add), f"attT {n}")
            split_for(f"glar {KT // 2 - 1}")
            settled()
            for hd in range(GLA_H):
                dve.wait_ge(*scalar.did(f"dev gs {hd}"))
                step(nc.vector.reciprocal(dve_t[hd][:, 0:S], act_t[hd][:, 0:S]), f"rinv gs {hd}")
            split_for(f"glar {KT // 2}")
            for n in range(KT):
                after(f"rinv gs {n // 2}")
                step(nc.vector.scalar_tensor_tensor(gla_o[:, n, :], gla_o[:, n, :], param("gla_g")[:, n % 2:n % 2 + 1],
                                                    dve_t[n // 2][:, 0:S], ALU.mult, ALU.mult), f"gon {n}")
                if n == 3:
                    split_for(f"glar {KT // 2 + 1}")
            for n in range(KT):
                if KT // 2 + 1 < n:
                    split_for(f"glar {n}")
                dve.wait_ge(*scalar.did(f"r_sil {n}"))
                after(f"gon {n}")
                step(nc.vector.tensor_tensor(gla_o[:, n, :], gla_o[:, n, :], r_sil[:, n, :], ALU.mult), f"gla_y {n}")
            block_parts("gla", gla_o, 1)
            ffn(1)

    return dict(tensor=tensor.now, vector=vector.now, scalar=scalar.now)


WEIGHTS = ("w_mod", "w_in", "w_branch", "w_out", "ada_w_2", "ffn_w_up_2", "ffn_w_down_2", "rg_w_in_2", "rg_wa_2",
           "rg_wx_2", "rg_w_out_2", "gla_w_in_2", "gla_w_out_2", "gla_w_alpha_2")


def shape_tables():
    p, i = np.arange(P), np.arange(S)
    out = {"ident": np.eye(P), "ones": np.ones((P, P)), "eps": np.full((P, 1), EPS)}
    turn = np.zeros((P, P))
    half = ATT_DH // 2
    for m in range(P):
        r = m % ATT_DH
        turn[m + half if r < half else m - half, m] = -1.0 if r < half else 1.0
    out["turn"] = turn
    freqs = ATT_DH // 4
    inv = (np.float32(10000.0) ** (-np.arange(freqs, dtype=np.float32) / np.float32(freqs))).astype(np.float32)
    row, col = (i // 64).astype(np.float32), (i % 64).astype(np.float32)
    angle = np.concatenate([inv[:, None] * row[None], inv[:, None] * col[None]], 0).astype(np.float32)
    angle = np.tile(angle, (P // half, 1))
    out["cos"], out["sin"] = np.cos(angle), np.sin(angle)
    j = p[:, None, None] + P * np.arange(ST)[None, :, None]
    dist = i[None, None, :] - j
    out["behind"] = np.maximum(dist, 0).reshape(P, -1)
    out["ahead"] = np.maximum(-dist, 0).reshape(P, -1)
    out["q_pos"] = np.tile(np.concatenate([i + 1, S - i])[None], (P, 1))
    pos = p[:, None] + P * np.arange(ST)[None]
    out["k_pos"] = np.concatenate([S - 1 - pos, pos], 1)
    q, k = p[:, None], p[None, :]
    out["band"] = np.concatenate([np.where(k <= q, 0.0, -1e30), np.where(k >= q, 0.0, -1e30)], 1)
    masks = []
    for s in LEVELS:
        a, b = p[:, None], p[None, :]
        masks.append((a // (2 * s) == b // (2 * s)) & (a % (2 * s) < s) & (b % (2 * s) >= s))
    masks.append(np.eye(P, dtype=bool))
    level = np.concatenate([m.astype(np.float32) for m in masks], 1)
    return np.concatenate([out[n].reshape(P, -1).astype(np.float32) for n in TABLES], 1), level


def pack_params(a):
    def cols(v):
        v = np.asarray(v)
        v = v.reshape(v.shape[:-1] + (v.shape[-1] // P, P))
        return np.moveaxis(v, -1, 0).reshape(P, -1)

    def rows(v):
        return np.broadcast_to(np.asarray(v).reshape(1, -1), (P, np.asarray(v).size))

    c_vec = np.stack([cols(a["c"][0]), cols(a["c_ctx"]), cols(a["c_2"][0])], 2).reshape(P, -1)
    wz = np.asarray(a["gla_w_in_2"])[0][:, 3072:3088].reshape(KT, P, 16).transpose(1, 0, 2).reshape(P, -1)
    parts = dict(norm_w=cols(a["norm_w"]), gn_w=cols(a["ret_gn_w"]), sc_w=cols(a["sc_conv_w"]), cf_w=cols(a["cf_conv_w"]),
                 cf_b=cols(a["cf_conv_b"]), ln_w=cols(a["cf_ln_w"]), ln_b=cols(a["cf_ln_b"]), sink=rows(a["att_sink"]),
                 b_mod=cols(a["b_mod"]), fin_w=cols(a["final_norm_w"]), decay=rows(a["ret_decay"]),
                 lam=cols(a["rg_lambda_2"]), c_vec=c_vec, ada_b=cols(a["ada_b_2"]), norm_g=cols(a["norm_g_2"]),
                 ff_w=cols(a["ffn_conv_w_2"]), ff_b=cols(a["ffn_conv_b_2"]), rg_w=cols(a["rg_conv_w_2"]),
                 rg_b=cols(a["rg_conv_b_2"]), rg_ba=cols(a["rg_ba_2"]), rg_bx=cols(a["rg_bx_2"]),
                 gla_b=cols(a["gla_b_alpha_2"]), gla_g=cols(a["gla_norm_g_2"]), gla_z=wz)
    for n, v in parts.items():
        assert v.shape == (P, PARAMS[n]), (n, v.shape)
    return np.ascontiguousarray(np.concatenate([parts[n] for n in PARAMS], 1))


def kernel(**inputs):
    import concourse.bacc as _bacc
    from concourse.bass_utils import run_bass_kernel_spmd as _run

    arrays = {n: np.ascontiguousarray(np.asarray(inputs[n])) for n in WEIGHTS}
    arrays["x"] = np.ascontiguousarray(np.asarray(inputs["x"])[0].T)
    arrays["ctx"] = np.ascontiguousarray(np.asarray(inputs["ctx"])[0].T)
    arrays["params"] = pack_params(inputs)
    arrays["tables"], arrays["level"] = shape_tables()

    def build(counts):
        nc = _bacc.Bacc("TRN2", target_bir_lowering=False, num_devices=1)
        io = {n: nc.dram_tensor(f"in_{n}", a.shape, F32, kind="ExternalInput").ap() for n, a in arrays.items()}
        io["out"] = nc.dram_tensor("out", (D, S), F32, kind="ExternalOutput").ap()
        return nc, program(nc, io, counts)

    _, counts = build(None)
    nc, again = build(counts)
    assert again == counts
    r = _run(nc, [{f"in_{n}": a for n, a in arrays.items()}], core_ids=[0])
    return np.ascontiguousarray(np.asarray(r.results[0]["out"]).T)[None]
```
